# Optimizing a Trainium2 kernel written in Bass

```python
import math
import jax
import jax.numpy as jnp
from jax import lax
import numpy as np

D_MODEL = 1024
BATCH = 1
SEQ = 1024
DEPTH = 2
DEC_BATCH = 8
DEC_SEQ = 8
PAST_LEN = 1024
PAGE_SIZE = 128

HEAD_DIM = 64
N_HEADS_A = 8
N_HEADS_B = 4
DIL_PAIRS = ((128, 1), (512, 4), (2048, 16))
WIN_MAX = 2048
Q_BLOCK = 128
ROPE_THETA = 500000.0
ROPE_DIM = HEAD_DIM // 4
A_W = N_HEADS_A * HEAD_DIM
B_W = N_HEADS_B * 2 * HEAD_DIM
D_IN = 3 * A_W + 3 * B_W
D_MIX = A_W + B_W
SPLITS = [A_W, 2 * A_W, 3 * A_W, 3 * A_W + B_W, 3 * A_W + 2 * B_W]
POOL_WINDOWS = (2, 4, 8, 16)
POOL_MAX = 16
POOL_STATE = POOL_MAX - 1
POOL_GROUP = D_MODEL // len(POOL_WINDOWS)
D_FF = -(-8 * D_MODEL // (3 * 256)) * 256
N_AB_LAYERS = (DEPTH + 1) // 2
N_POOL_LAYERS = DEPTH // 2
RMS_EPS = 1e-6
SUBLN_EPS = 1e-5
NEG = -1e30

kernel_name = 'hybrid_dilated_diff_pool_decoder_step'

def rms_norm(x, g, eps=RMS_EPS):
    xf = x.astype(jnp.float32)
    y = xf * lax.rsqrt(jnp.mean(xf * xf, axis=-1, keepdims=True) + eps)
    return (y * g.astype(jnp.float32)).astype(x.dtype)

def rope_partial(x, pos):
    half = ROPE_DIM // 2
    inv_freq = ROPE_THETA ** (-jnp.arange(half, dtype=jnp.float32) * 2.0 / ROPE_DIM)
    ang = pos.astype(jnp.float32)[:, None] * inv_freq[None, :]
    cos = jnp.cos(ang)[:, None, :]
    sin = jnp.sin(ang)[:, None, :]
    xf = x.astype(jnp.float32)
    x1 = xf[..., :half]
    x2 = xf[..., half:ROPE_DIM]
    out = jnp.concatenate([x1 * cos - x2 * sin, x2 * cos + x1 * sin, xf[..., ROPE_DIM:]], axis=-1)
    return out.astype(x.dtype)

def ab_project(xn, pos, w_in):
    B, S, _ = xn.shape
    h = jnp.einsum('bsd,de->bse', xn, w_in)
    qa, ka, va, qb, kb, vb = jnp.split(h, SPLITS, axis=-1)
    qa = rope_partial(qa.reshape(B, S, N_HEADS_A, HEAD_DIM), pos)
    ka = rope_partial(ka.reshape(B, S, N_HEADS_A, HEAD_DIM), pos)
    va = va.reshape(B, S, N_HEADS_A, HEAD_DIM)
    qb = rope_partial(qb.reshape(B, S, 2 * N_HEADS_B, HEAD_DIM), pos).reshape(B, S, N_HEADS_B, 2 * HEAD_DIM)
    kb = rope_partial(kb.reshape(B, S, 2 * N_HEADS_B, HEAD_DIM), pos).reshape(B, S, N_HEADS_B, 2 * HEAD_DIM)
    vb = vb.reshape(B, S, N_HEADS_B, 2 * HEAD_DIM)
    return qa, ka, va, qb, kb, vb

def dilated_branch_prompt(q, k, v, window, dil):
    B, S, H, hd = q.shape
    band = window // dil
    L = -(-S // (dil * Q_BLOCK)) * Q_BLOCK
    nb = L // Q_BLOCK
    pad = L * dil - S

    def to_residue_blocks(t):
        t = jnp.pad(t, ((0, 0), (0, pad), (0, 0), (0, 0)))
        t = t.reshape(B, L, dil, H, hd).transpose(0, 2, 1, 3, 4)
        return t.reshape(B, dil, nb, Q_BLOCK, H, hd)

    def with_prev(t):
        t = to_residue_blocks(t)
        prev = jnp.pad(t[:, :, :-1], ((0, 0), (0, 0), (1, 0), (0, 0), (0, 0), (0, 0)))
        return jnp.concatenate([prev, t], axis=3)

    qr = to_residue_blocks(q)
    kk = with_prev(k)
    vv = with_prev(v)
    s = jnp.einsum('brnqhd,brnkhd->brnhqk', qr, kk)
    qi = jnp.arange(Q_BLOCK)[:, None]
    kj = jnp.arange(2 * Q_BLOCK)[None, :]
    off = qi + Q_BLOCK - kj
    key_idx = jnp.arange(nb)[:, None, None] * Q_BLOCK - Q_BLOCK + kj[None]
    valid = (off >= 0) & (off <= band) & (key_idx >= 0)
    s = jnp.where(valid[None, None, :, None], s, NEG)
    m = jnp.max(s, axis=-1, keepdims=True)
    e = jnp.exp(s - m)
    den = jnp.sum(e, axis=-1, keepdims=True)
    o = jnp.einsum('brnhqk,brnkhd->brnhqd', e, vv) / den
    lse = (m + jnp.log(den))[..., 0]
    o = o.transpose(0, 2, 4, 1, 3, 5).reshape(B, L * dil, H, hd)[:, :S]
    lse = lse.transpose(0, 2, 4, 1, 3).reshape(B, L * dil, H)[:, :S]
    return o, lse

def dilated_branch_sample(q, k_all, v_all, window, dil, n_prev):
    T = q.shape[1]
    band = window // dil
    idx = n_prev + jnp.arange(T)[:, None] - dil * jnp.arange(band + 1)[None, :]
    valid = idx >= 0
    idx = jnp.maximum(idx, 0)
    kg = k_all[:, idx]
    vg = v_all[:, idx]
    s = jnp.einsum('bthd,btmhd->bthm', q, kg)
    s = jnp.where(valid[None, :, None, :], s, NEG)
    m = jnp.max(s, axis=-1, keepdims=True)
    e = jnp.exp(s - m)
    den = jnp.sum(e, axis=-1, keepdims=True)
    o = jnp.einsum('bthm,btmhd->bthd', e, vg) / den
    lse = (m + jnp.log(den))[..., 0]
    return o, lse

def combine_branches(outs, lses):
    w = jax.nn.softmax(jnp.stack(lses, axis=0), axis=0)
    return jnp.einsum('nbsh,nbshd->bshd', w, jnp.stack(outs, axis=0))

def dilated_attn_prompt(q, k, v):
    qf = q.astype(jnp.float32) * HEAD_DIM ** -0.5
    kf = k.astype(jnp.float32)
    vf = v.astype(jnp.float32)
    res = [dilated_branch_prompt(qf, kf, vf, w, d) for w, d in DIL_PAIRS]
    return combine_branches([r[0] for r in res], [r[1] for r in res])

def dilated_attn_sample(q, k_all, v_all, n_prev):
    qf = q.astype(jnp.float32) * HEAD_DIM ** -0.5
    kf = k_all.astype(jnp.float32)
    vf = v_all.astype(jnp.float32)
    res = [dilated_branch_sample(qf, kf, vf, w, d, n_prev) for w, d in DIL_PAIRS]
    return combine_branches([r[0] for r in res], [r[1] for r in res])

def diff_attn_prompt(q, k, v, lam):
    B, S, H, _ = q.shape
    nb = S // Q_BLOCK
    qf = q.astype(jnp.float32) * HEAD_DIM ** -0.5
    kf = k.astype(jnp.float32)
    vf = v.astype(jnp.float32)
    k1 = kf[..., :HEAD_DIM]
    k2 = kf[..., HEAD_DIM:]
    q_blocks = qf.reshape(B, nb, Q_BLOCK, H, 2 * HEAD_DIM).transpose(1, 0, 2, 3, 4)
    kpos = jnp.arange(S)

    def one_block(args):
        qb, n = args
        causal = kpos[None, :] <= (n * Q_BLOCK + jnp.arange(Q_BLOCK))[:, None]
        p1 = jax.nn.softmax(jnp.where(causal, jnp.einsum('bqhd,bkhd->bhqk', qb[..., :HEAD_DIM], k1), NEG), axis=-1)
        p2 = jax.nn.softmax(jnp.where(causal, jnp.einsum('bqhd,bkhd->bhqk', qb[..., HEAD_DIM:], k2), NEG), axis=-1)
        return jnp.einsum('bhqk,bkhd->bqhd', p1 - lam * p2, vf)

    o = lax.map(one_block, (q_blocks, jnp.arange(nb)))
    return o.transpose(1, 0, 2, 3, 4).reshape(B, S, H, 2 * HEAD_DIM)

def diff_attn_sample(q, k_past, v_past, k_new, v_new, lam):
    T = q.shape[1]
    P = k_past.shape[1]
    qf = q.astype(jnp.float32) * HEAD_DIM ** -0.5
    kp = k_past.astype(jnp.float32)
    kn = k_new.astype(jnp.float32)
    causal = jnp.arange(T)[None, :] <= jnp.arange(T)[:, None]

    def probs(qh, kph, knh):
        s_past = jnp.einsum('bthd,bkhd->bhtk', qh, kph)
        s_new = jnp.where(causal, jnp.einsum('bthd,bkhd->bhtk', qh, knh), NEG)
        return jax.nn.softmax(jnp.concatenate([s_past, s_new], axis=-1), axis=-1)

    a = (probs(qf[..., :HEAD_DIM], kp[..., :HEAD_DIM], kn[..., :HEAD_DIM])
         - lam * probs(qf[..., HEAD_DIM:], kp[..., HEAD_DIM:], kn[..., HEAD_DIM:]))
    return (jnp.einsum('bhtk,bkhd->bthd', a[..., :P], v_past.astype(jnp.float32))
            + jnp.einsum('bhtk,bkhd->bthd', a[..., P:], v_new.astype(jnp.float32)))

def ab_merge(o_a, o_b, g_sub, lam_init, w_out):
    B, S = o_a.shape[:2]
    o_b = rms_norm(o_b, g_sub, SUBLN_EPS) * (1.0 - lam_init)
    o = jnp.concatenate([o_a.reshape(B, S, A_W), o_b.reshape(B, S, B_W)], axis=-1).astype(w_out.dtype)
    return jnp.einsum('bse,ed->bsd', o, w_out)

def pool_mix(ext, pos, pool_w, pool_scale):
    S = pos.shape[0]
    cs = jnp.cumsum(ext.astype(jnp.float32), axis=1)
    cur = ext[:, POOL_MAX:].astype(jnp.float32)
    outs = []
    for g, w in enumerate(POOL_WINDOWS):
        lo, hi = g * POOL_GROUP, (g + 1) * POOL_GROUP
        win_sum = cs[:, POOL_MAX:, lo:hi] - cs[:, POOL_MAX - w:POOL_MAX - w + S, lo:hi]
        cnt = jnp.minimum(pos + 1, w).astype(jnp.float32)[None, :, None]
        outs.append(jnp.einsum('bsc,ce->bse', win_sum / cnt - cur[..., lo:hi], pool_w[g].astype(jnp.float32)))
    return (jnp.concatenate(outs, axis=-1) * pool_scale.astype(jnp.float32)).astype(ext.dtype)

def swiglu(xn, w_gate, w_up, w_down):
    h = jax.nn.silu(jnp.einsum('bsd,df->bsf', xn, w_gate)) * jnp.einsum('bsd,df->bsf', xn, w_up)
    return jnp.einsum('bsf,fd->bsd', h, w_down)

def setup_inputs(seed: int = 0) -> dict:
    key = jax.random.key(seed)
    ks = jax.random.split(key, 24)
    f32 = jnp.float32
    n_pages = PAST_LEN // PAGE_SIZE
    n_phys = (5 * DEC_BATCH * n_pages + 3) // 4
    win = min(WIN_MAX, PAST_LEN)

    def nrm(k, shape, scale=1.0):
        return jax.random.normal(k, shape, f32) * scale

    perm = jax.random.permutation(ks[7], n_phys)[: DEC_BATCH * n_pages]
    page_table = perm.reshape(DEC_BATCH, n_pages).astype(jnp.int32)
    return {
        'x_prompt': nrm(ks[0], (BATCH, SEQ, D_MODEL)),
        'x_sample': nrm(ks[1], (DEC_BATCH, DEC_SEQ, D_MODEL)),
        'cache_k_b': nrm(ks[2], (N_AB_LAYERS, n_phys, PAGE_SIZE, N_HEADS_B, 2 * HEAD_DIM)),
        'cache_v_b': nrm(ks[3], (N_AB_LAYERS, n_phys, PAGE_SIZE, N_HEADS_B, 2 * HEAD_DIM)),
        'cache_win_k_a': nrm(ks[4], (N_AB_LAYERS, DEC_BATCH, win, N_HEADS_A, HEAD_DIM)),
        'cache_win_v_a': nrm(ks[5], (N_AB_LAYERS, DEC_BATCH, win, N_HEADS_A, HEAD_DIM)),
        'state_pool': nrm(ks[6], (N_POOL_LAYERS, DEC_BATCH, POOL_STATE, D_MODEL)),
        'page_table': page_table,
        'ln_mix': 1.0 + nrm(ks[8], (DEPTH, D_MODEL), 0.05),
        'ln_ffn': 1.0 + nrm(ks[9], (DEPTH, D_MODEL), 0.05),
        'ln_final': 1.0 + nrm(ks[10], (D_MODEL,), 0.05),
        'w_in': nrm(ks[11], (N_AB_LAYERS, D_MODEL, D_IN), D_MODEL ** -0.5),
        'w_out': nrm(ks[12], (N_AB_LAYERS, D_MIX, D_MODEL), D_MIX ** -0.5),
        'lambda_q1': nrm(ks[13], (N_AB_LAYERS, HEAD_DIM), 0.1),
        'lambda_k1': nrm(ks[14], (N_AB_LAYERS, HEAD_DIM), 0.1),
        'lambda_q2': nrm(ks[15], (N_AB_LAYERS, HEAD_DIM), 0.1),
        'lambda_k2': nrm(ks[16], (N_AB_LAYERS, HEAD_DIM), 0.1),
        'subln_g': 1.0 + nrm(ks[17], (N_AB_LAYERS, 2 * HEAD_DIM), 0.05),
        'pool_w': nrm(ks[18], (N_POOL_LAYERS, len(POOL_WINDOWS), POOL_GROUP, POOL_GROUP), POOL_GROUP ** -0.5),
        'pool_scale': 0.5 + nrm(ks[19], (N_POOL_LAYERS, D_MODEL), 0.05),
        'w_gate': nrm(ks[20], (DEPTH, D_MODEL, D_FF), D_MODEL ** -0.5),
        'w_up': nrm(ks[21], (DEPTH, D_MODEL, D_FF), D_MODEL ** -0.5),
        'w_down': nrm(ks[22], (DEPTH, D_FF, D_MODEL), D_FF ** -0.5),
    }

def reference(x_prompt, x_sample, cache_k_b, cache_v_b, cache_win_k_a, cache_win_v_a, state_pool, page_table,
              ln_mix, ln_ffn, ln_final, w_in, w_out, lambda_q1, lambda_k1, lambda_q2, lambda_k2, subln_g,
              pool_w, pool_scale, w_gate, w_up, w_down):
    f32 = jnp.float32
    S = x_prompt.shape[1]
    DB, T = x_sample.shape[0], x_sample.shape[1]
    past = page_table.shape[1] * PAGE_SIZE
    pos_p = jnp.arange(S, dtype=jnp.int32)
    pos_s = past + jnp.arange(T, dtype=jnp.int32)
    win_s = cache_win_k_a.shape[2]
    win_p = min(WIN_MAX, S)
    hp, hs = x_prompt, x_sample
    kb_p, vb_p, kb_s, vb_s = [], [], [], []
    wk_p, wv_p, wk_s, wv_s = [], [], [], []
    pl_p, pl_s = [], []
    for layer in range(DEPTH):
        j = layer // 2
        xn_p = rms_norm(hp, ln_mix[layer])
        xn_s = rms_norm(hs, ln_mix[layer])
        if layer % 2 == 0:
            lam_init = 0.8 - 0.6 * math.exp(-0.3 * layer)
            lam = (jnp.exp(jnp.sum(lambda_q1[j].astype(f32) * lambda_k1[j].astype(f32)))
                   - jnp.exp(jnp.sum(lambda_q2[j].astype(f32) * lambda_k2[j].astype(f32))) + lam_init)
            qa, ka, va, qb, kb, vb = ab_project(xn_p, pos_p, w_in[j])
            o_a = dilated_attn_prompt(qa, ka, va)
            o_b = diff_attn_prompt(qb, kb, vb, lam)
            hp = hp + ab_merge(o_a, o_b, subln_g[j], lam_init, w_out[j])
            kb_p.append(kb)
            vb_p.append(vb)
            wk_p.append(ka[:, S - win_p:])
            wv_p.append(va[:, S - win_p:])
            qa, ka, va, qb, kb, vb = ab_project(xn_s, pos_s, w_in[j])
            ka_all = jnp.concatenate([cache_win_k_a[j].astype(ka.dtype), ka], axis=1)
            va_all = jnp.concatenate([cache_win_v_a[j].astype(va.dtype), va], axis=1)
            o_a = dilated_attn_sample(qa, ka_all, va_all, win_s)
            k_past = cache_k_b[j, page_table].reshape(DB, past, N_HEADS_B, 2 * HEAD_DIM)
            v_past = cache_v_b[j, page_table].reshape(DB, past, N_HEADS_B, 2 * HEAD_DIM)
            o_b = diff_attn_sample(qb, k_past, v_past, kb, vb, lam)
            hs = hs + ab_merge(o_a, o_b, subln_g[j], lam_init, w_out[j])
            kb_s.append(kb)
            vb_s.append(vb)
            wk_s.append(ka_all[:, -win_s:])
            wv_s.append(va_all[:, -win_s:])
        else:
            ext_p = jnp.pad(xn_p, ((0, 0), (POOL_MAX, 0), (0, 0)))
            hp = hp + pool_mix(ext_p, pos_p, pool_w[j], pool_scale[j])
            ext_s = jnp.concatenate([jnp.zeros((DB, 1, D_MODEL), xn_s.dtype),
                                     state_pool[j].astype(xn_s.dtype), xn_s], axis=1)
            hs = hs + pool_mix(ext_s, pos_s, pool_w[j], pool_scale[j])
            pl_p.append(xn_p[:, S - POOL_STATE:])
            pl_s.append(ext_s[:, -POOL_STATE:])
        hp = hp + swiglu(rms_norm(hp, ln_ffn[layer]), w_gate[layer], w_up[layer], w_down[layer])
        hs = hs + swiglu(rms_norm(hs, ln_ffn[layer]), w_gate[layer], w_up[layer], w_down[layer])
    y_prompt = rms_norm(hp, ln_final)
    y_sample = rms_norm(hs, ln_final)
    return (y_prompt, y_sample,
            jnp.stack(kb_p), jnp.stack(vb_p), jnp.stack(kb_s), jnp.stack(vb_s),
            jnp.stack(wk_p), jnp.stack(wv_p), jnp.stack(wk_s), jnp.stack(wv_s),
            jnp.stack(pl_p), jnp.stack(pl_s))


_drawn_inputs = setup_inputs


def setup_inputs(seed=0):
    import zlib

    import numpy as np

    out = dict(_drawn_inputs(seed))
    spreads = {}
    factors = {}
    for name, (base, spread) in spreads.items():
        noise = np.random.default_rng([zlib.crc32(name.encode()), seed]).standard_normal(out[name].shape)
        drawn = base * np.exp(spread * noise) if base else spread * noise
        out[name] = jnp.asarray(drawn.astype(out[name].dtype))
    for name, factor in factors.items():
        out[name] = (out[name] * factor).astype(out[name].dtype)
    return out
```

```python
from contextlib import ExitStack

import numpy as np

import concourse.bass as bass
from concourse import mybir

F32 = mybir.dt.float32
F32R = mybir.dt.float32r
I32 = mybir.dt.int32
ALU = mybir.AluOpType
ACT = mybir.ActivationFunctionType
AX = mybir.AxisListType

P = 128
D = 1024
KD = D // P
S = 1024
DB, T = 8, 8
NS = DB * T
NT = S + NS
NTILE = S // P
FF = 2816
PAIRS = FF // 256
CH = ((0, 364), (364, 364), (728, 360))
NC = len(CH)
CW = 364
PAST = 1024
PAGE = 128
NPAGE = PAST // PAGE
NPHYS = 80
NEG = -1e30
LAM0 = 0.2
PADW = 16 + S + DB * 24
STATE = 15

OFF = {}
W = 0
for _name, _n in (("ident", 128), ("cs", 9 * 32), ("maskA", 1024), ("maskB", 1024), ("decA", 1024), ("newA", 120),
                  ("newB", 120), ("comb0", 32), ("comb1", 32), ("corr", 64)):
    OFF[_name] = (W, _n)
    W += _n
CONST_W = W


def shape_constants():
    c = np.zeros((P, CONST_W), np.float32)

    def put(name, a):
        o, n = OFF[name]
        c[:a.shape[0], o:o + n] = a.reshape(a.shape[0], n)

    def times(off):
        return (((off >= 0) & (off <= 128)).astype(int) + ((off >= 0) & (off <= 512) & (off % 4 == 0))
                + ((off >= 0) & (off <= 2048) & (off % 16 == 0)))

    def log8(n):
        return np.where(n > 0, 8.0 * np.log(np.maximum(n, 1)), NEG).astype(np.float32)

    put("ident", np.eye(P, dtype=np.float32))
    inv = np.float32(500000.0) ** (-np.arange(8, dtype=np.float32) * np.float32(2.0) / np.float32(16))
    pos = np.zeros((9, P), np.float32)
    pos[:8] = np.arange(S).reshape(8, P)
    pos[8, :NS] = PAST + np.arange(NS) % T
    ang = (pos[..., None] * inv.astype(np.float32)).astype(np.float32).transpose(1, 0, 2)
    co, si = np.cos(ang).astype(np.float32), np.sin(ang).astype(np.float32)
    put("cs", np.concatenate([co, co, si, si], axis=-1))
    p, y = np.arange(P)[:, None], np.arange(1024)[None]
    put("maskA", log8(times(p + 896 - y)))
    put("maskB", np.where(p + 896 - y >= 0, 0, NEG).astype(np.float32))
    r = np.arange(P)[:, None]
    put("decA", log8(times(1024 + r % 8 - (8 * (y % 128) + y // 128))))
    z = np.arange(120)[None] - 56
    ok = (z >= 0) & (z <= r % 8)
    put("newA", np.where(ok, log8(times(r % 8 - z)), NEG).astype(np.float32))
    put("newB", np.where(ok, 0, NEG).astype(np.float32))
    o = np.arange(32)[None]
    for half in range(2):
        put(f"comb{half}", ((r // 32 == o // 8) & (r % 32 == 8 * half + o % 8)).astype(np.float32))
    corr = np.stack([w / np.minimum(np.arange(16) + 1, w) for w in (2, 4, 8, 16)]).astype(np.float32)
    put("corr", np.broadcast_to(corr.reshape(1, 64), (P, 64)))
    return c


def build_step(nc, d):
    st = ExitStack()
    with st:
        base = (nc.sbuf_base + 63) // 64 * 64
        at = [base]

        def persistent(name, shape, dt=F32):
            t = nc.alloc_sbuf_tensor_at(name, shape, dt, offset=at[0])
            at[0] += (int(np.prod(shape[1:])) * 4 + 31) // 32 * 32
            return t

        x = persistent("x", [P, KD, NT])
        ident = persistent("ident", [P, P])
        ones = persistent("ones", [P, P])
        gains = persistent("gains", [P, 49])
        small = persistent("small", [P, 24])
        xn_at = at[0]
        xn = persistent("xn", [P, KD, 2, NT], F32R)
        rest = at[0]

        def placed(name, off, shape, dt=F32):
            return nc.alloc_sbuf_tensor_at(name, shape, dt, offset=off)

        ws = [placed("ws0", rest, [P, 2, 2048], F32R), placed("ws1", rest + 32768, [P, 2, 2048], F32R),
              placed("ws2", rest + 49152, [P, 2, 2048], F32R)]
        wraw = placed("wraw", rest + 16384, [P, 2, 2048])
        hh = placed("hh", rest + 65536, [P, 2, 2, 2, NT], F32R)
        act_s = placed("act_s", rest + 100352, [P, 2, CW])
        act_h = placed("act_h", rest + 100352 + 2912, [P, 2, CW])
        nrm = rest + 106176 - 18880
        sq = placed("sq", nrm, [P, 2, NT])
        rstd = placed("rstd", nrm + 8704, [P, NT])
        xf = placed("xf", nrm + 13056, [P, 4, CW])
        xin = placed("xin", rest, [P, 3, D])
        grow = placed("grow", rest + 12288, [49, P])
        lamrow = placed("lamrow", rest + 12800, [1, 4, 64])
        lamtmp = placed("lamtmp", rest + 14080, [1, 2, 64])
        wp = placed("wp", rest, [P, 2, 2, KD, 512], F32R)
        wpraw = placed("wpraw", rest + 65536, [P, 2, 4, 512])
        tok = placed("tok", rest + 81920, [P, 3, 512])
        toks = placed("toks", rest + 88064, [NS, 6, 512])
        cs = placed("cs", rest + 100352, [P, 9, 32])
        rope = placed("rope", rest + 101504, [P, 2, 2, 128])
        osam = placed("osam", rest + 103552, [P, 2, 4, NS])
        kraw = placed("kraw", xn_at, [P, 2, 8, 512])
        vraw = placed("vraw", xn_at + 32768, [P, 2, 8, 512])
        q = rest
        dkT = placed("dkT", q, [P, 4, PAST])
        dse = placed("dse", q + 16384, [P, 2, PAST + NS])
        dpT = placed("dpT", q + 25088, [P, 2, 9, P])
        dom = placed("dom", q + 34304, [P, P])
        qblk = placed("qblk", q + 34816, [P, 2, DB, 4, 32])
        qcur = placed("qcur", q + 43008, [P, 2, 4, 32])
        knT = placed("knT", q + 44032, [P, 2, 4, NS])
        dmask = placed("dmask", q + 46080, [P, 2, PAST + NS])
        dnew = placed("dnew", q + 54784, [P, 2, 120])
        comb = placed("comb", q + 55744, [P, 3, 32])
        dmix = placed("dmix", q + 56128, [P, 2, 64])
        dstat = placed("dstat", q + 56640, [P, 2, 4])
        ptab = placed("ptab", q + 56704, [1, DB * NPAGE], I32)
        qkv = placed("qkv", rest, [P, 2, 3, 8, 128])
        qT = placed("qT", rest + 24576, [P, S])
        kT = placed("kT", rest + 28672, [P, S])
        sm = placed("sm", rest + 32768, [P, 4, S])
        pT = placed("pT", rest + 49152, [P, 2, 8, 512])
        ob = placed("ob", rest + 65536, [P, 4, S])
        pmask = placed("pmask", rest + 81920, [P, S])
        pstat = placed("pstat", rest + 86016, [P, 4, 4])
        osq = placed("osq", rest + 24576, [P, 2, 512])
        orms = placed("orms", rest + 32768, [P, 12, 512])
        yp = placed("yp", rest + 32768, [P, KD, PADW])
        pa = placed("pa", rest + 32768 + KD * PADW * 4, [P, 2, PADW])
        pf = placed("pf", rest + 32768 + (KD + 2) * PADW * 4, [P, NT])
        stin = placed("stin", rest + 32768 + KD * PADW * 4, [DB * STATE, D])
        corr = placed("corr", nrm - 256, [P, 4, 16])
        yf = placed("yf", xn_at, [P, KD, NT])
        yrow = placed("yrow", rest, [P, 3, D])
        prow = placed("prow", rest + 32768 + KD * PADW * 4, [P, 2, D])

        ps = st.enter_context(nc.psum_tensor("ps", [P, 8, 512], F32))
        pcomp = placed("pcomp", nrm, [P, KD, STATE * (DB + 1)])
        qs_dram = nc.dram_tensor("q_rows", [2, S, 512], F32, kind="Internal").ap()

        def sem(name):
            return st.enter_context(nc.semaphore(name))

        consts = d["consts"]

        def const(name, rows=P):
            o, n = OFF[name]
            return consts[0:rows, o:o + n]

        s_const = sem("s_const")
        s_xin = [sem(f"s_xin{i}") for i in range(3)]
        s_ones = sem("s_ones")
        s_xt = sem("s_xt")
        s_x = sem("s_x")
        s_gt, s_gains = sem("s_gt"), sem("s_gains")
        s_lam, s_lamv, s_lamb = sem("s_lam"), sem("s_lamv"), sem("s_lamb")
        s_sq, s_ss, s_rt, s_rstd = sem("s_sq"), sem("s_ss"), sem("s_rt"), sem("s_rstd")
        s_xf, s_xhi, s_xlo = sem("s_xf"), sem("s_xhi"), sem("s_xlo")
        s_praw = [sem(f"s_praw{i}") for i in range(2)]
        s_phi, s_plo = sem("s_phi"), sem("s_plo")
        s_cs = sem("s_cs")
        s_proj = sem("s_proj")
        s_tok = sem("s_tok")
        s_ropeP = sem("s_ropeP")
        s_rope = sem("s_rope")
        s_store = [sem(f"s_store{i}") for i in range(3)]
        s_sstore = sem("s_sstore")
        s_raw = [sem(f"s_raw{i}") for i in range(2)]
        s_whi, s_wlo = sem("s_whi"), sem("s_wlo")
        s_gu = sem("s_gu")
        s_silu, s_h, s_hhi, s_hlo = sem("s_silu"), sem("s_h"), sem("s_hhi"), sem("s_hlo")
        s_acc = sem("s_acc")
        s_added = sem("s_added")
        s_dc = sem("s_dc")
        s_dk = [sem(f"s_dk{i}") for i in range(2)]
        s_dv = [sem(f"s_dv{i}") for i in range(2)]
        s_win = sem("s_win")
        s_pt = sem("s_pt")
        s_qz, s_qk, s_qke, s_qb = sem("s_qz"), sem("s_qk"), sem("s_qke"), sem("s_qb")
        s_dtr, s_dev, s_dea = sem("s_dtr"), sem("s_dev"), sem("s_dea")
        s_qc, s_ds, s_dsm, s_dnm, s_de, s_drd, s_dmx = (sem(n) for n in ("s_qc", "s_ds", "s_dsm", "s_dnm", "s_de", "s_drd", "s_dmx"))
        s_dpt, s_dpe, s_dpv, s_dom, s_dot, s_dos = (sem(n) for n in ("s_dpt", "s_dpe", "s_dpv", "s_dom", "s_dot", "s_dos"))
        s_qd, s_dmk, s_cmbd = sem("s_qd"), sem("s_dmk"), sem("s_cmbd")
        s_pm = sem("s_pm")
        s_qkv = [sem(f"s_qkv{i}") for i in range(2)]
        s_qt, s_qte = sem("s_qt"), sem("s_qte")
        s_s, s_sm, s_nm, s_e, s_rd, s_p = (sem(n) for n in ("s_s", "s_sm", "s_nm", "s_e", "s_rd", "s_p"))
        s_tu, s_rdx, s_cmb, s_small = sem("s_tu"), sem("s_rdx"), sem("s_cmb"), sem("s_small")
        s_tp, s_tpe, s_pv, s_ohi, s_olo = (sem(n) for n in ("s_tp", "s_tpe", "s_pv", "s_ohi", "s_olo"))
        s_osq, s_oss, s_ort, s_orr, s_osc, s_oh, s_ol = (sem(n) for n in ("s_osq", "s_oss", "s_ort", "s_orr", "s_osc", "s_oh", "s_ol"))
        s_st, s_stt, s_yp, s_pz, s_lvl = sem("s_st"), sem("s_stt"), sem("s_yp"), sem("s_pz"), sem("s_lvl")
        s_corr, s_pf, s_pfh, s_pfl = sem("s_corr"), sem("s_pf"), sem("s_pfh"), sem("s_pfl")
        s_ot, s_oe = sem("s_ot"), sem("s_oe")
        s_out = [sem(f"s_out{i}") for i in range(3)]
        s_pout = sem("s_pout")
        s_pot, s_pc, s_prow = sem("s_pot"), sem("s_pc"), sem("s_prow")

        block = st.enter_context(nc.Block())

        FFN_U = (4, 38)
        FFN_A = (24, 312)
        GU_PER = 2 * NC
        FFN_G = (0, PAIRS * GU_PER)
        ADD_PER = KD * NC

        def unit_src(kind, layer, b):
            if kind == "out":
                return d["w_out"][0].rearrange("(k p) n -> p k n", p=P)[:, :, b * 256:(b + 1) * 256]
            if kind == "gate":
                return d["w_gate"][layer].rearrange("(k p) n -> p k n", p=P)[:, :, bass.ts(b, 256)]
            if kind == "up":
                return d["w_up"][layer].rearrange("(k p) n -> p k n", p=P)[:, :, bass.ts(b, 256)]
            if kind == "down":
                return d["w_down"][layer].rearrange("(b j p) n -> b p j n", p=P, j=2)[b]
            return d["pool_w"][0].rearrange("g (k p) n -> p (g k) n", p=P)

        def unit_of(layer, kind, b):
            u = FFN_U[layer]
            if isinstance(b, int) and b == 0 and kind != "down":
                return u + (kind == "up")
            if isinstance(b, int) and b == PAIRS - 1 and kind == "down":
                return u + 3 * PAIRS - 1
            return b * 3 + (u + {"gate": -1, "up": 0, "down": 4}[kind])

        def raw_slot(layer, kind, b, par):
            return (par + (kind == "gate")) % 2 if not isinstance(b, int) else unit_of(layer, kind, b) % 2

        HILO = (0, 1, 3)
        GAIN = (0, 16, 8, 24, 32)
        AFTER = (None, 0, 264, 288, 552)
        XF0 = (0, 24, 48, 80, 104)

        ROPE0 = {0: 0, 1: 9, 3: 18, 4: 27}

        def T2(par, n):
            return ps[:, 2 * par:2 * par + 2].rearrange("p a (k n) -> p (a k) n", n=P)[:, :, 0:n]

        def R2(par, n):
            return ps[0:n, 2 * par:2 * par + 2].rearrange("p a n -> p (a n)")

        def b_chunk(w):
            hd, c = divmod(w, 3)
            if c == 2:
                return osam[:, 1, hd], NS, S
            return ob[:, hd, c * 512:(c + 1) * 512], 512, c * 512

        def raw_count(n, slot):
            return 16 * (n // 2 + 1) if isinstance(n, int) else n * 8 + (8 if slot else 16)

        def prompt_dve(dve, mix, it, half):
            tt, ts, stt = dve.tensor_tensor, dve.tensor_scalar, dve.scalar_tensor_tensor
            jj = it * 2 + (mix * 4 + half)
            t0 = (it * 2 + half) * (12 if mix else 24) + (96 if mix else 0)
            t = 0
            for v in range(18):
                if v < 16:
                    i, u = v // 2, jj * 16 + v
                    n = P * (i + 1)
                    dve.wait_ge(s_s, u + 1)
                    if v < 4:
                        dve.memset(small[:, 11:12], 0.0)
                    if v >= 4:
                        dve.wait_ge(s_tp, t0 + groups_through(mix, v - 3 if mix and v % 2 == 0 else v - 4))
                        dve.memset(small[:, 11:12], 0.0)
                    st_ = pstat[:, v % 4]
                    dve.tensor_tensor_reduce(sm[:, v % 4, 0:n], ps[:, 2 * (v % 2):2 * (v % 2) + 2].rearrange("p a n -> p (a n)")[:, 0:n],
                                             pmask[:, S - n:S], 1.0, -3.0e38, ALU.add, ALU.max, st_[:, 0:1]).then_inc(s_sm, 1)
                    dve.wait_ge(s_sm, u + 1)
                    ts(st_[:, 1:2], st_[:, 0:1], -0.125, None, ALU.mult).then_inc(s_nm, 1)
                if 1 <= v < 17:
                    w, u = v - 1, jj * 16 + (v - 1)
                    st_ = pstat[:, w % 4]
                    dve.wait_ge(s_e, u + 1)
                    if mix and w % 2:
                        dve.reciprocal(st_[:, 0:1], st_[:, 2:3]).then_inc(s_rdx, 1)
                        dve.wait_ge(s_rdx, (it * 2 + half) * 8 + (w // 2 + 1))
                        ts(st_[:, 3:4], st_[:, 0:1], small[:, 6:7], None, ALU.mult).then_inc(s_rd, 1)
                        dve.wait_ge(s_rd, u + 1)
                        dve.wait_ge(s_p, (it * 2 + half) * 8 + (64 + w // 2 + 1))
                        n = P * (w // 2 + 1)
                        first = sm[:, (w - 1) % 4, 0:n]
                        stt(first, sm[:, w % 4, 0:n], st_[:, 3:4], first, ALU.mult, ALU.add).then_inc(s_cmb, 1)
                    else:
                        dve.reciprocal(st_[:, 3:4], st_[:, 2:3]).then_inc(s_rd, 1)
                if v >= 2 and not (mix and v % 2 == 0):
                    w = v - 2
                    i, s = w // 2, 0 if mix else w % 2
                    if w == mix:
                        dve.wait_ge(s_pv, jj * 2)
                    if w == 8 + mix:
                        dve.wait_ge(s_pv, jj * 2 + 1)
                    for k0 in range(0, i + 1, 4):
                        cnt = min(4, i + 1 - k0)
                        dve.wait_ge(s_tp, t0 + (t + 1))
                        dve.tensor_copy(pT[:, s, k0:k0 + cnt, (i % 4) * P:(i % 4) * P + P],
                                        ps[:, 4 + t % 2, 0:cnt * P].rearrange("p (k n) -> p k n", n=P)).then_inc(s_tpe, 1)
                        t += 1
                if mix == 0 and v in (14, 17):
                    g = int(v == 17)
                    dve.wait_ge(s_ohi, jj * 2 + (g + 1))
                    o = xn[:, bass.ds(it * 2 + half, 1), :, g * 512:(g + 1) * 512].rearrange("p a q n -> p (a q) n")
                    tt(o[:, 1], ps[:, 6 + g], o[:, 0].bitcast(F32), ALU.subtract).then_inc(s_olo, 1)

        def groups_through(mix, w):
            return sum((x // 2 + 4) // 4 for x in range(w + 1) if x % 2 or not mix)

        def prompt_pe(pe, mix, it, half):
            mm = pe.matmul
            jj = it * 2 + (mix * 4 + half)
            t0 = (it * 2 + half) * (12 if mix else 24) + (96 if mix else 0)
            t = 0
            pe.wait_ge(s_qkv[half], it * 48 + (48 + 96 * mix))
            pe.wait_ge(s_tpe, t0)
            for r in range(4):
                if r >= 2:
                    pe.wait_ge(s_qte, jj * 4 + (r - 1))
                for i in range(4):
                    q_ = pe.transpose(ps[:, 4 + r % 2, i * P:(i + 1) * P], qkv[:, half, r // 2, 4 * (r % 2) + i], ident[:])
                q_.then_inc(s_qt, 1)

            def values(g):
                pe.wait_ge(s_ohi, jj * 2)
                if mix == 0:
                    pe.wait_ge(s_olo, jj * 2)
                else:
                    pe.wait_ge(s_olo, 8)
                pe.wait_ge(s_tpe, t0 + t)
                nk = 4 * (g + 1)
                for kt in range(nk):
                    q0 = max(0, kt - 4 * g) * P
                    for s in range(1 if mix else 2):
                        rows = slice(0, P) if mix else slice(64 * s, 64 * s + 64)
                        q_ = mm(ps[rows, 6 + g, q0:512], qkv[:, half, 2, kt, rows], pT[:, s, kt, q0:512],
                                start=(kt == 0), stop=(kt == nk - 1))
                q_.then_inc(s_pv, 1)

            for v in range(18):
                if v < 16:
                    i, s = v // 2, v % 2
                    n = P * (i + 1)
                    if v == 0:
                        pe.wait_ge(s_qte, jj * 4 + 4)
                    if v < 2:
                        pe.wait_ge(s_sm, jj * 16)
                    else:
                        pe.wait_ge(s_sm, jj * 16 + (v - 1))
                    h64 = slice(64 * s, 64 * s + 64)
                    for a in range(0, n, 512):
                        w = min(512, n - a)
                        q_ = mm(ps[:, 2 * s + a // 512, 0:w], qT[h64, i * P:(i + 1) * P], kT[h64, a:a + w], start=True, stop=True)
                    q_.then_inc(s_s, 1)
                if v == 10 + mix:
                    values(0)
                if v >= 2 and not (mix and v % 2 == 0):
                    w = v - 2
                    i = w // 2
                    if mix:
                        pe.wait_ge(s_cmb, (it * 2 + half) * 8 + (i + 1))
                    else:
                        pe.wait_ge(s_p, jj * 16 + (w + 1))
                    src = sm[:, (w - mix) % 4]
                    for k0 in range(0, i + 1, 4):
                        cnt = min(4, i + 1 - k0)
                        if t >= 2:
                            pe.wait_ge(s_tpe, t0 + (t - 1))
                        for k in range(k0, k0 + cnt):
                            q_ = pe.transpose(ps[:, 4 + t % 2, (k - k0) * P:(k - k0 + 1) * P], src[:, k * P:(k + 1) * P], ident[:])
                        q_.then_inc(s_tp, 1)
                        t += 1
            values(1)

        def TK(j):
            return ps[:, 4 + j % 2].rearrange("p (k n) -> p k n", n=P)

        def sample_cols(row):
            return row[:, 16 + S:PADW].rearrange("p (b t) -> p b t", t=24)

        def by_sample(row):
            return row.rearrange("p (b t) -> p b t", t=T)

        KINDS = ("gate", "up", "down")
        TWOS = (PAIRS - 1) // 2

        @block.sync
        def _(sp):
            sp.dma_start(ident[:], const("ident")).then_inc(s_const, 16)
            for i in range(9):
                n = P if i < 8 else NS
                if i >= 3:
                    sp.wait_ge(s_xt, i - 2)
                src = d["x_prompt"][0, i * P:(i + 1) * P] if i < 8 else d["x_sample"].rearrange("b t n -> (b t) n")
                sp.dma_start(xin[0:n, i % 3], src).then_inc(s_xin[i % 3], 16)
                if i == 1:
                    for name, r0, rows in (("ln_mix", 0, 16), ("ln_ffn", 16, 16), ("ln_final", 32, 8), ("pool_scale", 40, 8),
                                           ("subln_g", 48, 1)):
                        src = d[name] if name == "ln_final" else d[name].rearrange("l n -> (l n)")
                        sp.dma_start(grow[r0:r0 + rows], src.rearrange("(k p) -> k p", p=P)).then_inc(s_const, 16)
                    for j, name in enumerate(("lambda_q1", "lambda_k1", "lambda_q2", "lambda_k2")):
                        sp.dma_start(lamrow[:, j], d[name]).then_inc(s_const, 16)

            w_in = d["w_in"][0].rearrange("(k p) n -> p k n", p=P)
            for m in range(12):
                g, half = divmod(m, 2)
                if m >= 2:
                    sp.wait_ge(s_plo, m - 1)
                sp.dma_start(wpraw[:, m % 2], w_in[:, 4 * half:4 * half + 4, g * 512:(g + 1) * 512]).then_inc(s_praw[m % 2], 16)
                if m == 1:
                    sp.wait_ge(s_xlo, 24)
                    sp.wait_ge(s_xhi, 24)
                    sp.dma_start(cs[:], const("cs").rearrange("p (i c) -> p i c", i=9)).then_inc(s_cs, 16)

            sp.wait_ge(s_tok, 54)
            sp.wait_ge(s_rope, 36)
            for name, dst in (("decA", dmask[:, 0, 0:PAST]), ("newA", dnew[:, 0]), ("newB", dnew[:, 1]), ("comb0", comb[:, 0]),
                              ("comb1", comb[:, 1])):
                sp.dma_start(dst, const(name)).then_inc(s_dc, 16)
            sp.dma_start(ptab[:], d["page_table"].rearrange("b n -> (b n)").rearrange("(a n) -> a n", a=1)).then_inc(s_pt, 16)
            sp.wait_ge(s_pt, 16)

            def load_window(b, raw, name, s):
                sp.dma_start(raw[:, 0], d[name][0, b].rearrange("(p j) h n -> p j (h n)", j=8)).then_inc(s[0], 16)

            def load_pages(pages, raw, name, s):
                for j, page in enumerate(pages):
                    sp.dma_start(raw[:, 1, j], d[name][0, bass.ds(page, 1)].rearrange("a p h n -> p (a h n)")).then_inc(s[1], 16)

            def page_numbers(b):
                return [sp.value_load(ptab[0:1, bass.ds(b * NPAGE + j, 1)], min_val=0, max_val=NPHYS - 1) for j in range(NPAGE)]

            load_window(0, kraw, "cache_win_k_a", s_dk)
            load_window(0, vraw, "cache_win_v_a", s_dv)
            pages = page_numbers(0)
            load_pages(pages, kraw, "cache_k_b", s_dk)
            load_pages(pages, vraw, "cache_v_b", s_dv)
            turned, used = (sp.alloc_register(n) for n in ("turned", "used"))
            for r in (turned, used):
                sp.reg_mov(r, 0)
            with sp.Fori(0, DB - 1) as b:
                pages = page_numbers(b + 1)
                for paged, names in enumerate((("cache_win_k_a", "cache_win_v_a"), ("cache_k_b", "cache_v_b"))):
                    sp.reg_add(turned, turned, 8)
                    sp.reg_add(used, used, 1)
                    n_turned, n_used = (sp.snap(r) for r in (turned, used))
                    for raw, name, s, done, n in ((kraw, names[0], s_dk, s_dtr, n_turned), (vraw, names[1], s_dv, s_dpv, n_used)):
                        sp.wait_ge(done, n)
                        if paged:
                            load_pages(pages, raw, name, s)
                        else:
                            load_window(b + 1, raw, name, s)

            sp.wait_ge(s_dos, 2 * DB)
            for i, n in enumerate((16, 16, 16)):
                sp.wait_ge(s_store[i], 16 * n)
            for mix in range(2):
                if mix:
                    sp.wait_ge(s_sm, 64)
                sp.dma_start(pmask[:], const("maskB" if mix else "maskA")).then_inc(s_pm, 16)
                kn, vn = ("o_kb_p", "o_vb_p") if mix else ("o_wk_p", "o_wv_p")
                srcs = (qs_dram[mix].rearrange("(i p) n -> p i n", p=P),
                        d[kn][0, 0].rearrange("(i p) h n -> p i (h n)", p=P),
                        d[vn][0, 0].rearrange("(i p) h n -> p i (h n)", p=P))
                for j in range(4):
                    if 4 * mix + j >= 2:
                        sp.wait_ge(s_pv, 2 * (4 * mix + j - 1))
                    for a in range(3):
                        sp.dma_start(qkv[:, j % 2, a], srcs[a][:, :, j * P:(j + 1) * P]).then_inc(s_qkv[j % 2], 16)

            sp.wait_ge(s_ol, 13)

            def load(kind, layer, b, n, slot):
                if not (isinstance(n, int) and n < 2):
                    sp.wait_ge(s_wlo, n - 1)
                k = {"down": 2, "pool": 8}.get(kind, 8)
                sp.dma_start(wraw[:, slot].rearrange("p (k n) -> p k n", k=k), unit_src(kind, layer, b)).then_inc(s_raw[slot], 16)

            for u in range(4):
                load("out", 0, u, u, u % 2)
            for layer in range(2):
                def block_loads(layer, b, kinds, par=0):
                    for kind in kinds:
                        load(kind, layer, b, unit_of(layer, kind, b), raw_slot(layer, kind, b, par))

                block_loads(layer, 0, ("gate", "up"))
                with sp.Fori(0, (PAIRS - 1) // 2) as i:
                    block_loads(layer, i * 2 + 1, ("gate", "up"), 1)
                    block_loads(layer, i * 2, ("down",), 0)
                    block_loads(layer, i * 2 + 2, ("gate", "up"), 0)
                    block_loads(layer, i * 2 + 1, ("down",), 1)
                block_loads(layer, PAIRS - 1, ("down",))
                if layer == 0:
                    load("pool", 0, 0, 37, 1)
                    sp.wait_ge(s_acc, FFN_A[0] + PAIRS * ADD_PER)
                    sp.dma_start(corr[:], const("corr").rearrange("p (g n) -> p g n", g=4)).then_inc(s_corr, 16)
                    sp.dma_start(stin[:], d["state_pool"][0].rearrange("b t n -> (b t) n")).then_inc(s_st, 16)

        @block.gpsimd
        def _(pool):
            for g in range(6):
                rot = ROPE0.get(g)
                for i in range(8):
                    t = g * 8 + i
                    if rot is None:
                        pool.wait_ge(s_tok, g * 9 + i + 1)
                    else:
                        pool.wait_ge(s_rope, rot + i + 1)
                    dst = (qs_dram[g // 3, i * P:(i + 1) * P] if g % 3 == 0 else
                           d[{1: "o_wk_p", 2: "o_wv_p", 4: "o_kb_p", 5: "o_vb_p"}[g]][0, 0, i * P:(i + 1) * P]
                           .rearrange("t h n -> t (h n)"))
                    pool.dma_start(dst, tok[:, t % 3]).then_inc(s_store[t % 3], 16)
                if rot is None:
                    pool.wait_ge(s_tok, g * 9 + 9)
                else:
                    pool.wait_ge(s_rope, rot + 9)
                if g in (4, 5):
                    dst = d["o_kb_s" if g == 4 else "o_vb_s"][0].rearrange("b t h n -> (b t) (h n)")
                    pool.dma_start(dst, toks[:, g]).then_inc(s_sstore, 16)
                if g in (1, 2):
                    dst = d["o_wk_s" if g == 1 else "o_wv_s"][0].rearrange("b t h n -> b t (h n)")
                    for b in range(DB):
                        pool.dma_start(dst[b, PAST - T:PAST], toks[b * T:(b + 1) * T, g]).then_inc(s_sstore, 16)

            pool.wait_ge(s_sstore, 16 * (2 + 2 * DB))

            def move_window(b):
                for src, dst in (("cache_win_k_a", "o_wk_s"), ("cache_win_v_a", "o_wv_s")):
                    a, o = (d[n][0, bass.ds(b, 1)].rearrange("a t h n -> (a t) (h n)") for n in (src, dst))
                    pool.dma_start(o[0:PAST - T], a[T:PAST]).then_inc(s_win, 16)

            for mix in range(2):
                with pool.Fori(0, 2) as it:
                    for half in range(2):
                        pool.wait_ge(s_pm, 16 * (mix + 1))
                        move_window(it * 2 + (mix * 4 + half))
                        for v in range(16):
                            if mix and v % 2:
                                continue
                            u = it * 32 + (mix * 64 + half * 16 + v)
                            n = P * (v // 2 + 1)
                            pool.wait_ge(s_rd, u + 1)
                            buf = sm[:, v % 4, 0:n]
                            pool.tensor_tensor(buf, buf, pstat[:, v % 4, 3:4].to_broadcast([P, n]), ALU.mult).then_inc(s_p, 1)

            pool.wait_ge(s_win, 32 * DB)

            pool.wait_ge(s_prow, 2)
            pool.dma_start(d["o_pl_p"][0, 0], prow[0:STATE, 0]).then_inc(s_pout, 16)
            pool.dma_start(d["o_pl_s"][0].rearrange("b t n -> (b t) n"), prow[0:DB * STATE, 1]).then_inc(s_pout, 16)
            pool.wait_ge(s_pout, 32)

            for i in range(9):
                n = P if i < 8 else NS
                pool.wait_ge(s_oe, i + 1)
                dst = d["o_y_p"][0, i * P:(i + 1) * P] if i < 8 else d["o_y_s"].rearrange("b t n -> (b t) n")
                pool.dma_start(dst, yrow[0:n, i % 3]).then_inc(s_out[i % 3], 16)
            for i in range(3):
                pool.wait_ge(s_out[i], 48)

        @block.scalar
        def _(act):
            for i in range(9):
                n = P if i < 8 else NS
                act.wait_ge(s_xt, i + 1)
                act.activation(x[:, :, i * P:i * P + n], T2(i % 2, n), ACT.Copy).then_inc(s_x, 1)
            act.wait_ge(s_lam, 2)
            act.activation(small[0:1, 2:4], small[0:1, 0:2], ACT.Exp).then_inc(s_lamv, 1)

            def norm(r):
                for k in range(KD):
                    if r == 0:
                        act.wait_ge(s_x, 9)
                    else:
                        act.wait_ge(s_added, AFTER[r] + NC * (k + 1))
                    if r == 3 and k == 0:
                        act.wait_ge(s_pot, 1)
                    if 8 * r + k >= 2:
                        act.wait_ge(s_ss, 8 * r + k - 1)
                    act.activation(sq[:, k % 2], x[:, k], ACT.Square).then_inc(s_sq, 1)
                act.wait_ge(s_ss, 8 * r + 8)
                for c, (c0, cn) in enumerate(CH):
                    act.activation(rstd[:, c0:c0 + cn], ps[:, c, 0:cn], ACT.Sqrt, bias=small[:, 8:9], scale=1.0 / D).then_inc(s_rt, 1)
                if r in HILO:
                    for c, (c0, cn) in enumerate(CH):
                        for k in range(KD):
                            f = c * KD + k
                            act.wait_ge(s_xf, XF0[r] + f + 1)
                            act.activation(xn[:, k, 0, c0:c0 + cn], xf[:, f % 4, 0:cn], ACT.Copy).then_inc(s_xhi, 1)

            norm(0)

            def proj_hi(m):
                g, half = divmod(m, 2)
                act.wait_ge(s_praw[m % 2], 16 * (m // 2 + 1))
                if g >= 2:
                    act.wait_ge(s_proj, 9 * (g - 1))
                act.activation(wp[:, g % 2, 0, 4 * half:4 * half + 4], wpraw[:, m % 2], ACT.Copy).then_inc(s_phi, 1)

            for m in range(4):
                proj_hi(m)
            for g in range(6):
                for i in range(9):
                    n = P if i < 8 else NS
                    m = g * 9 + i
                    act.wait_ge(s_proj, m + 1)
                    if i < 8:
                        t = g * 8 + i
                        if t >= 3:
                            act.wait_ge(s_store[t % 3], 16 * (t // 3))
                        act.activation(tok[:, t % 3], ps[:, m % 8], ACT.Copy).then_inc(s_tok, 1)
                    else:
                        act.activation(toks[:, g], ps[0:NS, m % 8], ACT.Copy).then_inc(s_tok, 1)
                if g + 2 < 6:
                    proj_hi(2 * g + 4)
                    proj_hi(2 * g + 5)

            def dec_evac(tr):
                for j in range(0, 8, 2):
                    act.wait_ge(s_dtr, tr + j + 1)
                    act.activation(dkT[:, :, j * P:(j + 1) * P], TK(j), ACT.Copy).then_inc(s_dea, 1)

            def out_rows(dd):
                act.wait_ge(s_dpv, dd + 1)
                act.activation(dom[:], ps[:, 3, 0:P], ACT.Copy).then_inc(s_dom, 1)

            def to_osam(b, m):
                act.wait_ge(s_dot, b * 2 + (m + 1))
                act.activation(osam[:, m, :, bass.ds(b * T, T)], ps[:, 3, 256:288].rearrange("p (j t) -> p j t", t=T),
                               ACT.Copy).then_inc(s_dos, 1)

            def dec_act(b, m, last=False):
                dd = b * 2 + m
                first = isinstance(dd, int) and dd == 0
                act.wait_ge(s_dnm, dd + 1)
                act.activation(dse[:, m], dse[:, m], ACT.Exp, bias=dstat[:, m, 1:2], scale=0.125,
                               accum_out=dstat[:, m, 2:3]).then_inc(s_de, 1)
                if not first:
                    out_rows(b * 2 + (m - 1))
                if not last:
                    act.wait_ge(s_ds, dd + 1)
                    dec_evac(dd * 8 + 8)
                if not first:
                    to_osam(*((b, 0) if m else (b - 1, 1)))

            dec_evac(0)
            dec_act(0, 0)
            dec_act(0, 1)
            with act.Fori(1, DB - 1) as b:
                dec_act(b, 0)
                dec_act(b, 1)
            dec_act(DB - 1, 0)
            dec_act(DB - 1, 1, True)
            out_rows(2 * DB - 1)
            to_osam(DB - 1, 1)

            for mix in range(2):
                with act.Fori(0, 2) as it:
                    for half in range(2):
                        jj = it * 2 + (mix * 4 + half)
                        for r in range(4):
                            act.wait_ge(s_qt, jj * 4 + (r + 1))
                            dst = (qT, kT)[r // 2][:, (r % 2) * 512:(r % 2) * 512 + 512]
                            act.activation(dst, ps[:, 4 + r % 2], ACT.Copy).then_inc(s_qte, 1)
                        for v in range(17):
                            if v < 16:
                                u = jj * 16 + v
                                n = P * (v // 2 + 1)
                                act.wait_ge(s_nm, u + 1)
                                act.activation(sm[:, v % 4, 0:n], sm[:, v % 4, 0:n], ACT.Exp, bias=pstat[:, v % 4, 1:2],
                                               scale=0.125, accum_out=pstat[:, v % 4, 2:3]).then_inc(s_e, 1)
                            if v in (13, 16):
                                g = int(v == 16)
                                act.wait_ge(s_pv, jj * 2 + (g + 1))
                                if mix == 0:
                                    dst = xn[:, bass.ds(it * 2 + half, 1), 0, g * 512:(g + 1) * 512].rearrange("p a n -> p (a n)")
                                else:
                                    dst = ob[:, bass.ds(it * 2 + half, 1), g * 512:(g + 1) * 512].rearrange("p a n -> p (a n)")
                                act.activation(dst, ps[:, 6 + g], ACT.Copy).then_inc(s_ohi, 1)
            act.activation(xn[:, 0:4, 0, S:NT], osam[:, 0], ACT.Copy).then_inc(s_oh, 1)
            for w in range(13):
                if w < 12:
                    if w >= 2:
                        act.wait_ge(s_oss, w - 1)
                    src, n, _ = b_chunk(w)
                    act.wait_ge(s_ohi, 16)
                    act.activation(osq[:, w % 2, 0:n], src, ACT.Square).then_inc(s_osq, 1)
                if w >= 1:
                    src, n, _ = b_chunk(w - 1)
                    act.wait_ge(s_oss, w)
                    act.activation(orms[:, w - 1, 0:n], ps[:, (w - 1) % 2, 0:n], ACT.Sqrt, bias=small[:, 9:10],
                                   scale=1.0 / P).then_inc(s_ort, 1)
            for w in range(12):
                src, n, t0 = b_chunk(w)
                act.wait_ge(s_osc, w + 1)
                act.activation(xn[:, 4 + w // 3, 0, t0:t0 + n], src, ACT.Copy).then_inc(s_oh, 1)

            def hi(n, slot, dst):
                act.wait_ge(s_raw[slot], raw_count(n, slot))
                act.activation(dst[:, 0], wraw[:, slot], ACT.Copy).then_inc(s_whi, 1)

            def ffn_hi(layer, b, kinds, par=0):
                for kind in kinds:
                    if kind == "down":
                        act.wait_ge(s_acc, b * ADD_PER + FFN_A[layer])
                    elif isinstance(b, int) and b == 0:
                        act.wait_ge(s_acc, FFN_A[layer])
                    else:
                        act.wait_ge(s_gu, b * GU_PER + FFN_G[layer])
                    hi(unit_of(layer, kind, b), raw_slot(layer, kind, b, par), ws[KINDS.index(kind)])

            def hidden(layer, b, par):
                g0 = b * GU_PER + FFN_G[layer]
                first = isinstance(b, int) and b == 0
                act.wait_ge(s_acc, FFN_A[layer] if first else b * ADD_PER + (FFN_A[layer] - ADD_PER))
                for n in range(GU_PER + 1):
                    if n < GU_PER:
                        act.wait_ge(s_gu, g0 + (n + 1))
                        if not (first and layer == 0 and n < 2):
                            act.wait_ge(s_h, g0 + (n - 1))
                        cn = CH[n % NC][1]
                        act.activation(act_s[:, n % 2, 0:cn], ps[:, 2 * (n % 2), 0:cn], ACT.Silu).then_inc(s_silu, 1)
                    if n >= 1:
                        j, c = divmod(n - 1, NC)
                        c0, cn = CH[c]
                        act.wait_ge(s_h, g0 + n)
                        act.activation(hh[:, par, j, 0, c0:c0 + cn], act_h[:, (n - 1) % 2, 0:cn], ACT.Copy).then_inc(s_hhi, 1)
                    if n == 2 and not first:
                        ffn_hi(layer, b - 1, ("down",), 1 - par)

            def ffn(layer):
                def two(i, last):
                    hidden(layer, i * 2 + 1, 1)
                    ffn_hi(layer, i * 2 + 2, ("gate", "up"), 0)
                    hidden(layer, i * 2 + 2, 0)
                    if not last:
                        ffn_hi(layer, i * 2 + 3, ("gate", "up"), 1)
                ffn_hi(layer, 0, ("gate", "up"))
                norm(1 + 2 * layer)
                act.wait_ge(s_xlo, 24 * (2 + layer))
                if layer == 1:
                    act.wait_ge(s_pout, 32)
                hidden(layer, 0, 0)
                ffn_hi(layer, 1, ("gate", "up"))
                with act.Fori(0, TWOS - 1) as i:
                    two(i, False)
                two(TWOS - 1, True)
                ffn_hi(layer, PAIRS - 1, ("down",))

            for u in range(4):
                if u == 3:
                    act.wait_ge(s_acc, 6)
                hi(u, u % 2, ws[u % 3])
            ffn(0)
            act.wait_ge(s_gu, FFN_G[1])
            hi(37, 1, ws[0])
            norm(2)
            for k in range(KD):
                act.wait_ge(s_pf, k + 1)
                act.activation(xn[:, k, 0], pf[:], ACT.Copy).then_inc(s_pfh, 1)
            act.wait_ge(s_pot, 1)
            act.activation(prow[0:STATE, 0], R2(0, STATE), ACT.Copy).then_inc(s_prow, 1)
            act.activation(prow[0:DB * STATE, 1], R2(1, DB * STATE), ACT.Copy).then_inc(s_prow, 1)
            ffn(1)
            norm(4)
            for i in range(9):
                n = P if i < 8 else NS
                act.wait_ge(s_ot, i + 1)
                if i >= 3:
                    act.wait_ge(s_out[i % 3], 16 * (i // 3))
                act.activation(yrow[0:n, i % 3], R2(i % 2, n), ACT.Copy).then_inc(s_oe, 1)

        @block.vector
        def _(dve):
            tt, ts, stt = dve.tensor_tensor, dve.tensor_scalar, dve.scalar_tensor_tensor
            dve.memset(ones[:], 1.0).then_inc(s_ones, 1)
            dve.memset(small[:, 8:9], 1e-6).then_inc(s_ones, 1)
            dve.memset(small[:, 9:10], 1e-5).then_inc(s_ones, 1)
            dve.wait_ge(s_const, 160)
            for j in range(2):
                dve.tensor_tensor_reduce(lamtmp[:, j], lamrow[:, 2 * j], lamrow[:, 2 * j + 1], 1.0, 0.0, ALU.mult, ALU.add,
                                         small[0:1, j:j + 1]).then_inc(s_lam, 1)
            dve.wait_ge(s_gt, 1)
            dve.tensor_copy(gains[:], ps[:, 6, 0:49]).then_inc(s_gains, 1)
            dve.wait_ge(s_lamv, 1)
            tt(small[0:1, 10:11], small[0:1, 2:3], small[0:1, 3:4], ALU.subtract).then_inc(s_small, 1)
            dve.wait_ge(s_small, 1)
            ts(small[0:1, 4:5], small[0:1, 10:11], LAM0, None, ALU.add).then_inc(s_small, 1)
            dve.wait_ge(s_lamb, 1)
            dve.tensor_copy(small[:, 5:6], ps[:, 7, 0:1]).then_inc(s_small, 1)
            ts(small[:, 6:7], ps[:, 7, 0:1], -1.0, None, ALU.mult).then_inc(s_small, 1)
            dve.wait_ge(s_gains, 1)
            ts(small[:, 7:8], gains[:, 48:49], 1.0 - LAM0, None, ALU.mult).then_inc(s_small, 1)
            dve.wait_ge(s_small, 5)

            def norm(r):
                if r == 0:
                    dve.wait_ge(s_x, 9)
                for c, (c0, cn) in enumerate(CH):
                    dve.wait_ge(s_rt, NC * r + c + 1)
                    dve.reciprocal(rstd[:, c0:c0 + cn], rstd[:, c0:c0 + cn]).then_inc(s_rstd, 1)
                f0 = XF0[r]
                if r == 2:
                    pieces = ((0, 364), (364, 364), (728, 296), (S, NS))
                else:
                    pieces = CH
                h0 = 24 * HILO.index(r) if r in HILO else None

                def low(f):
                    c, k = divmod(f, KD)
                    c0, cn = CH[c]
                    dve.wait_ge(s_xhi, h0 + f + 1)
                    tt(xn[:, k, 1, c0:c0 + cn], xf[:, f % 4, 0:cn], xn[:, k, 0, c0:c0 + cn].bitcast(F32), ALU.subtract).then_inc(s_xlo, 1)

                for c, (c0, cn) in enumerate(pieces):
                    dve.wait_ge(s_rstd, NC * r + min(c, 2) + 1)
                    for k in range(KD):
                        f = c * KD + k
                        src, rs = x[:, k, c0:c0 + cn], rstd[:, c0:c0 + cn]
                        if r in HILO:
                            dst = xf[:, f % 4, 0:cn]
                            if f >= 4:
                                dve.wait_ge(s_xlo, h0 + f - 3)
                        elif r == 4:
                            dst = yf[:, k, c0:c0 + cn]
                        elif c < 3:
                            dst = yp[:, k, 16 + c0:16 + c0 + cn]
                        else:
                            dst, src, rs = sample_cols(yp[:, k])[:, :, 16:24], by_sample(src), by_sample(rs)
                        stt(dst, src, gains[:, GAIN[r] + k:GAIN[r] + k + 1], rs, ALU.mult, ALU.mult).then_inc(s_xf, 1)
                        if r in HILO and f >= 2:
                            low(f - 2)
                if r in HILO:
                    low(22)
                    low(23)
                    dve.wait_ge(s_xlo, h0 + 24)

            def proj_lo(m):
                g, half = divmod(m, 2)
                dve.wait_ge(s_phi, m + 1)
                part = wp[:, g % 2, :, 4 * half:4 * half + 4]
                tt(part[:, 1], wpraw[:, m % 2], part[:, 0].bitcast(F32), ALU.subtract).then_inc(s_plo, 1)

            norm(0)
            for m in range(4):
                proj_lo(m)
            dve.wait_ge(s_cs, 16)
            for g in range(6):
                for i in range(9 if g in ROPE0 else 0):
                    n = P if i < 8 else NS
                    rows = tok[:, (g * 8 + i) % 3] if i < 8 else toks[:, g]
                    c = ROPE0[g] + i
                    r16 = rows.rearrange("p (h c) -> p h c", c=64)[:, :, 0:16]
                    co = rope[0:n, c % 2, 0].rearrange("p (h c) -> p h c", c=16)
                    si = rope[0:n, c % 2, 1].rearrange("p (h c) -> p h c", c=16)
                    dve.wait_ge(s_tok, g * 9 + i + 1)
                    tt(co, r16, cs[0:n, i:i + 1, 0:16].to_broadcast([n, 8, 16]), ALU.mult).then_inc(s_ropeP, 1)
                    tt(si, r16, cs[0:n, i:i + 1, 16:32].to_broadcast([n, 8, 16]), ALU.mult).then_inc(s_ropeP, 1)
                    dve.wait_ge(s_ropeP, 2 * c + 2)
                    tt(r16[:, :, 0:8], co[:, :, 0:8], si[:, :, 8:16], ALU.subtract)
                    tt(r16[:, :, 8:16], co[:, :, 8:16], si[:, :, 0:8], ALU.add).then_inc(s_rope, 1)
                if g + 2 < 6:
                    proj_lo(2 * g + 4)
                    proj_lo(2 * g + 5)

            dve.wait_ge(s_dc, 80)
            dve.memset(dmask[:, 1, 0:PAST], 0.0).then_inc(s_dmk, 1)
            dve.memset(qblk[:], 0.0).then_inc(s_qz, 1)
            stt(comb[:, 2], comb[:, 1], small[:, 6:7], comb[:, 0], ALU.mult, ALU.add).then_inc(s_cmbd, 1)
            dve.wait_ge(s_qz, 1)
            dve.wait_ge(s_qk, 4)
            for m in range(2):
                for jp in range(4):
                    for hf in range(2):
                        h64 = slice(64 * hf, 64 * hf + 64)
                        dve.tensor_copy(qblk[h64, m, :, jp, 8 * hf:8 * hf + 8],
                                        ps[h64, 2 * m, 64 * jp:64 * jp + 64].rearrange("p (b t) -> p b t", t=T)).then_inc(s_qb, 1)
                dve.tensor_copy(knT[:, m], ps[:, 2 * m + 1, 0:256].rearrange("p (j n) -> p j n", n=NS)).then_inc(s_qb, 1)
            dve.wait_ge(s_qb, 18)

            def next_q(b, m):
                dve.tensor_copy(qcur[:, m], qblk[:, m, bass.ds(b, 1)].rearrange("p a j n -> p (a j) n")).then_inc(s_qc, 1)
                dve.tensor_copy(dmask[:, m, PAST:PAST + NS], dnew[:, m, bass.ds(b * -8 + 56, NS)]).then_inc(s_dmk, 1)

            def dec_evac(tr):
                for j in range(1, 8, 2):
                    dve.wait_ge(s_dtr, tr + j + 1)
                    dve.tensor_copy(dkT[:, :, j * P:(j + 1) * P], TK(j)).then_inc(s_dev, 1)

            def dec_dve(b, m, final):
                dd = b * 2 + m
                dve.wait_ge(s_ds, dd + 1)
                dve.wait_ge(s_dmk, dd + 2)
                dve.memset(small[:, 11:12], 0.0)
                dve.tensor_tensor_reduce(dse[:, m], ps[:, 0:3].rearrange("p a n -> p (a n)")[:, 0:PAST + NS], dmask[:, m], 1.0,
                                         -3.0e38, ALU.add, ALU.max, dstat[:, m, 0:1]).then_inc(s_dsm, 1)
                dve.wait_ge(s_dsm, dd + 1)
                ts(dstat[:, m, 1:2], dstat[:, m, 0:1], -0.125, None, ALU.mult).then_inc(s_dnm, 1)
                if not final:
                    next_q(b + 1, m)
                if not (final and m):
                    dec_evac(dd * 8 + 8)
                dve.wait_ge(s_de, dd + 1)
                dve.reciprocal(dstat[:, m, 3:4], dstat[:, m, 2:3]).then_inc(s_drd, 1)
                dve.wait_ge(s_drd, dd + 1)
                mix_w = (dmix[:, 1, 0:32], comb[:, 2]) if m else (dmix[:, 0], comb[:, 0:2].rearrange("p a n -> p (a n)"))
                ts(*mix_w, dstat[:, m, 3:4], None, ALU.mult).then_inc(s_dmx, 1)
                dve.wait_ge(s_dpt, dd + 1)
                dve.tensor_copy(dpT[:, m, 0:8], ps[:, 6:8].rearrange("p a (k n) -> p (a k) n", n=P))
                dve.tensor_copy(dpT[0:64, m, 8], ps[0:64, 3, P:2 * P]).then_inc(s_dpe, 1)

            next_q(0, 0)
            next_q(0, 1)
            dec_evac(0)
            with dve.Fori(0, DB - 1) as b:
                dec_dve(b, 0, False)
                dec_dve(b, 1, False)
            dec_dve(DB - 1, 0, True)
            dec_dve(DB - 1, 1, True)

            for mix in range(2):
                dve.wait_ge(s_pm, 16 * (mix + 1))
                with dve.Fori(0, 2) as it:
                    for half in range(2):
                        prompt_dve(dve, mix, it, half)
            dve.wait_ge(s_oh, 1)
            tt(xn[:, 0:4, 1, S:NT], osam[:, 0], xn[:, 0:4, 0, S:NT].bitcast(F32), ALU.subtract).then_inc(s_ol, 1)
            for w in range(13):
                if w < 12:
                    src, n, _ = b_chunk(w)
                    dve.wait_ge(s_ort, w + 1)
                    dve.reciprocal(orms[:, w, 0:n], orms[:, w, 0:n]).then_inc(s_orr, 1)
                    dve.wait_ge(s_orr, w + 1)
                    stt(src, src, small[:, 7:8], orms[:, w, 0:n], ALU.mult, ALU.mult).then_inc(s_osc, 1)
                if w >= 1:
                    src, n, t0 = b_chunk(w - 1)
                    dve.wait_ge(s_oh, w + 1)
                    o = xn[:, 4 + (w - 1) // 3, :, t0:t0 + n]
                    tt(o[:, 1], src, o[:, 0].bitcast(F32), ALU.subtract).then_inc(s_ol, 1)

            def lo(n, slot, dst):
                dve.wait_ge(s_whi, n + 1)
                tt(dst[:, 1], wraw[:, slot], dst[:, 0].bitcast(F32), ALU.subtract).then_inc(s_wlo, 1)

            def ffn_lo(layer, b, kind, par=0):
                lo(unit_of(layer, kind, b), raw_slot(layer, kind, b, par), ws[KINDS.index(kind)])

            def add(a, idx, scale=None):
                k, c = divmod(idx, NC)
                c0, cn = CH[c]
                dst = x[:, k, c0:c0 + cn]
                dve.wait_ge(s_acc, a + 1)
                if scale is None:
                    tt(dst, ps[:, 4 + idx % 4, 0:cn], dst, ALU.add).then_inc(s_added, 1)
                else:
                    stt(dst, ps[:, 4 + idx % 4, 0:cn], scale, dst, ALU.mult, ALU.add).then_inc(s_added, 1)

            def hidden(layer, b, par):
                g0 = b * GU_PER + FFN_G[layer]
                first = isinstance(b, int) and b == 0
                for n in range(GU_PER + 1):
                    if n < GU_PER:
                        dve.wait_ge(s_silu, g0 + (n + 1))
                        if not (first and layer == 0 and n < 2):
                            dve.wait_ge(s_hlo, g0 + (n - 1))
                        cn = CH[n % NC][1]
                        tt(act_h[:, n % 2, 0:cn], act_s[:, n % 2, 0:cn], ps[:, 2 * (n % 2) + 1, 0:cn], ALU.mult).then_inc(s_h, 1)
                    if n >= 1:
                        j, c = divmod(n - 1, NC)
                        c0, cn = CH[c]
                        dve.wait_ge(s_hhi, g0 + n)
                        o = hh[:, par, j, :, c0:c0 + cn]
                        tt(o[:, 1], act_h[:, (n - 1) % 2, 0:cn], o[:, 0].bitcast(F32), ALU.subtract).then_inc(s_hlo, 1)
                    if n == 3 and not first:
                        ffn_lo(layer, b - 1, "down", 1 - par)

            def adds(layer, b, splits=()):
                for idx in range(ADD_PER):
                    add(b * ADD_PER + (FFN_A[layer] + idx), idx)
                    if splits and idx in (2, 6):
                        ffn_lo(layer, splits[0], ("gate", "up")[idx == 6], splits[1])

            def ffn(layer):
                def two(i, last):
                    hidden(layer, i * 2 + 1, 1)
                    adds(layer, i * 2, (i * 2 + 2, 0))
                    hidden(layer, i * 2 + 2, 0)
                    adds(layer, i * 2 + 1, () if last else (i * 2 + 3, 1))
                ffn_lo(layer, 0, "gate")
                ffn_lo(layer, 0, "up")
                norm(1 + 2 * layer)
                if layer == 1:
                    dve.wait_ge(s_pout, 32)
                hidden(layer, 0, 0)
                ffn_lo(layer, 1, "gate")
                ffn_lo(layer, 1, "up")
                with dve.Fori(0, TWOS - 1) as i:
                    two(i, False)
                two(TWOS - 1, True)
                ffn_lo(layer, PAIRS - 1, "down")
                adds(layer, PAIRS - 1)

            for u in range(3):
                lo(u, u % 2, ws[u])
            for idx in range(ADD_PER):
                add(idx, idx)
                if idx == 5:
                    lo(3, 1, ws[0])
            ffn(0)

            lo(37, 1, ws[0])
            dve.memset(yp[:, :, 0:16], 0.0)
            dve.memset(yp[:, :, 16 + S:PADW].rearrange("p k (b t) -> p k b t", t=24)[:, :, :, 0:1], 0.0).then_inc(s_pz, 1)
            dve.wait_ge(s_stt, 1)
            for a in range(2):
                src = ps[:, 4 + a].rearrange("p (k n) -> p k n", n=P)[:, :, 0:DB * STATE]
                for k in range(4):
                    dve.tensor_copy(sample_cols(yp[:, 4 * a + k])[:, :, 1:16], src[:, k].rearrange("p (b t) -> p b t", t=STATE)).then_inc(s_yp, 1)
            norm(2)
            dve.wait_ge(s_yp, 8)
            dve.wait_ge(s_pz, 1)
            dve.wait_ge(s_xf, XF0[3])
            dve.tensor_copy(pcomp[:, :, 0:STATE], yp[:, :, 1 + S:16 + S])
            for k in range(KD):
                dve.tensor_copy(pcomp[:, k, STATE:].rearrange("p (b t) -> p b t", t=STATE), sample_cols(yp[:, k])[:, :, 9:24]).then_inc(s_pc, 1)
            level = 0
            dve.wait_ge(s_corr, 16)
            for k in range(KD):
                g = k // 2
                src = yp[:, k]
                lead = 1
                if k:
                    dve.wait_ge(s_pfl, k)
                for e in range(g + 1):
                    dst = pa[:, e % 2]
                    step = 1 << e
                    if e:
                        dve.wait_ge(s_lvl, level)
                    tt(dst[:, lead:PADW], src[:, lead:PADW], src[:, lead - step:PADW - step], ALU.add).then_inc(s_lvl, 1)
                    level += 1
                    src = dst
                    lead += 2 * step
                dve.wait_ge(s_lvl, level)
                tt(src[:, 16:32], src[:, 16:32], corr[:, g], ALU.mult).then_inc(s_lvl, 1)
                level += 1
                dve.wait_ge(s_lvl, level)
                w = 0.5 / (1 << g)
                stt(pf[:, 0:S], src[:, 16:16 + S], w, yp[:, k, 16:16 + S], ALU.mult, ALU.subtract)
                stt(by_sample(pf[:, S:NT]), sample_cols(src)[:, :, 16:24], w, sample_cols(yp[:, k])[:, :, 16:24],
                    ALU.mult, ALU.subtract).then_inc(s_pf, 1)
                dve.wait_ge(s_pfh, k + 1)
                dve.wait_ge(s_pf, k + 1)
                tt(xn[:, k, 1], pf[:], xn[:, k, 0].bitcast(F32), ALU.subtract).then_inc(s_pfl, 1)
            for idx in range(ADD_PER):
                kk = idx // NC
                add(PAIRS * ADD_PER + FFN_A[0] + idx, idx, gains[:, 40 + kk:41 + kk])
            ffn(1)
            norm(4)

        @block.tensor
        def _(pe):
            mm = pe.matmul

            def product(out, pairs, last=None):
                n = len(pairs)
                for i, (w, m) in enumerate(pairs):
                    for q_, (a, b_) in enumerate(((1, 0), (0, 1), (0, 0))):
                        r = mm(out, w(a), m(b_), start=(i == 0 and q_ == 0), stop=(i == n - 1 and q_ == 2))
                return r

            pe.wait_ge(s_const, 160)
            for i in range(9):
                n = P if i < 8 else NS
                pe.wait_ge(s_xin[i % 3], 16 * (i // 3 + 1))
                if i >= 2:
                    pe.wait_ge(s_x, i - 1)
                for k in range(KD):
                    r = pe.transpose(T2(i % 2, n)[:, k], xin[0:n, i % 3, k * P:(k + 1) * P], ident[0:n, 0:n])
                r.then_inc(s_xt, 1)
            pe.transpose(ps[:, 6, 0:49], grow[:], ident[0:49, 0:49]).then_inc(s_gt, 1)
            pe.wait_ge(s_ones, 3)
            pe.wait_ge(s_small, 2)
            mm(ps[:, 7, 0:1], ones[0:1, :], small[0:1, 4:5], start=True, stop=True).then_inc(s_lamb, 1)

            def norm(r):
                for k in range(KD):
                    pe.wait_ge(s_sq, 8 * r + k + 1)
                    if r == 0 and k == 0:
                        pe.wait_ge(s_x, 9)
                    for c, (c0, cn) in enumerate(CH):
                        q_ = mm(ps[:, c, 0:cn], ones[:], sq[:, k % 2, c0:c0 + cn], start=(k == 0), stop=(k == KD - 1))
                    q_.then_inc(s_ss, 1)

            norm(0)
            for g in range(6):
                pe.wait_ge(s_plo, 2 * g + 2)
                for i in range(9):
                    n = P if i < 8 else NS
                    m = g * 9 + i
                    if g == 0:
                        c = 0 if i < 2 else 1 if i < 5 else 2
                        pe.wait_ge(s_xlo, 8 * (c + 1))
                    if m >= 8:
                        pe.wait_ge(s_tok, m - 7)
                    elif m < 3:
                        pe.wait_ge(s_rt, 3)
                    elif m >= 6:
                        pe.wait_ge(s_small, 5)
                    product(ps[0:n, m % 8], [(lambda a, k=k: xn[:, k, a, i * P:i * P + n], lambda a, k=k: wp[:, g % 2, a, k])
                                             for k in range(KD)]).then_inc(s_proj, 1)

            pe.wait_ge(s_tok, 54)
            pe.wait_ge(s_rope, 36)
            for m in range(2):
                for a in range(2):
                    for jp in range(4):
                        q_ = pe.transpose(ps[:, 2 * m + a, 64 * jp:64 * jp + 64], toks[:, 3 * m + a, jp * P:(jp + 1) * P], ident[0:NS, 0:NS])
                    q_.then_inc(s_qk, 1)

            def dec_transposes(b, m):
                dd = b * 2 + m
                first = isinstance(b, int) and b == 0 and m == 0
                pe.wait_ge(s_dk[m], (b + 1) * (128 if m else 16))
                for j in range(8):
                    if not (first and j < 2):
                        pe.wait_ge(s_dev if j % 2 else s_dea, dd * 4 + j // 2)
                    for jp in range(4):
                        q_ = pe.transpose(TK(j)[:, jp], kraw[:, m, j, jp * P:(jp + 1) * P], ident[:])
                    q_.then_inc(s_dtr, 1)

            def dec_scores(b, m):
                dd = b * 2 + m
                pe.wait_ge(s_qc, dd + 1)
                pe.wait_ge(s_dea, dd * 4 + 4)
                pe.wait_ge(s_dev, dd * 4 + 4)
                if not (isinstance(dd, int) and dd == 0):
                    pe.wait_ge(s_dsm, dd)
                for a in range(3):
                    for jp in range(4):
                        mv = knT[:, m, jp] if a == 2 else dkT[:, jp, a * 512:(a + 1) * 512]
                        q_ = mm(ps[32 * jp:32 * jp + 32, a, 0:(64 if a == 2 else 512)], qcur[:, m, jp], mv, start=True, stop=True)
                q_.then_inc(s_ds, 1)

            def dec_turn(dd, m):
                pe.wait_ge(s_de, dd + 1)
                pe.wait_ge(s_dpe, dd)
                for j in range(8):
                    if j == 7:
                        pe.wait_ge(s_dos, dd)
                    pe.transpose(ps[:, 6 + j // 4, (j % 4) * P:(j % 4 + 1) * P], dse[:, m, j * P:(j + 1) * P], ident[:])
                pe.transpose(ps[0:NS, 3, P:2 * P], dse[:, m, PAST:PAST + NS], ident[:]).then_inc(s_dpt, 1)

            def dec_values(b, m):
                dd = b * 2 + m
                pe.wait_ge(s_dpe, dd + 1)
                pe.wait_ge(s_dom, dd)
                pe.wait_ge(s_dv[m], (b + 1) * (128 if m else 16))
                for j in range(9):
                    for jp in range(4):
                        rows, cols = slice(32 * jp, 32 * jp + 32), slice(jp * P, (jp + 1) * P)
                        w, v = ((dpT[:, m, j, rows], vraw[:, m, j, cols]) if j < 8 else
                                (dpT[0:NS, m, 8, rows], toks[:, 3 * m + 2, cols]))
                        q_ = mm(ps[rows, 3, 0:P], w, v, start=(j == 0), stop=(j == 8))
                q_.then_inc(s_dpv, 1)

            def dec_combine(dd, m):
                pe.wait_ge(s_dom, dd + 1)
                pe.wait_ge(s_dmx, dd + 1)
                if m:
                    mm(ps[:, 3, 256:288], dom[:], dmix[:, 1, 0:32], start=True, stop=True).then_inc(s_dot, 1)
                else:
                    for hf in range(2):
                        h64 = slice(64 * hf, 64 * hf + 64)
                        q_ = mm(ps[h64, 3, 256:288], dom[:, h64], dmix[:, 0, 32 * hf:32 * hf + 32], start=True, stop=True)
                    q_.then_inc(s_dot, 1)

            def dec_step(b, m, last=False):
                dd = b * 2 + m
                nxt = (b + 1, 0) if m else (b, 1)
                if not last:
                    dec_transposes(*nxt)
                if not (isinstance(dd, int) and dd == 0):
                    dec_combine(b * 2 + (m - 1), 1 - m)
                dec_turn(dd, m)
                if not last:
                    dec_scores(*nxt)
                dec_values(b, m)

            dec_transposes(0, 0)
            dec_scores(0, 0)
            dec_step(0, 0)
            dec_step(0, 1)
            with pe.Fori(1, DB - 1) as b:
                dec_step(b, 0)
                dec_step(b, 1)
            dec_step(DB - 1, 0)
            dec_step(DB - 1, 1, True)
            dec_combine(2 * DB - 1, 1)

            for mix in range(2):
                with pe.Fori(0, 2) as it:
                    for half in range(2):
                        prompt_pe(pe, mix, it, half)
            for w in range(12):
                _, n, _ = b_chunk(w)
                pe.wait_ge(s_osq, w + 1)
                if w >= 2:
                    pe.wait_ge(s_ort, w - 1)
                mm(ps[:, w % 2, 0:n], ones[:], osq[:, w % 2, 0:n], start=True, stop=True).then_inc(s_oss, 1)

            def group(a, idx, pairs):
                k, c = divmod(idx, NC)
                if not isinstance(a, int) or a >= 4:
                    pe.wait_ge(s_added, a - 3)
                product(ps[:, 4 + idx % 4, 0:CH[c][1]], pairs).then_inc(s_acc, 1)

            def moving(k, c):
                c0, cn = CH[c]
                return lambda a: xn[:, k, a, c0:c0 + cn]

            pe.wait_ge(s_ol, 13)
            for idx in range(ADD_PER):
                kt, c = divmod(idx, NC)
                u, e = divmod(kt, 2)
                pe.wait_ge(s_wlo, u + 1)
                group(idx, idx, [(lambda a, k=k: ws[u % 3][:, a, k * 256 + e * P:k * 256 + e * P + P], moving(k, c)) for k in range(KD)])

            def hidden(layer, b):
                g0 = b * GU_PER + FFN_G[layer]
                first = isinstance(b, int) and b == 0
                pe.wait_ge(s_wlo, unit_of(layer, "up", b) + 1)
                for n in range(GU_PER):
                    j, c = divmod(n, NC)
                    if first and j == 0:
                        f0 = 24 * (1 + layer) + 8 * (c + 1)
                        pe.wait_ge(s_xlo, f0)
                    if not (first and layer == 0 and n < 2):
                        pe.wait_ge(s_h, g0 + (n - 1))
                    elif n == 0:
                        pe.wait_ge(s_rt, 6)
                    for a_ in range(2):
                        q_ = product(ps[:, 2 * (n % 2) + a_, 0:CH[c][1]],
                                     [(lambda a, k=k: ws[a_][:, a, k * 256 + j * P:k * 256 + j * P + P], moving(k, c)) for k in range(KD)])
                    q_.then_inc(s_gu, 1)

            def down(layer, b, par):
                pe.wait_ge(s_hlo, b * GU_PER + (FFN_G[layer] + GU_PER))
                pe.wait_ge(s_wlo, unit_of(layer, "down", b) + 1)
                for idx in range(ADD_PER):
                    kt, c = divmod(idx, NC)
                    c0, cn = CH[c]
                    group(b * ADD_PER + (FFN_A[layer] + idx), idx,
                          [(lambda a, j=j: ws[2][:, a, j * D + kt * P:j * D + kt * P + P], lambda a, j=j: hh[:, par, j, a, c0:c0 + cn])
                           for j in range(2)])

            def ffn(layer):
                norm(1 + 2 * layer)
                hidden(layer, 0)
                with pe.Fori(0, TWOS) as i:
                    hidden(layer, i * 2 + 1)
                    down(layer, i * 2, 0)
                    hidden(layer, i * 2 + 2)
                    down(layer, i * 2 + 1, 1)
                down(layer, PAIRS - 1, 0)

            ffn(0)
            pe.wait_ge(s_st, 16)
            pe.wait_ge(s_added, FFN_A[0] + PAIRS * ADD_PER)
            for k in range(KD):
                q_ = pe.transpose(ps[:, 4 + k // 4, (k % 4) * P:(k % 4) * P + DB * STATE], stin[:, k * P:(k + 1) * P], ident[0:120, 0:120])
            q_.then_inc(s_stt, 1)
            norm(2)
            pe.wait_ge(s_pc, KD)
            pe.wait_ge(s_rt, 9)
            for k in range(KD):
                pe.transpose(R2(0, STATE)[:, k * P:(k + 1) * P], pcomp[:, k, 0:STATE], ident[:])
                q_ = pe.transpose(R2(1, DB * STATE)[:, k * P:(k + 1) * P], pcomp[:, k, STATE:], ident[:])
            q_.then_inc(s_pot, 1)
            pe.wait_ge(s_wlo, 38)
            for idx in range(ADD_PER):
                kt, c = divmod(idx, NC)
                g, e = divmod(kt, 2)
                pe.wait_ge(s_pfl, 2 * g + 2)
                group(PAIRS * ADD_PER + FFN_A[0] + idx, idx,
                      [(lambda a, j=j: ws[0][:, a, (2 * g + j) * 256 + e * P:(2 * g + j) * 256 + e * P + P], moving(2 * g + j, c)) for j in range(2)])
            pe.wait_ge(s_prow, 2)
            ffn(1)
            norm(4)
            for i in range(9):
                n = P if i < 8 else NS
                c = 0 if i < 2 else 1 if i < 5 else 2
                pe.wait_ge(s_xf, XF0[4] + 8 * (c + 1))
                if i >= 2:
                    pe.wait_ge(s_oe, i - 1)
                else:
                    pe.wait_ge(s_rt, 15)
                for k in range(KD):
                    q_ = pe.transpose(R2(i % 2, n)[:, k * P:(k + 1) * P], yf[:, k, i * P:i * P + n], ident[:])
                q_.then_inc(s_ot, 1)


_INS = ["x_prompt", "x_sample", "cache_k_b", "cache_v_b", "cache_win_k_a", "cache_win_v_a", "state_pool", "page_table",
        "ln_mix", "ln_ffn", "ln_final", "w_in", "w_out", "lambda_q1", "lambda_k1", "lambda_q2", "lambda_k2", "subln_g",
        "pool_w", "pool_scale", "w_gate", "w_up", "w_down"]
_OUTS = [("o_y_p", (1, S, D)), ("o_y_s", (DB, T, D)),
         ("o_kb_p", (1, 1, S, 4, 128)), ("o_vb_p", (1, 1, S, 4, 128)),
         ("o_kb_s", (1, DB, T, 4, 128)), ("o_vb_s", (1, DB, T, 4, 128)),
         ("o_wk_p", (1, 1, S, 8, 64)), ("o_wv_p", (1, 1, S, 8, 64)),
         ("o_wk_s", (1, DB, PAST, 8, 64)), ("o_wv_s", (1, DB, PAST, 8, 64)),
         ("o_pl_p", (1, 1, STATE, D)), ("o_pl_s", (1, DB, STATE, D))]


def kernel(**inputs):
    import numpy as _np
    import concourse.bacc as _bacc
    from concourse import mybir as _mybir
    from concourse.bass_utils import run_bass_kernel_spmd as _run

    nc = _bacc.Bacc("TRN2", target_bir_lowering=False, num_devices=1)
    arrays, aps = {}, {}
    for name in _INS:
        a = _np.ascontiguousarray(inputs[name])
        arrays[name] = a
        aps[name] = nc.dram_tensor(name, a.shape, _mybir.dt.from_np(a.dtype), kind="ExternalInput").ap()
    arrays["consts"] = shape_constants()
    aps["consts"] = nc.dram_tensor("consts", (P, CONST_W), F32, kind="ExternalInput").ap()
    for name, shape in _OUTS:
        aps[name] = nc.dram_tensor(name, shape, F32, kind="ExternalOutput").ap()
    build_step(nc, aps)
    r = _run(nc, [arrays], core_ids=[0])
    return tuple(r.results[0][name] for name, _ in _OUTS)
```

```python
from contextlib import ExitStack

import numpy as np

import concourse.bass as bass
from concourse import mybir

F32 = mybir.dt.float32
F32R = mybir.dt.float32r
I32 = mybir.dt.int32
ALU = mybir.AluOpType
ACT = mybir.ActivationFunctionType
AX = mybir.AxisListType

P = 128
D = 1024
KD = D // P
S = 1024
DB, T = 8, 8
NS = DB * T
NT = S + NS
NTILE = S // P
FF = 2816
PAIRS = FF // 256
CH = ((0, 364), (364, 364), (728, 360))
NC = len(CH)
CW = 364
PAST = 1024
PAGE = 128
NPAGE = PAST // PAGE
NPHYS = 80
NEG = -1e30
RING, LAG = 8, 3
LAM0 = 0.2
PADW = 16 + S + DB * 24
STATE = 15

OFF = {}
W = 0
for _name, _n in (("ident", 128), ("cs", 9 * 32), ("maskA", 1024), ("maskB", 1024), ("decA", 1024), ("newA", 120),
                  ("newB", 120), ("comb0", 32), ("comb1", 32), ("corr", 64)):
    OFF[_name] = (W, _n)
    W += _n
CONST_W = W


def shape_constants():
    c = np.zeros((P, CONST_W), np.float32)

    def put(name, a):
        o, n = OFF[name]
        c[:a.shape[0], o:o + n] = a.reshape(a.shape[0], n)

    def times(off):
        return (((off >= 0) & (off <= 128)).astype(int) + ((off >= 0) & (off <= 512) & (off % 4 == 0))
                + ((off >= 0) & (off <= 2048) & (off % 16 == 0)))

    def log8(n):
        return np.where(n > 0, 8.0 * np.log(np.maximum(n, 1)), NEG).astype(np.float32)

    put("ident", np.eye(P, dtype=np.float32))
    inv = np.float32(500000.0) ** (-np.arange(8, dtype=np.float32) * np.float32(2.0) / np.float32(16))
    pos = np.zeros((9, P), np.float32)
    pos[:8] = np.arange(S).reshape(8, P)
    pos[8, :NS] = PAST + np.arange(NS) % T
    ang = (pos[..., None] * inv.astype(np.float32)).astype(np.float32).transpose(1, 0, 2)
    co, si = np.cos(ang).astype(np.float32), np.sin(ang).astype(np.float32)
    put("cs", np.concatenate([co, co, si, si], axis=-1))
    p, y = np.arange(P)[:, None], np.arange(1024)[None]
    put("maskA", log8(times(p + 896 - y)))
    put("maskB", np.where(p + 896 - y >= 0, 0, NEG).astype(np.float32))
    r = np.arange(P)[:, None]
    put("decA", log8(times(1024 + r % 8 - (8 * (y % 128) + y // 128))))
    z = np.arange(120)[None] - 56
    ok = (z >= 0) & (z <= r % 8)
    put("newA", np.where(ok, log8(times(r % 8 - z)), NEG).astype(np.float32))
    put("newB", np.where(ok, 0, NEG).astype(np.float32))
    o = np.arange(32)[None]
    for half in range(2):
        put(f"comb{half}", ((r // 32 == o // 8) & (r % 32 == 8 * half + o % 8)).astype(np.float32))
    corr = np.stack([w / np.minimum(np.arange(16) + 1, w) for w in (2, 4, 8, 16)]).astype(np.float32)
    put("corr", np.broadcast_to(corr.reshape(1, 64), (P, 64)))
    return c


def build_step(nc, d):
    st = ExitStack()
    with st:
        base = (nc.sbuf_base + 63) // 64 * 64
        at = [base]

        def persistent(name, shape, dt=F32):
            t = nc.alloc_sbuf_tensor_at(name, shape, dt, offset=at[0])
            at[0] += (int(np.prod(shape[1:])) * 4 + 31) // 32 * 32
            return t

        x = persistent("x", [P, KD, NT])
        ident = persistent("ident", [P, P])
        ones = persistent("ones", [P, P])
        gains = persistent("gains", [P, 49])
        small = persistent("small", [P, 24])
        xn_at = at[0]
        xn = persistent("xn", [P, KD, 2, NT], F32R)
        rest = at[0]

        def placed(name, off, shape, dt=F32):
            return nc.alloc_sbuf_tensor_at(name, shape, dt, offset=off)

        ws = [placed("ws0", rest, [P, 2, 2048], F32R), placed("ws1", rest + 32768, [P, 2, 2048], F32R),
              placed("ws2", rest + 49152, [P, 2, 2048], F32R)]
        wraw = placed("wraw", rest + 16384, [P, 2, 2048])
        hh = placed("hh", rest + 65536, [P, 2, 2, 2, NT], F32R)
        act_s = placed("act_s", rest + 100352, [P, 2, CW])
        act_h = placed("act_h", rest + 100352 + 2912, [P, 2, CW])
        nrm = rest + 106176 - 18880
        sq = placed("sq", nrm, [P, 2, NT])
        rstd = placed("rstd", nrm + 8704, [P, NT])
        xf = placed("xf", nrm + 13056, [P, 4, CW])
        xin = placed("xin", rest, [P, 3, D])
        grow = placed("grow", rest + 12288, [49, P])
        lamrow = placed("lamrow", rest + 12800, [1, 4, 64])
        lamtmp = placed("lamtmp", rest + 14080, [1, 2, 64])
        wp = placed("wp", rest, [P, 2, 2, KD, 512], F32R)
        wpraw = placed("wpraw", rest + 65536, [P, 2, 4, 512])
        tok = placed("tok", rest + 81920, [P, 3, 512])
        toks = placed("toks", rest + 88064, [NS, 6, 512])
        cs = placed("cs", rest + 100352, [P, 9, 32])
        rope = placed("rope", rest + 101504, [P, 2, 2, 128])
        osam = placed("osam", rest + 103552, [P, 2, 4, NS])
        kraw, vraw = ([placed(f"{name}{m}", rest + 32768 * m + off, [P, 8, 512]) for m in range(2)]
                      for name, off in (("kraw", 0), ("vraw", 16384)))
        q = xn_at
        dkT = placed("dkT", q, [P, 4, PAST])
        dse = placed("dse", q + 16384, [P, 2, PAST + NS])
        dpT = placed("dpT", q + 25088, [P, 2, 9, P])
        dom = placed("dom", q + 34304, [P, P])
        qblk = placed("qblk", q + 34816, [P, 2, DB, 4, 32])
        qcur = placed("qcur", q + 43008, [P, 2, 4, 32])
        knT = placed("knT", q + 44032, [P, 2, 4, NS])
        dmask = placed("dmask", q + 46080, [P, 2, PAST + NS])
        dnew = placed("dnew", q + 54784, [P, 2, 120])
        comb = placed("comb", q + 55744, [P, 3, 32])
        dmix = placed("dmix", q + 56128, [P, 2, 64])
        dstat = placed("dstat", q + 56640, [P, 2, 4])
        ptab = placed("ptab", rest + 105600, [1, DB * NPAGE], I32)
        qkv = placed("qkv", rest, [P, 2, 3, 8, 128])
        qT = placed("qT", rest + 24576, [P, S])
        kT = placed("kT", rest + 28672, [P, S])
        sm = placed("sm", rest + 32768, [P, RING, S])
        pT = placed("pT", rest + 65536, [P, 2, 8, 512])
        ob = placed("ob", rest + 81920, [P, 4, S])
        pmask = placed("pmask", rest + 98304, [P, S])
        pstat = placed("pstat", rest + 102400, [P, RING, 4])
        osq = placed("osq", rest + 73728, [P, 2, 512])
        orms = placed("orms", rest + 65536, [P, 4, 512])
        yp = placed("yp", rest + 32768, [P, KD, PADW])
        pa = placed("pa", rest + 32768 + KD * PADW * 4, [P, 2, PADW])
        pf = (placed("pf0", rest + 32768 + (KD + 2) * PADW * 4, [P, NT]), placed("pf1", nrm + 13056, [P, NT]))
        stin = placed("stin", rest + 32768 + KD * PADW * 4, [DB * STATE, D])
        corr = placed("corr", nrm - 256, [P, 4, 16])
        yf = placed("yf", xn_at, [P, KD, NT])
        yrow = placed("yrow", rest, [P, 3, D])
        prow = placed("prow", rest + 32768 + KD * PADW * 4, [P, 2, D])

        ps = st.enter_context(nc.psum_tensor("ps", [P, 8, 512], F32))
        pcomp = placed("pcomp", nrm, [P, KD, STATE * (DB + 1)])
        qs_dram = nc.dram_tensor("q_rows", [2, S, 512], F32, kind="Internal").ap()

        def sem(name):
            return st.enter_context(nc.semaphore(name))

        consts = d["consts"]

        def const(name, rows=P):
            o, n = OFF[name]
            return consts[0:rows, o:o + n]

        s_const = sem("s_const")
        s_xin = [sem(f"s_xin{i}") for i in range(3)]
        s_ones = sem("s_ones")
        s_xt = sem("s_xt")
        s_x = sem("s_x")
        s_gt, s_gains = sem("s_gt"), sem("s_gains")
        s_lam, s_lamv, s_lamb = sem("s_lam"), sem("s_lamv"), sem("s_lamb")
        s_sq, s_fold, s_ss, s_rt, s_rstd = (sem(n) for n in ("s_sq", "s_fold", "s_ss", "s_rt", "s_rstd"))
        s_xf, s_xhi, s_xlo = sem("s_xf"), sem("s_xhi"), sem("s_xlo")
        s_praw = [sem(f"s_praw{i}") for i in range(2)]
        s_phi, s_plo = sem("s_phi"), sem("s_plo")
        s_cs = sem("s_cs")
        s_proj = sem("s_proj")
        s_tok = sem("s_tok")
        s_ropeP = sem("s_ropeP")
        s_rope = sem("s_rope")
        s_store = [sem(f"s_store{i}") for i in range(3)]
        s_sstore = sem("s_sstore")
        s_raw = [sem(f"s_raw{i}") for i in range(2)]
        s_whi, s_wlo = sem("s_whi"), sem("s_wlo")
        s_gu = sem("s_gu")
        s_silu, s_h, s_hhi, s_hlo = sem("s_silu"), sem("s_h"), sem("s_hhi"), sem("s_hlo")
        s_acc = sem("s_acc")
        s_added = sem("s_added")
        s_dc = sem("s_dc")
        s_dk = [sem(f"s_dk{i}") for i in range(2)]
        s_dv = [sem(f"s_dv{i}") for i in range(2)]
        s_win = sem("s_win")
        s_pt = sem("s_pt")
        s_qz, s_qk, s_qke, s_qb = sem("s_qz"), sem("s_qk"), sem("s_qke"), sem("s_qb")
        s_dtr, s_dev, s_dea = sem("s_dtr"), sem("s_dev"), sem("s_dea")
        s_qc, s_ds, s_dsm, s_dnm, s_de, s_drd, s_dmx = (sem(n) for n in ("s_qc", "s_ds", "s_dsm", "s_dnm", "s_de", "s_drd", "s_dmx"))
        s_dpt, s_dpe, s_dpv, s_dom, s_dot, s_dos = (sem(n) for n in ("s_dpt", "s_dpe", "s_dpv", "s_dom", "s_dot", "s_dos"))
        s_qd, s_dmk, s_cmbd = sem("s_qd"), sem("s_dmk"), sem("s_cmbd")
        s_pm = sem("s_pm")
        s_qkv = [sem(f"s_qkv{i}") for i in range(2)]
        s_qt, s_qte, s_kte = sem("s_qt"), sem("s_qte"), sem("s_kte")
        s_s, s_sm, s_nm, s_e, s_rd, s_p = (sem(n) for n in ("s_s", "s_sm", "s_nm", "s_e", "s_rd", "s_p"))
        s_tu, s_rdx, s_cmb, s_small = sem("s_tu"), sem("s_rdx"), sem("s_cmb"), sem("s_small")
        s_tp, s_tpe, s_pv, s_ohi, s_olo = (sem(n) for n in ("s_tp", "s_tpe", "s_pv", "s_ohi", "s_olo"))
        s_osq, s_oss, s_ort, s_orr, s_osc, s_oh, s_ol = (sem(n) for n in ("s_osq", "s_oss", "s_ort", "s_orr", "s_osc", "s_oh", "s_ol"))
        s_st, s_stt, s_yp, s_pz, s_lvl = sem("s_st"), sem("s_stt"), sem("s_yp"), sem("s_pz"), sem("s_lvl")
        s_corr, s_pf, s_pfh, s_pfl = sem("s_corr"), sem("s_pf"), sem("s_pfh"), sem("s_pfl")
        s_ot, s_oe = sem("s_ot"), sem("s_oe")
        s_out = [sem(f"s_out{i}") for i in range(3)]
        s_pout = sem("s_pout")
        s_pot, s_pc, s_prow = sem("s_pot"), sem("s_pc"), sem("s_prow")

        block = st.enter_context(nc.Block())

        FFN_U = (4, 38)
        FFN_A = (24, 312)
        GU_PER = 2 * NC
        FFN_G = (0, PAIRS * GU_PER)
        ADD_PER = KD * NC

        def unit_src(kind, layer, b):
            if kind == "out":
                return d["w_out"][0].rearrange("(k p) n -> p k n", p=P)[:, :, b * 256:(b + 1) * 256]
            if kind == "gate":
                return d["w_gate"][layer].rearrange("(k p) n -> p k n", p=P)[:, :, bass.ts(b, 256)]
            if kind == "up":
                return d["w_up"][layer].rearrange("(k p) n -> p k n", p=P)[:, :, bass.ts(b, 256)]
            if kind == "down":
                return d["w_down"][layer].rearrange("(b j p) n -> b p j n", p=P, j=2)[b]
            return d["pool_w"][0].rearrange("g (k p) n -> p (g k) n", p=P)

        def unit_of(layer, kind, b):
            u = FFN_U[layer]
            if isinstance(b, int) and b == 0 and kind != "down":
                return u + (kind == "up")
            if isinstance(b, int) and b == PAIRS - 1 and kind == "down":
                return u + 3 * PAIRS - 1
            return b * 3 + (u + {"gate": -1, "up": 0, "down": 4}[kind])

        def raw_slot(layer, kind, b, par):
            return (par + (kind == "gate")) % 2 if not isinstance(b, int) else unit_of(layer, kind, b) % 2

        HILO = (0, 1, 3)
        GAIN = (0, 16, 8, 24, 32)
        AFTER = (None, 0, 264, 288, 552)
        XF0 = (0, 24, 48, 80, 104)
        SQUARES, FOLDS = KD - 1 + NC, KD - 2 + NC

        ROPE0 = {0: 0, 1: 9, 3: 18, 4: 27}

        def T2(par, n):
            return ps[:, 2 * par:2 * par + 2].rearrange("p a (k n) -> p (a k) n", n=P)[:, :, 0:n]

        def R2(par, n):
            return ps[0:n, 2 * par:2 * par + 2].rearrange("p a n -> p (a n)")

        def b_chunk(w):
            c, hd = divmod(w, 4)
            if c == 2:
                return osam[:, 1, hd], NS, S
            return ob[:, hd, c * 512:(c + 1) * 512], 512, c * 512

        def raw_count(n, slot):
            return 16 * (n // 2 + 1) if isinstance(n, int) else n * 8 + (8 if slot else 16)

        def number(pair):
            mix, it, half = pair
            return it * 2 + (mix * 4 + half)

        def groups_before(pair):
            mix, it, half = pair
            return (it * 2 + half) * (12 if mix else 24) + (96 if mix else 0)

        def groups_through(mix, w):
            return sum((x // 2 + 4) // 4 for x in range(w + 1) if x % 2 or not mix)

        def prompt_loop(eng, start, body):
            start((0, 0, 0))
            with eng.Fori(0, 2) as it:
                body((0, it, 0), (0, it, 1), 16)
                body((0, it, 1), (0, it + 1, 0), it * 16 + 16)
            for it in range(2):
                body((1, it, 0), (1, it, 1), 32)
                body((1, it, 1), (1, 1, 0) if it == 0 else None, 32)

        def prompt_dve(dve):
            tt, ts, stt = dve.tensor_tensor, dve.tensor_scalar, dve.scalar_tensor_tensor

            def masked(pair, v, turned):
                u = number(pair) * 16 + v
                n = P * (v // 2 + 1)
                dve.wait_ge(s_s, u + 1)
                if turned is not None:
                    dve.wait_ge(s_tp, turned)
                dve.memset(small[:, 11:12], 0.0)
                st_ = pstat[:, v % RING]
                dve.tensor_tensor_reduce(sm[:, v % RING, 0:n], ps[:, 2 * (v % 2):2 * (v % 2) + 2].rearrange("p a n -> p (a n)")[:, 0:n],
                                         pmask[:, S - n:S], 1.0, -3.0e38, ALU.add, ALU.max, st_[:, 0:1]).then_inc(s_sm, 1)
                dve.wait_ge(s_sm, u + 1)
                ts(st_[:, 1:2], st_[:, 0:1], -0.125, None, ALU.mult).then_inc(s_nm, 1)

            def weight(pair, w):
                mix, it, half = pair
                u = number(pair) * 16 + w
                st_ = pstat[:, w % RING]
                dve.wait_ge(s_e, u + 1)
                if mix and w % 2:
                    dve.reciprocal(st_[:, 0:1], st_[:, 2:3]).then_inc(s_rdx, 1)
                    dve.wait_ge(s_rdx, (it * 2 + half) * 8 + (w // 2 + 1))
                    ts(st_[:, 3:4], st_[:, 0:1], small[:, 6:7], None, ALU.mult).then_inc(s_rd, 1)
                    dve.wait_ge(s_rd, u + 1)
                    dve.wait_ge(s_p, (it * 2 + half) * 8 + (64 + w // 2 + 1))
                    n = P * (w // 2 + 1)
                    first = sm[:, (w - 1) % RING, 0:n]
                    stt(first, sm[:, w % RING, 0:n], st_[:, 3:4], first, ALU.mult, ALU.add).then_inc(s_cmb, 1)
                else:
                    dve.reciprocal(st_[:, 3:4], st_[:, 2:3]).then_inc(s_rd, 1)

            def gather(pair, w):
                mix, it, half = pair
                if mix and w % 2 == 0:
                    return
                jj, t0 = number(pair), groups_before(pair)
                i, s = w // 2, 0 if mix else w % 2
                if w == mix:
                    dve.wait_ge(s_pv, jj * 2)
                if w == 8 + mix:
                    dve.wait_ge(s_pv, jj * 2 + 1)
                t = groups_through(mix, w - 1)
                for k0 in range(0, i + 1, 4):
                    cnt = min(4, i + 1 - k0)
                    dve.wait_ge(s_tp, t0 + (t + 1))
                    dve.tensor_copy(pT[:, s, k0:k0 + cnt, (i % 4) * P:(i % 4) * P + P],
                                    ps[:, 4 + t % 2, 0:cnt * P].rearrange("p (k n) -> p k n", n=P)).then_inc(s_tpe, 1)
                    t += 1

            def low(pair, g):
                mix, it, half = pair
                if mix == 0:
                    dve.wait_ge(s_ohi, number(pair) * 2 + (g + 1))
                    o = xn[:, bass.ds(it * 2 + half, 1), :, g * 512:(g + 1) * 512].rearrange("p a q n -> p (a q) n")
                    tt(o[:, 1], ps[:, 6 + g], o[:, 0].bitcast(F32), ALU.subtract).then_inc(s_olo, 1)

            def k_out(pair):
                for r in range(2):
                    dve.wait_ge(s_qt, number(pair) * 4 + (r + 3))
                    dve.tensor_copy(kT[:, r * 512:(r + 1) * 512], ps[:, 6 + r]).then_inc(s_kte, 1)

            def start(pair):
                k_out(pair)
                dve.wait_ge(s_pm, 16)
                for v in range(LAG):
                    masked(pair, v, None)
                    if v == 1:
                        weight(pair, 0)

            def body(pair, nxt, masks):
                mix, t0 = pair[0], groups_before(pair)
                weight(pair, 1)
                for v in range(LAG, 16):
                    masked(pair, v, t0 if v < RING else t0 + groups_through(mix, v - RING + int(mix and v % 2 == 0)))
                    weight(pair, v - 1)
                    gather(pair, v - LAG)
                    if v == 14:
                        low(pair, 0)
                if nxt:
                    k_out(nxt)
                weight(pair, 15)
                if nxt:
                    dve.wait_ge(s_pm, masks)
                for v in range(LAG):
                    gather(pair, 16 - LAG + v)
                    if nxt:
                        masked(nxt, v, t0 + groups_through(mix, v + 16 - RING + int(mix and v % 2 == 0)))
                    if nxt and v == 1:
                        weight(nxt, 0)
                low(pair, 1)

            prompt_loop(dve, start, body)

        def prompt_act(act):
            def q_out(pair):
                for r in range(2):
                    act.wait_ge(s_qt, number(pair) * 4 + (r + 1))
                    act.activation(qT[:, r * 512:(r + 1) * 512], ps[:, 6 + r], ACT.Copy).then_inc(s_qte, 1)

            def exponentials(pair, v):
                n = P * (v // 2 + 1)
                act.wait_ge(s_nm, number(pair) * 16 + (v + 1))
                act.activation(sm[:, v % RING, 0:n], sm[:, v % RING, 0:n], ACT.Exp, bias=pstat[:, v % RING, 1:2],
                               scale=0.125, accum_out=pstat[:, v % RING, 2:3]).then_inc(s_e, 1)

            def out(pair, g):
                mix, it, half = pair
                act.wait_ge(s_pv, number(pair) * 2 + (g + 1))
                dst = (ob[:, bass.ds(it * 2 + half, 1), g * 512:(g + 1) * 512] if mix else
                       xn[:, bass.ds(it * 2 + half, 1), 0, g * 512:(g + 1) * 512])
                act.activation(dst.rearrange("p a n -> p (a n)"), ps[:, 6 + g], ACT.Copy).then_inc(s_ohi, 1)

            def start(pair):
                q_out(pair)
                for v in range(LAG):
                    exponentials(pair, v)

            def body(pair, nxt, masks):
                for v in range(LAG, 16):
                    exponentials(pair, v)
                    if v == 12:
                        out(pair, 0)
                    if v == 14 and nxt:
                        q_out(nxt)
                if nxt:
                    for v in range(LAG):
                        exponentials(nxt, v)
                out(pair, 1)

            prompt_loop(act, start, body)

        def prompt_pe(pe):
            mm = pe.matmul

            def turn_qk(pair, rs, before=None):
                mix, it, half = pair
                jj = number(pair)
                for r in rs:
                    if r == 0:
                        pe.wait_ge(s_qkv[half], it * 48 + (48 + 96 * mix))
                        if before is not None:
                            pe.wait_ge(s_ohi, jj * 2 - 1)
                            pe.wait_ge(s_olo, 8 if before else jj * 2 - 1)
                    if r >= 2:
                        pe.wait_ge(s_qte, jj * 2 + (r - 1))
                    for i in range(4):
                        q_ = pe.transpose(ps[:, 6 + r % 2, i * P:(i + 1) * P], qkv[:, half, r // 2, 4 * (r % 2) + i], ident[:])
                    q_.then_inc(s_qt, 1)

            def scores(pair, v, first=False):
                jj = number(pair)
                i, s = v // 2, v % 2
                n = P * (i + 1)
                if v == 0:
                    pe.wait_ge(s_qte, jj * 2 + 2)
                    pe.wait_ge(s_kte, jj * 2 + 2)
                if not first:
                    pe.wait_ge(s_sm, jj * 16 + (v - 1))
                h64 = slice(64 * s, 64 * s + 64)
                for a in range(0, n, 512):
                    w = min(512, n - a)
                    q_ = mm(ps[:, 2 * s + a // 512, 0:w], qT[h64, i * P:(i + 1) * P], kT[h64, a:a + w], start=True, stop=True)
                q_.then_inc(s_s, 1)

            def turn_p(pair, w):
                mix, it, half = pair
                if mix and w % 2 == 0:
                    return
                i, t0, t = w // 2, groups_before(pair), groups_through(mix, w - 1)
                if mix:
                    pe.wait_ge(s_cmb, (it * 2 + half) * 8 + (i + 1))
                else:
                    pe.wait_ge(s_p, number(pair) * 16 + (w + 1))
                src = sm[:, (w - mix) % RING]
                for k0 in range(0, i + 1, 4):
                    cnt = min(4, i + 1 - k0)
                    if t >= 2:
                        pe.wait_ge(s_tpe, t0 + (t - 1))
                    else:
                        pe.wait_ge(s_tpe, t0)
                    for k in range(k0, k0 + cnt):
                        q_ = pe.transpose(ps[:, 4 + t % 2, (k - k0) * P:(k - k0 + 1) * P], src[:, k * P:(k + 1) * P], ident[:])
                    q_.then_inc(s_tp, 1)
                    t += 1

            def values(pair, g, more=False):
                mix, it, half = pair
                jj = number(pair)
                pe.wait_ge(s_ohi, jj * 2)
                pe.wait_ge(s_olo, 8 if mix else jj * 2)
                pe.wait_ge(s_kte, jj * 2 + (4 if more else 2))
                pe.wait_ge(s_tpe, groups_before(pair) + groups_through(mix, 7 + 8 * g))
                nk = 4 * (g + 1)
                for kt in range(nk):
                    q0 = max(0, kt - 4 * g) * P
                    for s in range(1 if mix else 2):
                        rows = slice(0, P) if mix else slice(64 * s, 64 * s + 64)
                        q_ = mm(ps[rows, 6 + g, q0:512], qkv[:, half, 2, kt, rows], pT[:, s, kt, q0:512],
                                start=(kt == 0), stop=(kt == nk - 1))
                q_.then_inc(s_pv, 1)

            def start(pair):
                turn_qk(pair, range(4))
                for v in range(LAG):
                    scores(pair, v, v < 2)

            def body(pair, nxt, masks):
                mix = pair[0]
                for v in range(LAG, 16):
                    scores(pair, v)
                    if v == 8 + LAG:
                        values(pair, 0)
                    if v == 15 and nxt:
                        turn_qk(nxt, (0, 1), mix)
                    turn_p(pair, v - LAG)
                if nxt:
                    turn_qk(nxt, (2, 3))
                for v in range(LAG):
                    turn_p(pair, 16 - LAG + v)
                    if nxt:
                        scores(nxt, v)
                values(pair, 1, nxt is not None)

            prompt_loop(pe, start, body)

        def TK(j):
            return ps[:, 4 + j % 2].rearrange("p (k n) -> p k n", n=P)

        def sample_cols(row):
            if len(row.shape) == 3:
                return row[:, :, 16 + S:PADW].rearrange("p k (b t) -> p k b t", t=24)
            return row[:, 16 + S:PADW].rearrange("p (b t) -> p b t", t=24)

        def by_sample(row):
            return row.rearrange("p (b t) -> p b t", t=T)

        KINDS = ("gate", "up", "down")
        TWOS = (PAIRS - 1) // 2

        @block.sync
        def _(sp):
            sp.dma_start(ident[:], const("ident")).then_inc(s_const, 16)
            for i in range(9):
                n = P if i < 8 else NS
                if i >= 3:
                    sp.wait_ge(s_xt, i - 2)
                src = d["x_prompt"][0, i * P:(i + 1) * P] if i < 8 else d["x_sample"].rearrange("b t n -> (b t) n")
                sp.dma_start(xin[0:n, i % 3], src).then_inc(s_xin[i % 3], 16)
                if i == 1:
                    for name, r0, rows in (("ln_mix", 0, 16), ("ln_ffn", 16, 16), ("ln_final", 32, 8), ("pool_scale", 40, 8),
                                           ("subln_g", 48, 1)):
                        src = d[name] if name == "ln_final" else d[name].rearrange("l n -> (l n)")
                        sp.dma_start(grow[r0:r0 + rows], src.rearrange("(k p) -> k p", p=P)).then_inc(s_const, 16)
                    for j, name in enumerate(("lambda_q1", "lambda_k1", "lambda_q2", "lambda_k2")):
                        sp.dma_start(lamrow[:, j], d[name]).then_inc(s_const, 16)

            w_in = d["w_in"][0].rearrange("(k p) n -> p k n", p=P)
            for m in range(12):
                g, half = divmod(m, 2)
                if m >= 2:
                    sp.wait_ge(s_plo, m - 1)
                sp.dma_start(wpraw[:, m % 2], w_in[:, 4 * half:4 * half + 4, g * 512:(g + 1) * 512]).then_inc(s_praw[m % 2], 16)
                if m == 1:
                    sp.wait_ge(s_xlo, 24)
                    sp.wait_ge(s_xhi, 24)
                    sp.dma_start(cs[:], const("cs").rearrange("p (i c) -> p i c", i=9)).then_inc(s_cs, 16)

            def load_window(b, raw, name, s):
                sp.dma_start(raw[0][:], d[name][0, b].rearrange("(p j) h n -> p j (h n)", j=8)).then_inc(s[0], 16)

            def load_pages(pages, raw, name, s):
                for j, page in enumerate(pages):
                    sp.dma_start(raw[1][:, j], d[name][0, bass.ds(page, 1)].rearrange("a p h n -> p (a h n)")).then_inc(s[1], 16)

            def page_numbers(b):
                return [sp.value_load(ptab[0:1, bass.ds(b * NPAGE + j, 1)], min_val=0, max_val=NPHYS - 1) for j in range(NPAGE)]

            sp.dma_start(ptab[:], d["page_table"].rearrange("b n -> (b n)").rearrange("(a n) -> a n", a=1)).then_inc(s_pt, 16)
            sp.wait_ge(s_proj, 45)
            load_window(0, kraw, "cache_win_k_a", s_dk)
            load_window(0, vraw, "cache_win_v_a", s_dv)
            sp.wait_ge(s_pt, 16)
            pages = page_numbers(0)
            sp.wait_ge(s_tok, 54)
            sp.wait_ge(s_rope, 36)
            for name, dst in (("decA", dmask[:, 0, 0:PAST]), ("newA", dnew[:, 0]), ("newB", dnew[:, 1]), ("comb0", comb[:, 0]),
                              ("comb1", comb[:, 1])):
                sp.dma_start(dst, const(name)).then_inc(s_dc, 16)
            load_pages(pages, kraw, "cache_k_b", s_dk)
            load_pages(pages, vraw, "cache_v_b", s_dv)
            turned, used = (sp.alloc_register(n) for n in ("turned", "used"))
            for r in (turned, used):
                sp.reg_mov(r, 0)
            with sp.Fori(0, DB - 1) as b:
                pages = page_numbers(b + 1)
                for paged, names in enumerate((("cache_win_k_a", "cache_win_v_a"), ("cache_k_b", "cache_v_b"))):
                    sp.reg_add(turned, turned, 8)
                    sp.reg_add(used, used, 1)
                    n_turned, n_used = (sp.snap(r) for r in (turned, used))
                    for raw, name, s, done, n in ((kraw, names[0], s_dk, s_dtr, n_turned), (vraw, names[1], s_dv, s_dpv, n_used)):
                        sp.wait_ge(done, n)
                        if paged:
                            load_pages(pages, raw, name, s)
                        else:
                            load_window(b + 1, raw, name, s)

            sp.wait_ge(s_sstore, 16 * (2 + 2 * DB))
            sp.wait_ge(s_dpv, 2 * DB - 1)
            sp.wait_ge(s_dtr, 8 * (2 * DB - 1))
            for i, n in enumerate((16, 16, 16)):
                sp.wait_ge(s_store[i], 16 * n)
            for mix in range(2):
                kn, vn = ("o_kb_p", "o_vb_p") if mix else ("o_wk_p", "o_wv_p")
                srcs = (qs_dram[mix].rearrange("(i p) n -> p i n", p=P),
                        d[kn][0, 0].rearrange("(i p) h n -> p i (h n)", p=P),
                        d[vn][0, 0].rearrange("(i p) h n -> p i (h n)", p=P))
                for j in range(4):
                    if 4 * mix + j >= 2:
                        sp.wait_ge(s_pv, 2 * (4 * mix + j - 1))
                    for a in range(3):
                        sp.dma_start(qkv[:, j % 2, a], srcs[a][:, :, j * P:(j + 1) * P]).then_inc(s_qkv[j % 2], 16)
                    if j == 0:
                        if mix:
                            sp.wait_ge(s_sm, 64)
                        else:
                            sp.wait_ge(s_dos, 2 * DB)
                        sp.dma_start(pmask[:], const("maskB" if mix else "maskA")).then_inc(s_pm, 16)

            sp.wait_ge(s_pv, 16)

            def load(kind, layer, b, n, slot):
                if not (isinstance(n, int) and n < 2):
                    sp.wait_ge(s_wlo, n - 1)
                k = {"down": 2, "pool": 8}.get(kind, 8)
                sp.dma_start(wraw[:, slot].rearrange("p (k n) -> p k n", k=k), unit_src(kind, layer, b)).then_inc(s_raw[slot], 16)

            for u in range(4):
                load("out", 0, u, u, u % 2)
            for layer in range(2):
                def block_loads(layer, b, kinds, par=0):
                    for kind in kinds:
                        load(kind, layer, b, unit_of(layer, kind, b), raw_slot(layer, kind, b, par))

                block_loads(layer, 0, ("gate", "up"))
                with sp.Fori(0, (PAIRS - 1) // 2) as i:
                    block_loads(layer, i * 2 + 1, ("gate", "up"), 1)
                    block_loads(layer, i * 2, ("down",), 0)
                    block_loads(layer, i * 2 + 2, ("gate", "up"), 0)
                    block_loads(layer, i * 2 + 1, ("down",), 1)
                block_loads(layer, PAIRS - 1, ("down",))
                if layer == 0:
                    load("pool", 0, 0, 37, 1)
                    sp.wait_ge(s_acc, FFN_A[0] + PAIRS * ADD_PER)
                    sp.dma_start(corr[:], const("corr").rearrange("p (g n) -> p g n", g=4)).then_inc(s_corr, 16)
                    sp.dma_start(stin[:], d["state_pool"][0].rearrange("b t n -> (b t) n")).then_inc(s_st, 16)

        @block.gpsimd
        def _(pool):
            for g in range(6):
                rot = ROPE0.get(g)
                for i in range(8):
                    t = g * 8 + i
                    if rot is None:
                        pool.wait_ge(s_tok, g * 9 + i + 1)
                    else:
                        pool.wait_ge(s_rope, rot + i + 1)
                    dst = (qs_dram[g // 3, i * P:(i + 1) * P] if g % 3 == 0 else
                           d[{1: "o_wk_p", 2: "o_wv_p", 4: "o_kb_p", 5: "o_vb_p"}[g]][0, 0, i * P:(i + 1) * P]
                           .rearrange("t h n -> t (h n)"))
                    pool.dma_start(dst, tok[:, t % 3]).then_inc(s_store[t % 3], 16)
                if rot is None:
                    pool.wait_ge(s_tok, g * 9 + 9)
                else:
                    pool.wait_ge(s_rope, rot + 9)
                if g in (4, 5):
                    dst = d["o_kb_s" if g == 4 else "o_vb_s"][0].rearrange("b t h n -> (b t) (h n)")
                    pool.dma_start(dst, toks[:, g]).then_inc(s_sstore, 16)
                if g in (1, 2):
                    dst = d["o_wk_s" if g == 1 else "o_wv_s"][0].rearrange("b t h n -> b t (h n)")
                    for b in range(DB):
                        pool.dma_start(dst[b, PAST - T:PAST], toks[b * T:(b + 1) * T, g]).then_inc(s_sstore, 16)

            pool.wait_ge(s_sstore, 16 * (2 + 2 * DB))

            def move_window(b):
                for src, dst in (("cache_win_k_a", "o_wk_s"), ("cache_win_v_a", "o_wv_s")):
                    a, o = (d[n][0, bass.ds(b, 1)].rearrange("a t h n -> (a t) (h n)") for n in (src, dst))
                    pool.dma_start(o[0:PAST - T], a[T:PAST]).then_inc(s_win, 16)

            for mix in range(2):
                with pool.Fori(0, 2) as it:
                    for half in range(2):
                        for v in range(16):
                            if v == 6:
                                pool.wait_ge(s_pm, 16)
                                move_window(it * 2 + (mix * 4 + half))
                            if mix and v % 2:
                                continue
                            u = it * 32 + (mix * 64 + half * 16 + v)
                            n = P * (v // 2 + 1)
                            pool.wait_ge(s_rd, u + 1)
                            buf = sm[:, v % RING, 0:n]
                            pool.tensor_tensor(buf, buf, pstat[:, v % RING, 3:4].to_broadcast([P, n]), ALU.mult).then_inc(s_p, 1)

            pool.wait_ge(s_win, 32 * DB)

            pool.wait_ge(s_acc, FFN_A[0] + PAIRS * ADD_PER)
            pool.memset(yp[:, :, 0:16], 0.0).then_inc(s_pz, 1)
            pool.memset(sample_cols(yp[:])[:, :, :, 0:1], 0.0).then_inc(s_pz, 1)
            pool.wait_ge(s_prow, 2)
            pool.dma_start(d["o_pl_p"][0, 0], prow[0:STATE, 0]).then_inc(s_pout, 16)
            pool.dma_start(d["o_pl_s"][0].rearrange("b t n -> (b t) n"), prow[0:DB * STATE, 1]).then_inc(s_pout, 16)
            pool.wait_ge(s_pout, 32)

            for i in range(9):
                n = P if i < 8 else NS
                pool.wait_ge(s_oe, i + 1)
                dst = d["o_y_p"][0, i * P:(i + 1) * P] if i < 8 else d["o_y_s"].rearrange("b t n -> (b t) n")
                pool.dma_start(dst, yrow[0:n, i % 3]).then_inc(s_out[i % 3], 16)
            for i in range(3):
                pool.wait_ge(s_out[i], 48)

        @block.scalar
        def _(act):
            for i in range(9):
                n = P if i < 8 else NS
                act.wait_ge(s_xt, i + 1)
                act.activation(x[:, :, i * P:i * P + n], T2(i % 2, n), ACT.Copy).then_inc(s_x, 1)
            act.wait_ge(s_lam, 2)
            act.activation(small[0:1, 2:4], small[0:1, 0:2], ACT.Exp).then_inc(s_lamv, 1)

            def square(r, k):
                for c, (c0, cn) in enumerate(CH if k == KD - 1 else ((0, NT),)):
                    if r == 0:
                        act.wait_ge(s_x, 9)
                    else:
                        act.wait_ge(s_added, AFTER[r] + NC * k + (c + 1 if k == KD - 1 else NC))
                    if k >= 3:
                        act.wait_ge(s_fold, FOLDS * r + k - 2)
                    dst = sq[:, k % 2, c0:c0 + cn] if k else rstd[:]
                    act.activation(dst, x[:, k, c0:c0 + cn], ACT.Square).then_inc(s_sq, 1)

            def norm(r, between=None, done=0):
                if r:
                    act.wait_ge(s_xf, XF0[r])
                for k in range(done, KD):
                    square(r, k)
                for c, (c0, cn) in enumerate(CH):
                    act.wait_ge(s_ss, NC * r + c + 1)
                    act.activation(rstd[:, c0:c0 + cn], ps[:, c, 0:cn], ACT.Sqrt, bias=small[:, 8:9], scale=1.0 / D).then_inc(s_rt, 1)
                if between:
                    between()
                if r in HILO:
                    for c, (c0, cn) in enumerate(CH):
                        for k in range(KD):
                            f = c * KD + k
                            act.wait_ge(s_xf, XF0[r] + f + 1)
                            act.activation(xn[:, k, 0, c0:c0 + cn], xf[:, f % 4, 0:cn], ACT.Copy).then_inc(s_xhi, 1)

            def proj_hi(m):
                g, half = divmod(m, 2)
                act.wait_ge(s_praw[m % 2], 16 * (m // 2 + 1))
                if g >= 2:
                    act.wait_ge(s_proj, 9 * (g - 1))
                act.activation(wp[:, g % 2, 0, 4 * half:4 * half + 4], wpraw[:, m % 2], ACT.Copy).then_inc(s_phi, 1)

            norm(0, lambda: (proj_hi(0), proj_hi(1)))
            for m in range(2, 4):
                proj_hi(m)
            for g in range(6):
                for i in range(9):
                    n = P if i < 8 else NS
                    m = g * 9 + i
                    act.wait_ge(s_proj, m + 1)
                    if i < 8:
                        t = g * 8 + i
                        if t >= 3:
                            act.wait_ge(s_store[t % 3], 16 * (t // 3))
                        act.activation(tok[:, t % 3], ps[:, m % 8], ACT.Copy).then_inc(s_tok, 1)
                    else:
                        act.activation(toks[:, g], ps[0:NS, m % 8], ACT.Copy).then_inc(s_tok, 1)
                if g + 2 < 6:
                    proj_hi(2 * g + 4)
                    proj_hi(2 * g + 5)

            def dec_evac(tr):
                for j in range(0, 8, 2):
                    act.wait_ge(s_dtr, tr + j + 1)
                    act.activation(dkT[:, :, j * P:(j + 1) * P], TK(j), ACT.Copy).then_inc(s_dea, 1)

            def out_rows(dd):
                act.wait_ge(s_dpv, dd + 1)
                act.activation(dom[:], ps[:, 3, 0:P], ACT.Copy).then_inc(s_dom, 1)

            def to_osam(b, m):
                act.wait_ge(s_dot, b * 2 + (m + 1))
                act.activation(osam[:, m, :, bass.ds(b * T, T)], ps[:, 3, 256:288].rearrange("p (j t) -> p j t", t=T),
                               ACT.Copy).then_inc(s_dos, 1)

            def dec_act(b, m, last=False):
                dd = b * 2 + m
                first = isinstance(dd, int) and dd == 0
                act.wait_ge(s_dnm, dd + 1)
                act.activation(dse[:, m], dse[:, m], ACT.Exp, bias=dstat[:, m, 1:2], scale=0.125,
                               accum_out=dstat[:, m, 2:3]).then_inc(s_de, 1)
                if not first:
                    out_rows(b * 2 + (m - 1))
                if not last:
                    act.wait_ge(s_ds, dd + 1)
                    dec_evac(dd * 8 + 8)
                if not first:
                    to_osam(*((b, 0) if m else (b - 1, 1)))

            dec_evac(0)
            dec_act(0, 0)
            dec_act(0, 1)
            with act.Fori(1, DB - 1) as b:
                dec_act(b, 0)
                dec_act(b, 1)
            dec_act(DB - 1, 0)
            dec_act(DB - 1, 1, True)
            out_rows(2 * DB - 1)
            to_osam(DB - 1, 1)

            prompt_act(act)
            act.activation(xn[:, 0:4, 0, S:NT], osam[:, 0], ACT.Copy).then_inc(s_oh, 1)
            def hi(n, slot, dst):
                act.wait_ge(s_raw[slot], raw_count(n, slot))
                act.activation(dst[:, 0], wraw[:, slot], ACT.Copy).then_inc(s_whi, 1)

            for w in range(14):
                if w < 12:
                    if w >= 2:
                        act.wait_ge(s_oss, w - 1)
                    src, n, _ = b_chunk(w)
                    act.wait_ge(s_ohi, 16)
                    act.activation(osq[:, w % 2, 0:n], src, ACT.Square).then_inc(s_osq, 1)
                if 1 <= w < 13:
                    src, n, _ = b_chunk(w - 1)
                    act.wait_ge(s_oss, w)
                    if w >= 5:
                        act.wait_ge(s_osc, w - 4)
                    act.activation(orms[:, (w - 1) % 4, 0:n], ps[:, (w - 1) % 2, 0:n], ACT.Sqrt, bias=small[:, 9:10],
                                   scale=1.0 / P).then_inc(s_ort, 1)
                if w >= 2:
                    src, n, t0 = b_chunk(w - 2)
                    act.wait_ge(s_osc, w - 1)
                    act.activation(xn[:, 4 + (w - 2) % 4, 0, t0:t0 + n], src, ACT.Copy).then_inc(s_oh, 1)
                if w in (5, 9):
                    hi(w // 4 - 1, w // 4 - 1, ws[w // 4 - 1])

            def ffn_hi(layer, b, kinds, par=0):
                for kind in kinds:
                    if kind == "down":
                        act.wait_ge(s_acc, b * ADD_PER + FFN_A[layer])
                    elif isinstance(b, int) and b == 0:
                        act.wait_ge(s_acc, FFN_A[layer])
                    else:
                        act.wait_ge(s_gu, b * GU_PER + FFN_G[layer])
                    hi(unit_of(layer, kind, b), raw_slot(layer, kind, b, par), ws[KINDS.index(kind)])

            def hidden(layer, b, par):
                g0 = b * GU_PER + FFN_G[layer]
                first = isinstance(b, int) and b == 0
                act.wait_ge(s_acc, FFN_A[layer] if first else b * ADD_PER + (FFN_A[layer] - ADD_PER))
                for n in range(GU_PER + 1):
                    if n < GU_PER:
                        act.wait_ge(s_gu, g0 + (n + 1))
                        if not (first and layer == 0 and n < 2):
                            act.wait_ge(s_h, g0 + (n - 1))
                        cn = CH[n % NC][1]
                        act.activation(act_s[:, n % 2, 0:cn], ps[:, 2 * (n % 2), 0:cn], ACT.Silu).then_inc(s_silu, 1)
                    if n >= 1:
                        j, c = divmod(n - 1, NC)
                        c0, cn = CH[c]
                        act.wait_ge(s_h, g0 + n)
                        act.activation(hh[:, par, j, 0, c0:c0 + cn], act_h[:, (n - 1) % 2, 0:cn], ACT.Copy).then_inc(s_hhi, 1)
                    if n == 2 and not first:
                        ffn_hi(layer, b - 1, ("down",), 1 - par)

            def ffn(layer):
                def two(i, last):
                    hidden(layer, i * 2 + 1, 1)
                    ffn_hi(layer, i * 2 + 2, ("gate", "up"), 0)
                    hidden(layer, i * 2 + 2, 0)
                    if not last:
                        ffn_hi(layer, i * 2 + 3, ("gate", "up"), 1)
                norm(1 + 2 * layer, lambda: ffn_hi(layer, 0, ("gate", "up")), 3 * layer)
                act.wait_ge(s_xlo, 24 * (2 + layer))
                if layer == 1:
                    act.wait_ge(s_pout, 32)
                hidden(layer, 0, 0)
                ffn_hi(layer, 1, ("gate", "up"))
                with act.Fori(0, TWOS - 1) as i:
                    two(i, False)
                two(TWOS - 1, True)
                ffn_hi(layer, PAIRS - 1, ("down",))

            for u in range(2, 4):
                if u == 3:
                    act.wait_ge(s_acc, 6)
                hi(u, u % 2, ws[u % 3])
            ffn(0)
            act.wait_ge(s_gu, FFN_G[1])
            hi(37, 1, ws[0])
            def state_rows():
                act.wait_ge(s_stt, 1)
                for k in range(KD):
                    src = ps[:, 4 + k // 4, (k % 4) * P:(k % 4) * P + DB * STATE]
                    act.activation(sample_cols(yp[:, k])[:, :, 1:16], src.rearrange("p (b t) -> p b t", t=STATE), ACT.Copy).then_inc(s_yp, 1)

            norm(2, state_rows)
            act.wait_ge(s_yp, 8)
            act.wait_ge(s_xf, XF0[3])
            act.activation(pcomp[:, :, 0:STATE], yp[:, :, 1 + S:16 + S], ACT.Copy)
            for k in range(KD):
                act.activation(pcomp[:, k, STATE:].rearrange("p (b t) -> p b t", t=STATE), sample_cols(yp[:, k])[:, :, 9:24],
                               ACT.Copy).then_inc(s_pc, 1)
            for k in range(KD):
                act.wait_ge(s_pf, k + 1)
                act.activation(xn[:, k, 0], pf[k % 2][:], ACT.Copy).then_inc(s_pfh, 1)
                if k == 5:
                    act.wait_ge(s_pot, 1)
                    square(3, 0)
                    square(3, 1)
                if k == 6:
                    square(3, 2)
            act.wait_ge(s_pot, 1)
            act.activation(prow[0:STATE, 0], R2(0, STATE), ACT.Copy).then_inc(s_prow, 1)
            act.activation(prow[0:DB * STATE, 1], R2(1, DB * STATE), ACT.Copy).then_inc(s_prow, 1)
            ffn(1)
            norm(4)
            for i in range(9):
                n = P if i < 8 else NS
                act.wait_ge(s_ot, i + 1)
                if i >= 3:
                    act.wait_ge(s_out[i % 3], 16 * (i // 3))
                act.activation(yrow[0:n, i % 3], R2(i % 2, n), ACT.Copy).then_inc(s_oe, 1)

        @block.vector
        def _(dve):
            tt, ts, stt = dve.tensor_tensor, dve.tensor_scalar, dve.scalar_tensor_tensor
            dve.memset(ones[:], 1.0).then_inc(s_ones, 1)
            dve.memset(small[:, 8:9], 1e-6).then_inc(s_ones, 1)
            dve.memset(small[:, 9:10], 1e-5).then_inc(s_ones, 1)
            dve.wait_ge(s_const, 160)
            for j in range(2):
                dve.tensor_tensor_reduce(lamtmp[:, j], lamrow[:, 2 * j], lamrow[:, 2 * j + 1], 1.0, 0.0, ALU.mult, ALU.add,
                                         small[0:1, j:j + 1]).then_inc(s_lam, 1)
            dve.wait_ge(s_gt, 1)
            dve.tensor_copy(gains[:], ps[:, 6, 0:49]).then_inc(s_gains, 1)
            dve.wait_ge(s_lamv, 1)
            tt(small[0:1, 10:11], small[0:1, 2:3], small[0:1, 3:4], ALU.subtract).then_inc(s_small, 1)
            dve.wait_ge(s_small, 1)
            ts(small[0:1, 4:5], small[0:1, 10:11], LAM0, None, ALU.add).then_inc(s_small, 1)
            dve.wait_ge(s_lamb, 1)
            dve.tensor_copy(small[:, 5:6], ps[:, 7, 0:1]).then_inc(s_small, 1)
            ts(small[:, 6:7], ps[:, 7, 0:1], -1.0, None, ALU.mult).then_inc(s_small, 1)
            dve.wait_ge(s_gains, 1)
            ts(small[:, 7:8], gains[:, 48:49], 1.0 - LAM0, None, ALU.mult).then_inc(s_small, 1)
            dve.wait_ge(s_small, 5)

            def fold(r, k):
                for c, (c0, cn) in enumerate(CH if k == KD - 1 else ((0, NT),)):
                    dve.wait_ge(s_sq, SQUARES * r + k + 1 + c)
                    dve.wait_ge(s_fold, FOLDS * r + min(k - 1, KD - 2))
                    tt(rstd[:, c0:c0 + cn], rstd[:, c0:c0 + cn], sq[:, k % 2, c0:c0 + cn], ALU.add).then_inc(s_fold, 1)

            def folds_at(r, idx):
                k, c = divmod(idx, NC)
                if c == NC - 1 and k >= 2:
                    fold(r, k - 1)
                if idx == ADD_PER - 1:
                    fold(r, KD - 1)

            def norm(r, between=None):
                if r == 0:
                    dve.wait_ge(s_x, 9)
                    for k in range(1, KD):
                        fold(0, k)
                for c, (c0, cn) in enumerate(CH):
                    dve.wait_ge(s_rt, NC * r + c + 1)
                    dve.reciprocal(rstd[:, c0:c0 + cn], rstd[:, c0:c0 + cn]).then_inc(s_rstd, 1)
                if between:
                    between()
                if r == 2:
                    pieces = ((0, 364), (364, 364), (728, 296), (S, NS))
                else:
                    pieces = CH
                h0 = 24 * HILO.index(r) if r in HILO else None

                def low(f):
                    c, k = divmod(f, KD)
                    c0, cn = CH[c]
                    dve.wait_ge(s_xhi, h0 + f + 1)
                    tt(xn[:, k, 1, c0:c0 + cn], xf[:, f % 4, 0:cn], xn[:, k, 0, c0:c0 + cn].bitcast(F32), ALU.subtract).then_inc(s_xlo, 1)

                for c, (c0, cn) in enumerate(pieces):
                    dve.wait_ge(s_rstd, NC * r + min(c, 2) + 1)
                    for k in range(KD):
                        f = c * KD + k
                        src, rs = x[:, k, c0:c0 + cn], rstd[:, c0:c0 + cn]
                        if r in HILO:
                            dst = xf[:, f % 4, 0:cn]
                            if f >= 4:
                                dve.wait_ge(s_xlo, h0 + f - 3)
                        elif r == 4:
                            dst = yf[:, k, c0:c0 + cn]
                        elif c < 3:
                            dst = yp[:, k, 16 + c0:16 + c0 + cn]
                        else:
                            dst, src, rs = sample_cols(yp[:, k])[:, :, 16:24], by_sample(src), by_sample(rs)
                        stt(dst, src, gains[:, GAIN[r] + k:GAIN[r] + k + 1], rs, ALU.mult, ALU.mult).then_inc(s_xf, 1)
                        if r in HILO and f >= 2:
                            low(f - 2)
                if r in HILO:
                    low(22)
                    low(23)
                    dve.wait_ge(s_xlo, h0 + 24)

            def proj_lo(m):
                g, half = divmod(m, 2)
                dve.wait_ge(s_phi, m + 1)
                part = wp[:, g % 2, :, 4 * half:4 * half + 4]
                tt(part[:, 1], wpraw[:, m % 2], part[:, 0].bitcast(F32), ALU.subtract).then_inc(s_plo, 1)

            norm(0, lambda: (proj_lo(0), proj_lo(1)))
            for m in range(2, 4):
                proj_lo(m)
            dve.wait_ge(s_cs, 16)
            for g in range(6):
                for i in range(9 if g in ROPE0 else 0):
                    n = P if i < 8 else NS
                    rows = tok[:, (g * 8 + i) % 3] if i < 8 else toks[:, g]
                    c = ROPE0[g] + i
                    r16 = rows.rearrange("p (h c) -> p h c", c=64)[:, :, 0:16]
                    co = rope[0:n, c % 2, 0].rearrange("p (h c) -> p h c", c=16)
                    si = rope[0:n, c % 2, 1].rearrange("p (h c) -> p h c", c=16)
                    dve.wait_ge(s_tok, g * 9 + i + 1)
                    tt(co, r16, cs[0:n, i:i + 1, 0:16].to_broadcast([n, 8, 16]), ALU.mult).then_inc(s_ropeP, 1)
                    tt(si, r16, cs[0:n, i:i + 1, 16:32].to_broadcast([n, 8, 16]), ALU.mult).then_inc(s_ropeP, 1)
                    dve.wait_ge(s_ropeP, 2 * c + 2)
                    tt(r16[:, :, 0:8], co[:, :, 0:8], si[:, :, 8:16], ALU.subtract)
                    tt(r16[:, :, 8:16], co[:, :, 8:16], si[:, :, 0:8], ALU.add).then_inc(s_rope, 1)
                if g + 2 < 6:
                    proj_lo(2 * g + 4)
                    proj_lo(2 * g + 5)

            dve.wait_ge(s_dc, 80)
            dve.memset(dmask[:, 1, 0:PAST], 0.0).then_inc(s_dmk, 1)
            dve.memset(qblk[:], 0.0).then_inc(s_qz, 1)
            stt(comb[:, 2], comb[:, 1], small[:, 6:7], comb[:, 0], ALU.mult, ALU.add).then_inc(s_cmbd, 1)
            dve.wait_ge(s_qz, 1)
            dve.wait_ge(s_qk, 4)
            for m in range(2):
                for jp in range(4):
                    for hf in range(2):
                        h64 = slice(64 * hf, 64 * hf + 64)
                        dve.tensor_copy(qblk[h64, m, :, jp, 8 * hf:8 * hf + 8],
                                        ps[h64, 2 * m, 64 * jp:64 * jp + 64].rearrange("p (b t) -> p b t", t=T)).then_inc(s_qb, 1)
                dve.tensor_copy(knT[:, m], ps[:, 2 * m + 1, 0:256].rearrange("p (j n) -> p j n", n=NS)).then_inc(s_qb, 1)
            dve.wait_ge(s_qb, 18)

            def next_q(b, m):
                dve.tensor_copy(qcur[:, m], qblk[:, m, bass.ds(b, 1)].rearrange("p a j n -> p (a j) n")).then_inc(s_qc, 1)
                dve.tensor_copy(dmask[:, m, PAST:PAST + NS], dnew[:, m, bass.ds(b * -8 + 56, NS)]).then_inc(s_dmk, 1)

            def dec_evac(tr):
                for j in range(1, 8, 2):
                    dve.wait_ge(s_dtr, tr + j + 1)
                    dve.tensor_copy(dkT[:, :, j * P:(j + 1) * P], TK(j)).then_inc(s_dev, 1)

            def dec_dve(b, m, final):
                dd = b * 2 + m
                dve.wait_ge(s_ds, dd + 1)
                dve.wait_ge(s_dmk, dd + 2)
                dve.memset(small[:, 11:12], 0.0)
                dve.tensor_tensor_reduce(dse[:, m], ps[:, 0:3].rearrange("p a n -> p (a n)")[:, 0:PAST + NS], dmask[:, m], 1.0,
                                         -3.0e38, ALU.add, ALU.max, dstat[:, m, 0:1]).then_inc(s_dsm, 1)
                dve.wait_ge(s_dsm, dd + 1)
                ts(dstat[:, m, 1:2], dstat[:, m, 0:1], -0.125, None, ALU.mult).then_inc(s_dnm, 1)
                if not final:
                    next_q(b + 1, m)
                if not (final and m):
                    dec_evac(dd * 8 + 8)
                dve.wait_ge(s_de, dd + 1)
                dve.reciprocal(dstat[:, m, 3:4], dstat[:, m, 2:3]).then_inc(s_drd, 1)
                dve.wait_ge(s_drd, dd + 1)
                mix_w = (dmix[:, 1, 0:32], comb[:, 2]) if m else (dmix[:, 0], comb[:, 0:2].rearrange("p a n -> p (a n)"))
                ts(*mix_w, dstat[:, m, 3:4], None, ALU.mult).then_inc(s_dmx, 1)
                dve.wait_ge(s_dpt, dd + 1)
                dve.tensor_copy(dpT[:, m, 0:8], ps[:, 6:8].rearrange("p a (k n) -> p (a k) n", n=P))
                dve.tensor_copy(dpT[0:64, m, 8], ps[0:64, 3, P:2 * P]).then_inc(s_dpe, 1)

            next_q(0, 0)
            next_q(0, 1)
            dec_evac(0)
            with dve.Fori(0, DB - 1) as b:
                dec_dve(b, 0, False)
                dec_dve(b, 1, False)
            dec_dve(DB - 1, 0, True)
            dec_dve(DB - 1, 1, True)

            prompt_dve(dve)
            dve.wait_ge(s_oh, 1)
            tt(xn[:, 0:4, 1, S:NT], osam[:, 0], xn[:, 0:4, 0, S:NT].bitcast(F32), ALU.subtract).then_inc(s_ol, 1)
            def lo(n, slot, dst):
                dve.wait_ge(s_whi, n + 1)
                tt(dst[:, 1], wraw[:, slot], dst[:, 0].bitcast(F32), ALU.subtract).then_inc(s_wlo, 1)

            for w in range(13):
                if w < 12:
                    src, n, _ = b_chunk(w)
                    root = orms[:, w % 4, 0:n]
                    dve.wait_ge(s_ort, w + 1)
                    dve.reciprocal(root, root).then_inc(s_orr, 1)
                    dve.wait_ge(s_orr, w + 1)
                    stt(src, src, small[:, 7:8], root, ALU.mult, ALU.mult).then_inc(s_osc, 1)
                if w >= 1:
                    src, n, t0 = b_chunk(w - 1)
                    dve.wait_ge(s_oh, w + 1)
                    o = xn[:, 4 + (w - 1) % 4, :, t0:t0 + n]
                    tt(o[:, 1], src, o[:, 0].bitcast(F32), ALU.subtract).then_inc(s_ol, 1)
                if w in (6, 10):
                    lo(w // 4 - 1, w // 4 - 1, ws[w // 4 - 1])

            def ffn_lo(layer, b, kind, par=0):
                lo(unit_of(layer, kind, b), raw_slot(layer, kind, b, par), ws[KINDS.index(kind)])

            def add(a, idx, scale=None):
                k, c = divmod(idx, NC)
                c0, cn = CH[c]
                dst = x[:, k, c0:c0 + cn]
                dve.wait_ge(s_acc, a + 1)
                if scale is None:
                    tt(dst, ps[:, 4 + idx % 4, 0:cn], dst, ALU.add).then_inc(s_added, 1)
                else:
                    stt(dst, ps[:, 4 + idx % 4, 0:cn], scale, dst, ALU.mult, ALU.add).then_inc(s_added, 1)

            def hidden(layer, b, par):
                g0 = b * GU_PER + FFN_G[layer]
                first = isinstance(b, int) and b == 0
                for n in range(GU_PER + 1):
                    if n < GU_PER:
                        dve.wait_ge(s_silu, g0 + (n + 1))
                        if not (first and layer == 0 and n < 2):
                            dve.wait_ge(s_hlo, g0 + (n - 1))
                        cn = CH[n % NC][1]
                        tt(act_h[:, n % 2, 0:cn], act_s[:, n % 2, 0:cn], ps[:, 2 * (n % 2) + 1, 0:cn], ALU.mult).then_inc(s_h, 1)
                    if n >= 1:
                        j, c = divmod(n - 1, NC)
                        c0, cn = CH[c]
                        dve.wait_ge(s_hhi, g0 + n)
                        o = hh[:, par, j, :, c0:c0 + cn]
                        tt(o[:, 1], act_h[:, (n - 1) % 2, 0:cn], o[:, 0].bitcast(F32), ALU.subtract).then_inc(s_hlo, 1)
                    if n == 3 and not first:
                        ffn_lo(layer, b - 1, "down", 1 - par)

            def adds(layer, b, splits=()):
                for idx in range(ADD_PER):
                    add(b * ADD_PER + (FFN_A[layer] + idx), idx)
                    if isinstance(b, int) and b == PAIRS - 1:
                        folds_at(2 * layer + 2, idx)
                    if splits and idx in (2, 6):
                        ffn_lo(layer, splits[0], ("gate", "up")[idx == 6], splits[1])

            def ffn(layer):
                def two(i, last):
                    hidden(layer, i * 2 + 1, 1)
                    adds(layer, i * 2, (i * 2 + 2, 0))
                    hidden(layer, i * 2 + 2, 0)
                    adds(layer, i * 2 + 1, () if last else (i * 2 + 3, 1))
                def first_weights():
                    ffn_lo(layer, 0, "gate")
                    ffn_lo(layer, 0, "up")
                norm(1 + 2 * layer, first_weights)
                if layer == 1:
                    dve.wait_ge(s_pout, 32)
                hidden(layer, 0, 0)
                ffn_lo(layer, 1, "gate")
                ffn_lo(layer, 1, "up")
                with dve.Fori(0, TWOS - 1) as i:
                    two(i, False)
                two(TWOS - 1, True)
                ffn_lo(layer, PAIRS - 1, "down")
                adds(layer, PAIRS - 1)

            lo(2, 0, ws[2])
            for idx in range(ADD_PER):
                add(idx, idx)
                folds_at(1, idx)
                if idx == 5:
                    lo(3, 1, ws[0])
            ffn(0)

            lo(37, 1, ws[0])
            norm(2)
            dve.wait_ge(s_yp, 8)
            dve.wait_ge(s_pz, 2)
            dve.wait_ge(s_xf, XF0[3])
            def pool_low(k):
                dve.wait_ge(s_pfh, k + 1)
                dve.wait_ge(s_pf, k + 1)
                tt(xn[:, k, 1], pf[k % 2][:], xn[:, k, 0].bitcast(F32), ALU.subtract).then_inc(s_pfl, 1)

            def pool_adds(g):
                for idx in range(2 * NC * g, 2 * NC * (g + 1)):
                    kk = idx // NC
                    add(PAIRS * ADD_PER + FFN_A[0] + idx, idx, gains[:, 40 + kk:41 + kk])
                    if g == 3:
                        folds_at(3, idx)

            level = 0
            dve.wait_ge(s_corr, 16)
            for k in range(KD):
                g = k // 2
                src = yp[:, k]
                lead = 1
                if k:
                    dve.wait_ge(s_pf, k)
                for e in range(g + 1):
                    dst = pa[:, e % 2]
                    step = 1 << e
                    if e:
                        dve.wait_ge(s_lvl, level)
                    tt(dst[:, lead:PADW], src[:, lead:PADW], src[:, lead - step:PADW - step], ALU.add).then_inc(s_lvl, 1)
                    level += 1
                    src = dst
                    lead += 2 * step
                dve.wait_ge(s_lvl, level)
                tt(src[:, 16:32], src[:, 16:32], corr[:, g], ALU.mult).then_inc(s_lvl, 1)
                level += 1
                dve.wait_ge(s_lvl, level)
                w = 0.5 / (1 << g)
                if k >= 2:
                    dve.wait_ge(s_pfl, k - 1)
                stt(pf[k % 2][:, 0:S], src[:, 16:16 + S], w, yp[:, k, 16:16 + S], ALU.mult, ALU.subtract)
                stt(by_sample(pf[k % 2][:, S:NT]), sample_cols(src)[:, :, 16:24], w, sample_cols(yp[:, k])[:, :, 16:24],
                    ALU.mult, ALU.subtract).then_inc(s_pf, 1)
                if k:
                    pool_low(k - 1)
                if k == 6:
                    fold(3, 1)
                if k % 2 and k > 1:
                    pool_adds(g - 1)
            fold(3, 2)
            pool_low(KD - 1)
            fold(3, 3)
            fold(3, 4)
            pool_adds(3)
            ffn(1)
            norm(4)

        @block.tensor
        def _(pe):
            mm = pe.matmul

            def product(out, pairs, last=None):
                n = len(pairs)
                for i, (w, m) in enumerate(pairs):
                    for q_, (a, b_) in enumerate(((1, 0), (0, 1), (0, 0))):
                        r = mm(out, w(a), m(b_), start=(i == 0 and q_ == 0), stop=(i == n - 1 and q_ == 2))
                return r

            pe.wait_ge(s_const, 160)
            for i in range(9):
                n = P if i < 8 else NS
                pe.wait_ge(s_xin[i % 3], 16 * (i // 3 + 1))
                if i >= 2:
                    pe.wait_ge(s_x, i - 1)
                for k in range(KD):
                    r = pe.transpose(T2(i % 2, n)[:, k], xin[0:n, i % 3, k * P:(k + 1) * P], ident[0:n, 0:n])
                r.then_inc(s_xt, 1)
            pe.transpose(ps[:, 6, 0:49], grow[:], ident[0:49, 0:49]).then_inc(s_gt, 1)
            pe.wait_ge(s_ones, 3)
            pe.wait_ge(s_small, 2)
            mm(ps[:, 7, 0:1], ones[0:1, :], small[0:1, 4:5], start=True, stop=True).then_inc(s_lamb, 1)

            def norm(r):
                for c, (c0, cn) in enumerate(CH):
                    pe.wait_ge(s_fold, FOLDS * r + KD - 1 + c)
                    mm(ps[:, c, 0:cn], ones[:], rstd[:, c0:c0 + cn], start=True, stop=True).then_inc(s_ss, 1)

            norm(0)
            for g in range(6):
                pe.wait_ge(s_plo, 2 * g + 2)
                for i in range(9):
                    n = P if i < 8 else NS
                    m = g * 9 + i
                    if g == 0:
                        c = 0 if i < 2 else 1 if i < 5 else 2
                        pe.wait_ge(s_xlo, 8 * (c + 1))
                    if m >= 8:
                        pe.wait_ge(s_tok, m - 7)
                    elif m < 3:
                        pe.wait_ge(s_rt, 3)
                    elif m >= 6:
                        pe.wait_ge(s_small, 5)
                    product(ps[0:n, m % 8], [(lambda a, k=k: xn[:, k, a, i * P:i * P + n], lambda a, k=k: wp[:, g % 2, a, k])
                                             for k in range(KD)]).then_inc(s_proj, 1)

            pe.wait_ge(s_tok, 54)
            pe.wait_ge(s_rope, 36)
            for m in range(2):
                for a in range(2):
                    for jp in range(4):
                        q_ = pe.transpose(ps[:, 2 * m + a, 64 * jp:64 * jp + 64], toks[:, 3 * m + a, jp * P:(jp + 1) * P], ident[0:NS, 0:NS])
                    q_.then_inc(s_qk, 1)

            def dec_transposes(b, m):
                dd = b * 2 + m
                first = isinstance(b, int) and b == 0 and m == 0
                pe.wait_ge(s_dk[m], (b + 1) * (128 if m else 16))
                for j in range(8):
                    if not (first and j < 2):
                        pe.wait_ge(s_dev if j % 2 else s_dea, dd * 4 + j // 2)
                    for jp in range(4):
                        q_ = pe.transpose(TK(j)[:, jp], kraw[m][:, j, jp * P:(jp + 1) * P], ident[:])
                    q_.then_inc(s_dtr, 1)

            def dec_scores(b, m):
                dd = b * 2 + m
                pe.wait_ge(s_qc, dd + 1)
                pe.wait_ge(s_dea, dd * 4 + 4)
                pe.wait_ge(s_dev, dd * 4 + 4)
                if not (isinstance(dd, int) and dd == 0):
                    pe.wait_ge(s_dsm, dd)
                for a in range(3):
                    for jp in range(4):
                        mv = knT[:, m, jp] if a == 2 else dkT[:, jp, a * 512:(a + 1) * 512]
                        q_ = mm(ps[32 * jp:32 * jp + 32, a, 0:(64 if a == 2 else 512)], qcur[:, m, jp], mv, start=True, stop=True)
                q_.then_inc(s_ds, 1)

            def dec_turn(dd, m):
                pe.wait_ge(s_de, dd + 1)
                pe.wait_ge(s_dpe, dd)
                for j in range(8):
                    if j == 7:
                        pe.wait_ge(s_dos, dd)
                    pe.transpose(ps[:, 6 + j // 4, (j % 4) * P:(j % 4 + 1) * P], dse[:, m, j * P:(j + 1) * P], ident[:])
                pe.transpose(ps[0:NS, 3, P:2 * P], dse[:, m, PAST:PAST + NS], ident[:]).then_inc(s_dpt, 1)

            def dec_values(b, m):
                dd = b * 2 + m
                pe.wait_ge(s_dpe, dd + 1)
                pe.wait_ge(s_dom, dd)
                pe.wait_ge(s_dv[m], (b + 1) * (128 if m else 16))
                for j in range(9):
                    for jp in range(4):
                        rows, cols = slice(32 * jp, 32 * jp + 32), slice(jp * P, (jp + 1) * P)
                        w, v = ((dpT[:, m, j, rows], vraw[m][:, j, cols]) if j < 8 else
                                (dpT[0:NS, m, 8, rows], toks[:, 3 * m + 2, cols]))
                        q_ = mm(ps[rows, 3, 0:P], w, v, start=(j == 0), stop=(j == 8))
                q_.then_inc(s_dpv, 1)

            def dec_combine(dd, m):
                pe.wait_ge(s_dom, dd + 1)
                pe.wait_ge(s_dmx, dd + 1)
                if m:
                    mm(ps[:, 3, 256:288], dom[:], dmix[:, 1, 0:32], start=True, stop=True).then_inc(s_dot, 1)
                else:
                    for hf in range(2):
                        h64 = slice(64 * hf, 64 * hf + 64)
                        q_ = mm(ps[h64, 3, 256:288], dom[:, h64], dmix[:, 0, 32 * hf:32 * hf + 32], start=True, stop=True)
                    q_.then_inc(s_dot, 1)

            def dec_step(b, m, last=False):
                dd = b * 2 + m
                nxt = (b + 1, 0) if m else (b, 1)
                if not last:
                    dec_transposes(*nxt)
                if not (isinstance(dd, int) and dd == 0):
                    dec_combine(b * 2 + (m - 1), 1 - m)
                dec_turn(dd, m)
                if not last:
                    dec_scores(*nxt)
                dec_values(b, m)

            dec_transposes(0, 0)
            dec_scores(0, 0)
            dec_step(0, 0)
            dec_step(0, 1)
            with pe.Fori(1, DB - 1) as b:
                dec_step(b, 0)
                dec_step(b, 1)
            dec_step(DB - 1, 0)
            dec_step(DB - 1, 1, True)
            dec_combine(2 * DB - 1, 1)

            prompt_pe(pe)
            def head_squares(ws_):
                for w in ws_:
                    _, n, _ = b_chunk(w)
                    pe.wait_ge(s_osq, w + 1)
                    if w >= 2:
                        pe.wait_ge(s_ort, w - 1)
                    mm(ps[:, w % 2, 0:n], ones[:], osq[:, w % 2, 0:n], start=True, stop=True).then_inc(s_oss, 1)

            head_squares(range(8))
            def group(a, idx, pairs):
                k, c = divmod(idx, NC)
                if not isinstance(a, int) or a >= 4:
                    pe.wait_ge(s_added, a - 3)
                product(ps[:, 4 + idx % 4, 0:CH[c][1]], pairs).then_inc(s_acc, 1)

            def moving(k, c):
                c0, cn = CH[c]
                return lambda a: xn[:, k, a, c0:c0 + cn]

            for idx in range(ADD_PER):
                kt, c = divmod(idx, NC)
                u, e = divmod(kt, 2)
                if idx == 1:
                    head_squares(range(8, 12))
                pe.wait_ge(s_wlo, u + 1)
                if kt == 0:
                    pe.wait_ge(s_ol, 5 + 4 * c)
                group(idx, idx, [(lambda a, k=k: ws[u % 3][:, a, k * 256 + e * P:k * 256 + e * P + P], moving(k, c)) for k in range(KD)])

            def hidden(layer, b):
                g0 = b * GU_PER + FFN_G[layer]
                first = isinstance(b, int) and b == 0
                pe.wait_ge(s_wlo, unit_of(layer, "up", b) + 1)
                for n in range(GU_PER):
                    j, c = divmod(n, NC)
                    if first and j == 0:
                        f0 = 24 * (1 + layer) + 8 * (c + 1)
                        pe.wait_ge(s_xlo, f0)
                    if not (first and layer == 0 and n < 2):
                        pe.wait_ge(s_h, g0 + (n - 1))
                    elif n == 0:
                        pe.wait_ge(s_rt, 6)
                    for a_ in range(2):
                        q_ = product(ps[:, 2 * (n % 2) + a_, 0:CH[c][1]],
                                     [(lambda a, k=k: ws[a_][:, a, k * 256 + j * P:k * 256 + j * P + P], moving(k, c)) for k in range(KD)])
                    q_.then_inc(s_gu, 1)

            def down(layer, b, par):
                pe.wait_ge(s_hlo, b * GU_PER + (FFN_G[layer] + GU_PER))
                pe.wait_ge(s_wlo, unit_of(layer, "down", b) + 1)
                for idx in range(ADD_PER):
                    kt, c = divmod(idx, NC)
                    c0, cn = CH[c]
                    group(b * ADD_PER + (FFN_A[layer] + idx), idx,
                          [(lambda a, j=j: ws[2][:, a, j * D + kt * P:j * D + kt * P + P], lambda a, j=j: hh[:, par, j, a, c0:c0 + cn])
                           for j in range(2)])

            def ffn(layer):
                norm(1 + 2 * layer)
                hidden(layer, 0)
                with pe.Fori(0, TWOS) as i:
                    hidden(layer, i * 2 + 1)
                    down(layer, i * 2, 0)
                    hidden(layer, i * 2 + 2)
                    down(layer, i * 2 + 1, 1)
                down(layer, PAIRS - 1, 0)

            ffn(0)
            pe.wait_ge(s_st, 16)
            pe.wait_ge(s_added, FFN_A[0] + PAIRS * ADD_PER)
            for k in range(KD):
                q_ = pe.transpose(ps[:, 4 + k // 4, (k % 4) * P:(k % 4) * P + DB * STATE], stin[:, k * P:(k + 1) * P], ident[0:120, 0:120])
            q_.then_inc(s_stt, 1)
            norm(2)
            pe.wait_ge(s_pc, KD)
            pe.wait_ge(s_rt, 9)
            for k in range(KD):
                pe.transpose(R2(0, STATE)[:, k * P:(k + 1) * P], pcomp[:, k, 0:STATE], ident[:])
                q_ = pe.transpose(R2(1, DB * STATE)[:, k * P:(k + 1) * P], pcomp[:, k, STATE:], ident[:])
            q_.then_inc(s_pot, 1)
            pe.wait_ge(s_wlo, 38)
            for idx in range(ADD_PER):
                kt, c = divmod(idx, NC)
                g, e = divmod(kt, 2)
                pe.wait_ge(s_pfl, 2 * g + 2)
                group(PAIRS * ADD_PER + FFN_A[0] + idx, idx,
                      [(lambda a, j=j: ws[0][:, a, (2 * g + j) * 256 + e * P:(2 * g + j) * 256 + e * P + P], moving(2 * g + j, c)) for j in range(2)])
            pe.wait_ge(s_prow, 2)
            ffn(1)
            norm(4)
            for i in range(9):
                n = P if i < 8 else NS
                c = 0 if i < 2 else 1 if i < 5 else 2
                pe.wait_ge(s_xf, XF0[4] + 8 * (c + 1))
                if i >= 2:
                    pe.wait_ge(s_oe, i - 1)
                else:
                    pe.wait_ge(s_rt, 15)
                for k in range(KD):
                    q_ = pe.transpose(R2(i % 2, n)[:, k * P:(k + 1) * P], yf[:, k, i * P:i * P + n], ident[:])
                q_.then_inc(s_ot, 1)


_INS = ["x_prompt", "x_sample", "cache_k_b", "cache_v_b", "cache_win_k_a", "cache_win_v_a", "state_pool", "page_table",
        "ln_mix", "ln_ffn", "ln_final", "w_in", "w_out", "lambda_q1", "lambda_k1", "lambda_q2", "lambda_k2", "subln_g",
        "pool_w", "pool_scale", "w_gate", "w_up", "w_down"]
_OUTS = [("o_y_p", (1, S, D)), ("o_y_s", (DB, T, D)),
         ("o_kb_p", (1, 1, S, 4, 128)), ("o_vb_p", (1, 1, S, 4, 128)),
         ("o_kb_s", (1, DB, T, 4, 128)), ("o_vb_s", (1, DB, T, 4, 128)),
         ("o_wk_p", (1, 1, S, 8, 64)), ("o_wv_p", (1, 1, S, 8, 64)),
         ("o_wk_s", (1, DB, PAST, 8, 64)), ("o_wv_s", (1, DB, PAST, 8, 64)),
         ("o_pl_p", (1, 1, STATE, D)), ("o_pl_s", (1, DB, STATE, D))]


def kernel(**inputs):
    import numpy as _np
    import concourse.bacc as _bacc
    from concourse import mybir as _mybir
    from concourse.bass_utils import run_bass_kernel_spmd as _run

    nc = _bacc.Bacc("TRN2", target_bir_lowering=False, num_devices=1)
    arrays, aps = {}, {}
    for name in _INS:
        a = _np.ascontiguousarray(inputs[name])
        arrays[name] = a
        aps[name] = nc.dram_tensor(name, a.shape, _mybir.dt.from_np(a.dtype), kind="ExternalInput").ap()
    arrays["consts"] = shape_constants()
    aps["consts"] = nc.dram_tensor("consts", (P, CONST_W), F32, kind="ExternalInput").ap()
    for name, shape in _OUTS:
        aps[name] = nc.dram_tensor(name, shape, F32, kind="ExternalOutput").ap()
    build_step(nc, aps)
    r = _run(nc, [arrays], core_ids=[0])
    return tuple(r.results[0][name] for name, _ in _OUTS)
```

```python
from contextlib import ExitStack

import numpy as np

import concourse.bass as bass
from concourse import mybir

F32 = mybir.dt.float32
F32R = mybir.dt.float32r
I32 = mybir.dt.int32
ALU = mybir.AluOpType
ACT = mybir.ActivationFunctionType
AX = mybir.AxisListType

P = 128
D = 1024
KD = D // P
S = 1024
DB, T = 8, 8
NS = DB * T
NT = S + NS
NTILE = S // P
FF = 2816
PAIRS = FF // 256
CH = ((0, 364), (364, 364), (728, 360))
NC = len(CH)
CW = 364
PAST = 1024
PAGE = 128
NPAGE = PAST // PAGE
NPHYS = 80
NEG = -1e30
RING, LAG = 8, 3
LAM0 = 0.2
PADW = 16 + S + DB * 24
STATE = 15

OFF = {}
W = 0
for _name, _n in (("ident", 128), ("cs", 9 * 32), ("maskA", 1024), ("maskB", 1024), ("decA", 1024), ("newA", 120),
                  ("newB", 120), ("comb0", 32), ("comb1", 32), ("corr", 64)):
    OFF[_name] = (W, _n)
    W += _n
CONST_W = W


def shape_constants():
    c = np.zeros((P, CONST_W), np.float32)

    def put(name, a):
        o, n = OFF[name]
        c[:a.shape[0], o:o + n] = a.reshape(a.shape[0], n)

    def times(off):
        return (((off >= 0) & (off <= 128)).astype(int) + ((off >= 0) & (off <= 512) & (off % 4 == 0))
                + ((off >= 0) & (off <= 2048) & (off % 16 == 0)))

    def log8(n):
        return np.where(n > 0, 8.0 * np.log(np.maximum(n, 1)), NEG).astype(np.float32)

    put("ident", np.eye(P, dtype=np.float32))
    inv = np.float32(500000.0) ** (-np.arange(8, dtype=np.float32) * np.float32(2.0) / np.float32(16))
    pos = np.zeros((9, P), np.float32)
    pos[:8] = np.arange(S).reshape(8, P)
    pos[8, :NS] = PAST + np.arange(NS) % T
    ang = (pos[..., None] * inv.astype(np.float32)).astype(np.float32).transpose(1, 0, 2)
    co, si = np.cos(ang).astype(np.float32), np.sin(ang).astype(np.float32)
    put("cs", np.concatenate([co, co, si, si], axis=-1))
    p, y = np.arange(P)[:, None], np.arange(1024)[None]
    put("maskA", log8(times(p + 896 - y)))
    put("maskB", np.where(p + 896 - y >= 0, 0, NEG).astype(np.float32))
    r = np.arange(P)[:, None]
    put("decA", log8(times(1024 + r % 8 - (8 * (y % 128) + y // 128))))
    z = np.arange(120)[None] - 56
    ok = (z >= 0) & (z <= r % 8)
    put("newA", np.where(ok, log8(times(r % 8 - z)), NEG).astype(np.float32))
    put("newB", np.where(ok, 0, NEG).astype(np.float32))
    o = np.arange(32)[None]
    for half in range(2):
        put(f"comb{half}", ((r // 32 == o // 8) & (r % 32 == 8 * half + o % 8)).astype(np.float32))
    corr = np.stack([w / np.minimum(np.arange(16) + 1, w) for w in (2, 4, 8, 16)]).astype(np.float32)
    put("corr", np.broadcast_to(corr.reshape(1, 64), (P, 64)))
    return c


def build_step(nc, d):
    st = ExitStack()
    with st:
        base = (nc.sbuf_base + 63) // 64 * 64
        at = [base]

        def persistent(name, shape, dt=F32):
            t = nc.alloc_sbuf_tensor_at(name, shape, dt, offset=at[0])
            at[0] += (int(np.prod(shape[1:])) * 4 + 31) // 32 * 32
            return t

        x = persistent("x", [P, KD, NT])
        ident = persistent("ident", [P, P])
        ones = persistent("ones", [P, P])
        gains = persistent("gains", [P, 49])
        small = persistent("small", [P, 24])
        xn_at = at[0]
        xn = persistent("xn", [P, KD, 2, NT], F32R)
        rest = at[0]

        def placed(name, off, shape, dt=F32):
            return nc.alloc_sbuf_tensor_at(name, shape, dt, offset=off)

        ws = [placed("ws0", rest, [P, 2, 2048], F32R), placed("ws1", rest + 32768, [P, 2, 2048], F32R),
              placed("ws2", rest + 49152, [P, 2, 2048], F32R)]
        wraw = placed("wraw", rest + 16384, [P, 2, 2048])
        hh = placed("hh", rest + 65536, [P, 2, 2, 2, NT], F32R)
        act_s = placed("act_s", rest + 100352, [P, 2, CW])
        act_h = placed("act_h", rest + 100352 + 2912, [P, 2, CW])
        nrm = rest + 106176 - 18880
        sq = placed("sq", nrm, [P, 2, NT])
        rstd = placed("rstd", nrm + 8704, [P, NT])
        xf = placed("xf", nrm + 13056, [P, 4, CW])
        xin = placed("xin", rest, [P, 3, D])
        grow = placed("grow", rest + 12288, [49, P])
        lamrow = placed("lamrow", rest + 12800, [1, 4, 64])
        lamtmp = placed("lamtmp", rest + 14080, [1, 2, 64])
        wp = placed("wp", rest, [P, 2, 2, KD, 512], F32R)
        wpraw = placed("wpraw", rest + 65536, [P, 2, 4, 512])
        tok = placed("tok", rest + 81920, [P, 3, 512])
        toks = placed("toks", rest + 88064, [NS, 6, 512])
        cs = placed("cs", rest + 100352, [P, 9, 32])
        rope = placed("rope", rest + 101504, [P, 2, 2, 128])
        osam = placed("osam", rest + 103552, [P, 2, 4, NS])
        kraw, vraw = ([placed(f"{name}{m}", rest + 32768 * m + off, [P, 8, 512]) for m in range(2)]
                      for name, off in (("kraw", 0), ("vraw", 16384)))
        q = xn_at
        dkT = placed("dkT", q, [P, 4, PAST])
        dse = placed("dse", q + 16384, [P, 2, PAST + NS])
        dpT = placed("dpT", q + 25088, [P, 2, 9, P])
        dom = placed("dom", q + 34304, [P, P])
        qblk = placed("qblk", q + 34816, [P, 2, DB, 4, 32])
        qcur = placed("qcur", q + 43008, [P, 2, 4, 32])
        knT = placed("knT", q + 44032, [P, 2, 4, NS])
        dmask = placed("dmask", q + 46080, [P, 2, PAST + NS])
        dnew = placed("dnew", q + 54784, [P, 2, 120])
        comb = placed("comb", q + 55744, [P, 3, 32])
        dmix = placed("dmix", q + 56128, [P, 2, 64])
        dstat = placed("dstat", q + 56640, [P, 2, 4])
        ptab = placed("ptab", rest + 105600, [1, DB * NPAGE], I32)
        qkv = placed("qkv", rest, [P, 2, 3, 8, 128])
        qT = placed("qT", rest + 24576, [P, S])
        kT = placed("kT", rest + 28672, [P, S])
        sm = placed("sm", rest + 32768, [P, RING, S])
        pT = placed("pT", rest + 65536, [P, 2, 8, 512])
        ob = placed("ob", rest + 81920, [P, 4, S])
        pmask = placed("pmask", rest + 98304, [P, S])
        pstat = placed("pstat", rest + 102400, [P, RING, 4])
        osq = placed("osq", rest + 73728, [P, 2, 512])
        orms = placed("orms", rest + 65536, [P, 4, 512])
        yp = placed("yp", rest + 32768, [P, KD, PADW])
        pa = placed("pa", rest + 32768 + KD * PADW * 4, [P, 2, PADW])
        pf = (placed("pf0", rest + 32768 + (KD + 2) * PADW * 4, [P, NT]), placed("pf1", nrm + 13056, [P, NT]))
        stin = placed("stin", rest + 32768 + KD * PADW * 4, [DB * STATE, D])
        corr = placed("corr", nrm - 256, [P, 4, 16])
        yf = placed("yf", xn_at, [P, KD, NT])
        yrow = placed("yrow", rest, [P, 3, D])
        prow = placed("prow", rest + 32768 + KD * PADW * 4, [P, 2, D])

        ps = st.enter_context(nc.psum_tensor("ps", [P, 8, 512], F32))
        pcomp = placed("pcomp", nrm, [P, KD, STATE * (DB + 1)])
        qs_dram = nc.dram_tensor("q_rows", [2, S, 512], F32, kind="Internal").ap()

        def sem(name):
            return st.enter_context(nc.semaphore(name))

        consts = d["consts"]

        def const(name, rows=P):
            o, n = OFF[name]
            return consts[0:rows, o:o + n]

        consts_loaded = sem("consts_loaded")
        input_rows_loaded = [sem(f"input_rows_loaded{i}") for i in range(3)]
        fills_done = sem("fills_done")
        input_transposed = sem("input_transposed")
        x_ready = sem("x_ready")
        gains_transposed = sem("gains_transposed")
        gains_ready = sem("gains_ready")
        lambda_dots = sem("lambda_dots")
        lambda_exps = sem("lambda_exps")
        lambda_broadcast = sem("lambda_broadcast")
        small_ready = sem("small_ready")
        squares_ready = sem("squares_ready")
        squares_added = sem("squares_added")
        squares_summed = sem("squares_summed")
        roots_ready = sem("roots_ready")
        rstd_ready = sem("rstd_ready")
        norm_pieces = sem("norm_pieces")
        norm_hi = sem("norm_hi")
        norm_lo = sem("norm_lo")
        proj_w_loaded = [sem(f"proj_w_loaded{i}") for i in range(2)]
        proj_w_hi = sem("proj_w_hi")
        proj_w_lo = sem("proj_w_lo")
        rotary_loaded = sem("rotary_loaded")
        proj_done = sem("proj_done")
        proj_rows = sem("proj_rows")
        rotary_products = sem("rotary_products")
        rows_rotated = sem("rows_rotated")
        rows_stored = [sem(f"rows_stored{i}") for i in range(3)]
        sample_rows_stored = sem("sample_rows_stored")
        unit_loaded = [sem(f"unit_loaded{i}") for i in range(2)]
        unit_hi = sem("unit_hi")
        unit_lo = sem("unit_lo")
        gate_up_done = sem("gate_up_done")
        silu_ready = sem("silu_ready")
        hidden_ready = sem("hidden_ready")
        hidden_hi = sem("hidden_hi")
        hidden_lo = sem("hidden_lo")
        group_done = sem("group_done")
        group_added = sem("group_added")
        dec_tables_loaded = sem("dec_tables_loaded")
        dec_k_loaded = [sem(f"dec_k_loaded{i}") for i in range(2)]
        dec_v_loaded = [sem(f"dec_v_loaded{i}") for i in range(2)]
        windows_moved = sem("windows_moved")
        page_table_loaded = sem("page_table_loaded")
        dec_q_zeroed = sem("dec_q_zeroed")
        dec_qk_turned = sem("dec_qk_turned")
        dec_qk_ready = sem("dec_qk_ready")
        dec_k_turned = sem("dec_k_turned")
        dec_k_odd = sem("dec_k_odd")
        dec_k_even = sem("dec_k_even")
        dec_q_current = sem("dec_q_current")
        dec_scores_done = sem("dec_scores_done")
        dec_masked = sem("dec_masked")
        dec_negmax = sem("dec_negmax")
        dec_exps = sem("dec_exps")
        dec_recip = sem("dec_recip")
        dec_weights = sem("dec_weights")
        dec_p_turned = sem("dec_p_turned")
        dec_p_ready = sem("dec_p_ready")
        dec_values_done = sem("dec_values_done")
        dec_rows_out = sem("dec_rows_out")
        dec_combined = sem("dec_combined")
        dec_stored = sem("dec_stored")
        dec_mask_ready = sem("dec_mask_ready")
        dec_comb_ready = sem("dec_comb_ready")
        mask_loaded = sem("mask_loaded")
        qkv_loaded = [sem(f"qkv_loaded{i}") for i in range(2)]
        qk_turned = sem("qk_turned")
        q_ready = sem("q_ready")
        k_ready = sem("k_ready")
        scores_done = sem("scores_done")
        scores_masked = sem("scores_masked")
        negmax_ready = sem("negmax_ready")
        exps_ready = sem("exps_ready")
        second_recip = sem("second_recip")
        weight_ready = sem("weight_ready")
        probs_ready = sem("probs_ready")
        probs_combined = sem("probs_combined")
        probs_turned = sem("probs_turned")
        probs_out = sem("probs_out")
        values_done = sem("values_done")
        outputs_hi = sem("outputs_hi")
        outputs_lo = sem("outputs_lo")
        head_squares_ready = sem("head_squares_ready")
        head_squares_summed = sem("head_squares_summed")
        head_roots = sem("head_roots")
        head_recips = sem("head_recips")
        head_scaled = sem("head_scaled")
        attn_hi = sem("attn_hi")
        attn_lo = sem("attn_lo")
        state_loaded = sem("state_loaded")
        state_turned = sem("state_turned")
        state_ready = sem("state_ready")
        pads_zeroed = sem("pads_zeroed")
        levels_done = sem("levels_done")
        corr_loaded = sem("corr_loaded")
        pooled = sem("pooled")
        pooled_hi = sem("pooled_hi")
        pooled_lo = sem("pooled_lo")
        out_turned = sem("out_turned")
        out_rows_ready = sem("out_rows_ready")
        out_stored = [sem(f"out_stored{i}") for i in range(3)]
        state_stored = sem("state_stored")
        last_rows_turned = sem("last_rows_turned")
        last_rows_ready = sem("last_rows_ready")
        last_rows_out = sem("last_rows_out")

        block = st.enter_context(nc.Block())

        FFN_U = (4, 38)
        FFN_A = (24, 312)
        GU_PER = 2 * NC
        FFN_G = (0, PAIRS * GU_PER)
        ADD_PER = KD * NC

        def unit_src(kind, layer, b):
            if kind == "out":
                return d["w_out"][0].rearrange("(k p) n -> p k n", p=P)[:, :, b * 256:(b + 1) * 256]
            if kind == "gate":
                return d["w_gate"][layer].rearrange("(k p) n -> p k n", p=P)[:, :, bass.ts(b, 256)]
            if kind == "up":
                return d["w_up"][layer].rearrange("(k p) n -> p k n", p=P)[:, :, bass.ts(b, 256)]
            if kind == "down":
                return d["w_down"][layer].rearrange("(b j p) n -> b p j n", p=P, j=2)[b]
            return d["pool_w"][0].rearrange("g (k p) n -> p (g k) n", p=P)

        def unit_of(layer, kind, b):
            u = FFN_U[layer]
            if isinstance(b, int) and b == 0 and kind != "down":
                return u + (kind == "up")
            if isinstance(b, int) and b == PAIRS - 1 and kind == "down":
                return u + 3 * PAIRS - 1
            return b * 3 + (u + {"gate": -1, "up": 0, "down": 4}[kind])

        def raw_slot(layer, kind, b, par):
            return (par + (kind == "gate")) % 2 if not isinstance(b, int) else unit_of(layer, kind, b) % 2

        HILO = (0, 1, 3)
        GAIN = (0, 16, 8, 24, 32)
        AFTER = (None, 0, 264, 288, 552)
        XF0 = (0, 24, 48, 80, 104)
        SQUARES, FOLDS = KD - 1 + NC, KD - 2 + NC

        ROPE0 = {0: 0, 1: 9, 3: 18, 4: 27}

        def T2(par, n):
            return ps[:, 2 * par:2 * par + 2].rearrange("p a (k n) -> p (a k) n", n=P)[:, :, 0:n]

        def R2(par, n):
            return ps[0:n, 2 * par:2 * par + 2].rearrange("p a n -> p (a n)")

        def b_chunk(w):
            c, hd = divmod(w, 4)
            if c == 2:
                return osam[:, 1, hd], NS, S
            return ob[:, hd, c * 512:(c + 1) * 512], 512, c * 512

        def raw_count(n, slot):
            return 16 * (n // 2 + 1) if isinstance(n, int) else n * 8 + (8 if slot else 16)

        def number(pair):
            mix, it, half = pair
            return it * 2 + (mix * 4 + half)

        def groups_before(pair):
            mix, it, half = pair
            return (it * 2 + half) * (12 if mix else 24) + (96 if mix else 0)

        def groups_through(mix, w):
            return sum((x // 2 + 4) // 4 for x in range(w + 1) if x % 2 or not mix)

        def prompt_loop(eng, start, body):
            start((0, 0, 0))
            with eng.Fori(0, 2) as it:
                body((0, it, 0), (0, it, 1), 16)
                body((0, it, 1), (0, it + 1, 0), it * 16 + 16)
            for it in range(2):
                body((1, it, 0), (1, it, 1), 32)
                body((1, it, 1), (1, 1, 0) if it == 0 else None, 32)

        def prompt_dve(dve):
            tt, ts, stt = dve.tensor_tensor, dve.tensor_scalar, dve.scalar_tensor_tensor

            def masked(pair, v, turned):
                u = number(pair) * 16 + v
                n = P * (v // 2 + 1)
                dve.wait_ge(scores_done, u + 1)
                if turned is not None:
                    dve.wait_ge(probs_turned, turned)
                dve.memset(small[:, 11:12], 0.0)
                st_ = pstat[:, v % RING]
                dve.tensor_tensor_reduce(sm[:, v % RING, 0:n], ps[:, 2 * (v % 2):2 * (v % 2) + 2].rearrange("p a n -> p (a n)")[:, 0:n],
                                         pmask[:, S - n:S], 1.0, -3.0e38, ALU.add, ALU.max, st_[:, 0:1]).then_inc(scores_masked, 1)
                dve.wait_ge(scores_masked, u + 1)
                ts(st_[:, 1:2], st_[:, 0:1], -0.125, None, ALU.mult).then_inc(negmax_ready, 1)

            def weight(pair, w):
                mix, it, half = pair
                u = number(pair) * 16 + w
                st_ = pstat[:, w % RING]
                dve.wait_ge(exps_ready, u + 1)
                if mix and w % 2:
                    dve.reciprocal(st_[:, 0:1], st_[:, 2:3]).then_inc(second_recip, 1)
                    dve.wait_ge(second_recip, (it * 2 + half) * 8 + (w // 2 + 1))
                    ts(st_[:, 3:4], st_[:, 0:1], small[:, 6:7], None, ALU.mult).then_inc(weight_ready, 1)
                    dve.wait_ge(weight_ready, u + 1)
                    dve.wait_ge(probs_ready, (it * 2 + half) * 8 + (64 + w // 2 + 1))
                    n = P * (w // 2 + 1)
                    first = sm[:, (w - 1) % RING, 0:n]
                    stt(first, sm[:, w % RING, 0:n], st_[:, 3:4], first, ALU.mult, ALU.add).then_inc(probs_combined, 1)
                else:
                    dve.reciprocal(st_[:, 3:4], st_[:, 2:3]).then_inc(weight_ready, 1)

            def gather(pair, w):
                mix, it, half = pair
                if mix and w % 2 == 0:
                    return
                jj, t0 = number(pair), groups_before(pair)
                i, s = w // 2, 0 if mix else w % 2
                if w == mix:
                    dve.wait_ge(values_done, jj * 2)
                if w == 8 + mix:
                    dve.wait_ge(values_done, jj * 2 + 1)
                t = groups_through(mix, w - 1)
                for k0 in range(0, i + 1, 4):
                    cnt = min(4, i + 1 - k0)
                    dve.wait_ge(probs_turned, t0 + (t + 1))
                    dve.tensor_copy(pT[:, s, k0:k0 + cnt, (i % 4) * P:(i % 4) * P + P],
                                    ps[:, 4 + t % 2, 0:cnt * P].rearrange("p (k n) -> p k n", n=P)).then_inc(probs_out, 1)
                    t += 1

            def low(pair, g):
                mix, it, half = pair
                if mix == 0:
                    dve.wait_ge(outputs_hi, number(pair) * 2 + (g + 1))
                    o = xn[:, bass.ds(it * 2 + half, 1), :, g * 512:(g + 1) * 512].rearrange("p a q n -> p (a q) n")
                    tt(o[:, 1], ps[:, 6 + g], o[:, 0].bitcast(F32), ALU.subtract).then_inc(outputs_lo, 1)

            def k_out(pair):
                for r in range(2):
                    dve.wait_ge(qk_turned, number(pair) * 4 + (r + 3))
                    dve.tensor_copy(kT[:, r * 512:(r + 1) * 512], ps[:, 6 + r]).then_inc(k_ready, 1)

            def start(pair):
                k_out(pair)
                dve.wait_ge(mask_loaded, 16)
                for v in range(LAG):
                    masked(pair, v, None)
                    if v == 1:
                        weight(pair, 0)

            def body(pair, nxt, masks):
                mix, t0 = pair[0], groups_before(pair)
                weight(pair, 1)
                for v in range(LAG, 16):
                    masked(pair, v, t0 if v < RING else t0 + groups_through(mix, v - RING + int(mix and v % 2 == 0)))
                    weight(pair, v - 1)
                    gather(pair, v - LAG)
                    if v == 14:
                        low(pair, 0)
                if nxt:
                    k_out(nxt)
                weight(pair, 15)
                if nxt:
                    dve.wait_ge(mask_loaded, masks)
                for v in range(LAG):
                    gather(pair, 16 - LAG + v)
                    if nxt:
                        masked(nxt, v, t0 + groups_through(mix, v + 16 - RING + int(mix and v % 2 == 0)))
                    if nxt and v == 1:
                        weight(nxt, 0)
                low(pair, 1)

            prompt_loop(dve, start, body)

        def prompt_act(act):
            def q_out(pair):
                for r in range(2):
                    act.wait_ge(qk_turned, number(pair) * 4 + (r + 1))
                    act.activation(qT[:, r * 512:(r + 1) * 512], ps[:, 6 + r], ACT.Copy).then_inc(q_ready, 1)

            def exponentials(pair, v):
                n = P * (v // 2 + 1)
                act.wait_ge(negmax_ready, number(pair) * 16 + (v + 1))
                act.activation(sm[:, v % RING, 0:n], sm[:, v % RING, 0:n], ACT.Exp, bias=pstat[:, v % RING, 1:2],
                               scale=0.125, accum_out=pstat[:, v % RING, 2:3]).then_inc(exps_ready, 1)

            def out(pair, g):
                mix, it, half = pair
                act.wait_ge(values_done, number(pair) * 2 + (g + 1))
                dst = (ob[:, bass.ds(it * 2 + half, 1), g * 512:(g + 1) * 512] if mix else
                       xn[:, bass.ds(it * 2 + half, 1), 0, g * 512:(g + 1) * 512])
                act.activation(dst.rearrange("p a n -> p (a n)"), ps[:, 6 + g], ACT.Copy).then_inc(outputs_hi, 1)

            def start(pair):
                q_out(pair)
                for v in range(LAG):
                    exponentials(pair, v)

            def body(pair, nxt, masks):
                for v in range(LAG, 16):
                    exponentials(pair, v)
                    if v == 12 + pair[0]:
                        out(pair, 0)
                    if v == 14 and nxt:
                        q_out(nxt)
                if nxt:
                    for v in range(LAG):
                        exponentials(nxt, v)
                out(pair, 1)

            prompt_loop(act, start, body)

        def prompt_pe(pe):
            mm = pe.matmul

            def turn_qk(pair, rs, before=None):
                mix, it, half = pair
                jj = number(pair)
                for r in rs:
                    if r == 0:
                        pe.wait_ge(qkv_loaded[half], it * 48 + (48 + 96 * mix))
                        if before is not None:
                            pe.wait_ge(outputs_hi, jj * 2 - 1)
                            pe.wait_ge(outputs_lo, 8 if before else jj * 2 - 1)
                    if r >= 2:
                        pe.wait_ge(q_ready, jj * 2 + (r - 1))
                    for i in range(4):
                        q_ = pe.transpose(ps[:, 6 + r % 2, i * P:(i + 1) * P], qkv[:, half, r // 2, 4 * (r % 2) + i], ident[:])
                    q_.then_inc(qk_turned, 1)

            def scores(pair, v, first=False):
                jj = number(pair)
                i, s = v // 2, v % 2
                n = P * (i + 1)
                if v == 0:
                    pe.wait_ge(q_ready, jj * 2 + 2)
                    pe.wait_ge(k_ready, jj * 2 + 2)
                if not first:
                    pe.wait_ge(scores_masked, jj * 16 + (v - 1))
                h64 = slice(64 * s, 64 * s + 64)
                for a in range(0, n, 512):
                    w = min(512, n - a)
                    q_ = mm(ps[:, 2 * s + a // 512, 0:w], qT[h64, i * P:(i + 1) * P], kT[h64, a:a + w], start=True, stop=True)
                q_.then_inc(scores_done, 1)

            def turn_p(pair, w):
                mix, it, half = pair
                if mix and w % 2 == 0:
                    return
                i, t0, t = w // 2, groups_before(pair), groups_through(mix, w - 1)
                if mix:
                    pe.wait_ge(probs_combined, (it * 2 + half) * 8 + (i + 1))
                else:
                    pe.wait_ge(probs_ready, number(pair) * 16 + (w + 1))
                src = sm[:, (w - mix) % RING]
                for k0 in range(0, i + 1, 4):
                    cnt = min(4, i + 1 - k0)
                    if t >= 2:
                        pe.wait_ge(probs_out, t0 + (t - 1))
                    else:
                        pe.wait_ge(probs_out, t0)
                    for k in range(k0, k0 + cnt):
                        q_ = pe.transpose(ps[:, 4 + t % 2, (k - k0) * P:(k - k0 + 1) * P], src[:, k * P:(k + 1) * P], ident[:])
                    q_.then_inc(probs_turned, 1)
                    t += 1

            def values(pair, g, more=False):
                mix, it, half = pair
                jj = number(pair)
                pe.wait_ge(outputs_hi, jj * 2)
                pe.wait_ge(outputs_lo, 8 if mix else jj * 2)
                pe.wait_ge(k_ready, jj * 2 + (4 if more else 2))
                pe.wait_ge(probs_out, groups_before(pair) + groups_through(mix, 7 + 8 * g))
                nk = 4 * (g + 1)
                for kt in range(nk):
                    q0 = max(0, kt - 4 * g) * P
                    for s in range(1 if mix else 2):
                        rows = slice(0, P) if mix else slice(64 * s, 64 * s + 64)
                        q_ = mm(ps[rows, 6 + g, q0:512], qkv[:, half, 2, kt, rows], pT[:, s, kt, q0:512],
                                start=(kt == 0), stop=(kt == nk - 1))
                q_.then_inc(values_done, 1)

            def start(pair):
                turn_qk(pair, range(4))
                for v in range(LAG):
                    scores(pair, v, v < 2)

            def body(pair, nxt, masks):
                mix = pair[0]
                for v in range(LAG, 16):
                    scores(pair, v)
                    if v == 8 + LAG + mix:
                        values(pair, 0)
                    if v == 15 and nxt:
                        turn_qk(nxt, (0, 1), mix)
                    turn_p(pair, v - LAG)
                if nxt:
                    turn_qk(nxt, (2, 3))
                for v in range(LAG):
                    turn_p(pair, 16 - LAG + v)
                    if nxt:
                        scores(nxt, v)
                values(pair, 1, nxt is not None)

            prompt_loop(pe, start, body)

        def TK(j):
            return ps[:, 4 + j % 2].rearrange("p (k n) -> p k n", n=P)

        def sample_cols(row):
            if len(row.shape) == 3:
                return row[:, :, 16 + S:PADW].rearrange("p k (b t) -> p k b t", t=24)
            return row[:, 16 + S:PADW].rearrange("p (b t) -> p b t", t=24)

        def by_sample(row):
            return row.rearrange("p (b t) -> p b t", t=T)

        KINDS = ("gate", "up", "down")
        TWOS = (PAIRS - 1) // 2

        @block.sync
        def _(sp):
            sp.dma_start(ident[:], const("ident")).then_inc(consts_loaded, 16)
            for i in range(9):
                n = P if i < 8 else NS
                if i >= 3:
                    sp.wait_ge(input_transposed, i - 2)
                src = d["x_prompt"][0, i * P:(i + 1) * P] if i < 8 else d["x_sample"].rearrange("b t n -> (b t) n")
                sp.dma_start(xin[0:n, i % 3], src).then_inc(input_rows_loaded[i % 3], 16)
                if i == 1:
                    for name, r0, rows in (("ln_mix", 0, 16), ("ln_ffn", 16, 16), ("ln_final", 32, 8), ("pool_scale", 40, 8),
                                           ("subln_g", 48, 1)):
                        src = d[name] if name == "ln_final" else d[name].rearrange("l n -> (l n)")
                        sp.dma_start(grow[r0:r0 + rows], src.rearrange("(k p) -> k p", p=P)).then_inc(consts_loaded, 16)
                    for j, name in enumerate(("lambda_q1", "lambda_k1", "lambda_q2", "lambda_k2")):
                        sp.dma_start(lamrow[:, j], d[name]).then_inc(consts_loaded, 16)

            w_in = d["w_in"][0].rearrange("(k p) n -> p k n", p=P)
            for m in range(12):
                g, half = divmod(m, 2)
                if m >= 2:
                    sp.wait_ge(proj_w_lo, m - 1)
                sp.dma_start(wpraw[:, m % 2], w_in[:, 4 * half:4 * half + 4, g * 512:(g + 1) * 512]).then_inc(proj_w_loaded[m % 2], 16)
                if m == 1:
                    sp.wait_ge(norm_lo, 24)
                    sp.wait_ge(norm_hi, 24)
                    sp.dma_start(cs[:], const("cs").rearrange("p (i c) -> p i c", i=9)).then_inc(rotary_loaded, 16)

            def load_window(b, raw, name, s):
                sp.dma_start(raw[0][:], d[name][0, b].rearrange("(p j) h n -> p j (h n)", j=8)).then_inc(s[0], 16)

            def load_pages(pages, raw, name, s):
                for j, page in enumerate(pages):
                    sp.dma_start(raw[1][:, j], d[name][0, bass.ds(page, 1)].rearrange("a p h n -> p (a h n)")).then_inc(s[1], 16)

            def page_numbers(b):
                return [sp.value_load(ptab[0:1, bass.ds(b * NPAGE + j, 1)], min_val=0, max_val=NPHYS - 1) for j in range(NPAGE)]

            sp.dma_start(ptab[:], d["page_table"].rearrange("b n -> (b n)").rearrange("(a n) -> a n", a=1)).then_inc(page_table_loaded, 16)
            sp.wait_ge(proj_done, 45)
            load_window(0, kraw, "cache_win_k_a", dec_k_loaded)
            load_window(0, vraw, "cache_win_v_a", dec_v_loaded)
            sp.wait_ge(page_table_loaded, 16)
            pages = page_numbers(0)
            sp.wait_ge(proj_rows, 54)
            sp.wait_ge(rows_rotated, 36)
            for name, dst in (("decA", dmask[:, 0, 0:PAST]), ("newA", dnew[:, 0]), ("newB", dnew[:, 1]), ("comb0", comb[:, 0]),
                              ("comb1", comb[:, 1])):
                sp.dma_start(dst, const(name)).then_inc(dec_tables_loaded, 16)
            load_pages(pages, kraw, "cache_k_b", dec_k_loaded)
            load_pages(pages, vraw, "cache_v_b", dec_v_loaded)
            turned, used = (sp.alloc_register(n) for n in ("turned", "used"))
            for r in (turned, used):
                sp.reg_mov(r, 0)
            with sp.Fori(0, DB - 1) as b:
                pages = page_numbers(b + 1)
                for paged, names in enumerate((("cache_win_k_a", "cache_win_v_a"), ("cache_k_b", "cache_v_b"))):
                    sp.reg_add(turned, turned, 8)
                    sp.reg_add(used, used, 1)
                    n_turned, n_used = (sp.snap(r) for r in (turned, used))
                    for raw, name, s, done, n in ((kraw, names[0], dec_k_loaded, dec_k_turned, n_turned), (vraw, names[1], dec_v_loaded, dec_values_done, n_used)):
                        sp.wait_ge(done, n)
                        if paged:
                            load_pages(pages, raw, name, s)
                        else:
                            load_window(b + 1, raw, name, s)

            sp.wait_ge(sample_rows_stored, 16 * (2 + 2 * DB))
            sp.wait_ge(dec_values_done, 2 * DB - 1)
            sp.wait_ge(dec_k_turned, 8 * (2 * DB - 1))
            for slot in rows_stored:
                sp.wait_ge(slot, 16 * 6 * NTILE // 3)
            for mix in range(2):
                kn, vn = ("o_kb_p", "o_vb_p") if mix else ("o_wk_p", "o_wv_p")
                srcs = (qs_dram[mix].rearrange("(i p) n -> p i n", p=P),
                        d[kn][0, 0].rearrange("(i p) h n -> p i (h n)", p=P),
                        d[vn][0, 0].rearrange("(i p) h n -> p i (h n)", p=P))
                for j in range(4):
                    if 4 * mix + j >= 2:
                        sp.wait_ge(values_done, 2 * (4 * mix + j - 1))
                    for a in range(3):
                        sp.dma_start(qkv[:, j % 2, a], srcs[a][:, :, j * P:(j + 1) * P]).then_inc(qkv_loaded[j % 2], 16)
                    if j == 0:
                        if mix:
                            sp.wait_ge(scores_masked, 64)
                        else:
                            sp.wait_ge(dec_stored, 2 * DB)
                        sp.dma_start(pmask[:], const("maskB" if mix else "maskA")).then_inc(mask_loaded, 16)

            sp.wait_ge(values_done, 16)

            def load(kind, layer, b, n, slot):
                if not (isinstance(n, int) and n < 2):
                    sp.wait_ge(unit_lo, n - 1)
                k = {"down": 2, "pool": 8}.get(kind, 8)
                sp.dma_start(wraw[:, slot].rearrange("p (k n) -> p k n", k=k), unit_src(kind, layer, b)).then_inc(unit_loaded[slot], 16)

            for u in range(4):
                load("out", 0, u, u, u % 2)
            for layer in range(2):
                def block_loads(layer, b, kinds, par=0):
                    for kind in kinds:
                        load(kind, layer, b, unit_of(layer, kind, b), raw_slot(layer, kind, b, par))

                block_loads(layer, 0, ("gate", "up"))
                with sp.Fori(0, (PAIRS - 1) // 2) as i:
                    block_loads(layer, i * 2 + 1, ("gate", "up"), 1)
                    block_loads(layer, i * 2, ("down",), 0)
                    block_loads(layer, i * 2 + 2, ("gate", "up"), 0)
                    block_loads(layer, i * 2 + 1, ("down",), 1)
                block_loads(layer, PAIRS - 1, ("down",))
                if layer == 0:
                    load("pool", 0, 0, 37, 1)
                    sp.wait_ge(group_done, FFN_A[0] + PAIRS * ADD_PER)
                    sp.dma_start(corr[:], const("corr").rearrange("p (g n) -> p g n", g=4)).then_inc(corr_loaded, 16)
                    sp.dma_start(stin[:], d["state_pool"][0].rearrange("b t n -> (b t) n")).then_inc(state_loaded, 16)

        @block.gpsimd
        def _(pool):
            for g in range(6):
                rot = ROPE0.get(g)
                for i in range(8):
                    t = g * 8 + i
                    if rot is None:
                        pool.wait_ge(proj_rows, g * 9 + i + 1)
                    else:
                        pool.wait_ge(rows_rotated, rot + i + 1)
                    dst = (qs_dram[g // 3, i * P:(i + 1) * P] if g % 3 == 0 else
                           d[{1: "o_wk_p", 2: "o_wv_p", 4: "o_kb_p", 5: "o_vb_p"}[g]][0, 0, i * P:(i + 1) * P]
                           .rearrange("t h n -> t (h n)"))
                    pool.dma_start(dst, tok[:, t % 3]).then_inc(rows_stored[t % 3], 16)
                if rot is None:
                    pool.wait_ge(proj_rows, g * 9 + 9)
                else:
                    pool.wait_ge(rows_rotated, rot + 9)
                if g in (4, 5):
                    dst = d["o_kb_s" if g == 4 else "o_vb_s"][0].rearrange("b t h n -> (b t) (h n)")
                    pool.dma_start(dst, toks[:, g]).then_inc(sample_rows_stored, 16)
                if g in (1, 2):
                    dst = d["o_wk_s" if g == 1 else "o_wv_s"][0].rearrange("b t h n -> b t (h n)")
                    for b in range(DB):
                        pool.dma_start(dst[b, PAST - T:PAST], toks[b * T:(b + 1) * T, g]).then_inc(sample_rows_stored, 16)

            pool.wait_ge(sample_rows_stored, 16 * (2 + 2 * DB))

            def move_window(b):
                for src, dst in (("cache_win_k_a", "o_wk_s"), ("cache_win_v_a", "o_wv_s")):
                    a, o = (d[n][0, bass.ds(b, 1)].rearrange("a t h n -> (a t) (h n)") for n in (src, dst))
                    pool.dma_start(o[0:PAST - T], a[T:PAST]).then_inc(windows_moved, 16)

            for mix in range(2):
                with pool.Fori(0, 2) as it:
                    for half in range(2):
                        for v in range(16):
                            if v == 6:
                                pool.wait_ge(mask_loaded, 16)
                                move_window(it * 2 + (mix * 4 + half))
                            if mix and v % 2:
                                continue
                            u = it * 32 + (mix * 64 + half * 16 + v)
                            n = P * (v // 2 + 1)
                            pool.wait_ge(weight_ready, u + 1)
                            buf = sm[:, v % RING, 0:n]
                            pool.tensor_tensor(buf, buf, pstat[:, v % RING, 3:4].to_broadcast([P, n]), ALU.mult).then_inc(probs_ready, 1)

            pool.wait_ge(windows_moved, 32 * DB)

            pool.wait_ge(group_done, FFN_A[0] + PAIRS * ADD_PER)
            pool.memset(yp[:, :, 0:16], 0.0).then_inc(pads_zeroed, 1)
            pool.memset(sample_cols(yp[:])[:, :, :, 0:1], 0.0).then_inc(pads_zeroed, 1)
            pool.wait_ge(last_rows_out, 2)
            pool.dma_start(d["o_pl_p"][0, 0], prow[0:STATE, 0]).then_inc(state_stored, 16)
            pool.dma_start(d["o_pl_s"][0].rearrange("b t n -> (b t) n"), prow[0:DB * STATE, 1]).then_inc(state_stored, 16)
            pool.wait_ge(state_stored, 32)

            for i in range(9):
                n = P if i < 8 else NS
                pool.wait_ge(out_rows_ready, i + 1)
                dst = d["o_y_p"][0, i * P:(i + 1) * P] if i < 8 else d["o_y_s"].rearrange("b t n -> (b t) n")
                pool.dma_start(dst, yrow[0:n, i % 3]).then_inc(out_stored[i % 3], 16)
            for i in range(3):
                pool.wait_ge(out_stored[i], 48)

        @block.scalar
        def _(act):
            for i in range(9):
                n = P if i < 8 else NS
                act.wait_ge(input_transposed, i + 1)
                act.activation(x[:, :, i * P:i * P + n], T2(i % 2, n), ACT.Copy).then_inc(x_ready, 1)
            act.wait_ge(lambda_dots, 2)
            act.activation(small[0:1, 2:4], small[0:1, 0:2], ACT.Exp).then_inc(lambda_exps, 1)

            def square(r, k):
                for c, (c0, cn) in enumerate(CH if k == KD - 1 else ((0, NT),)):
                    if r == 0:
                        act.wait_ge(x_ready, 9)
                    else:
                        act.wait_ge(group_added, AFTER[r] + NC * k + (c + 1 if k == KD - 1 else NC))
                    if k >= 3:
                        act.wait_ge(squares_added, FOLDS * r + k - 2)
                    dst = sq[:, k % 2, c0:c0 + cn] if k else rstd[:]
                    act.activation(dst, x[:, k, c0:c0 + cn], ACT.Square).then_inc(squares_ready, 1)

            def norm(r, between=None, done=0, later=None):
                if r:
                    act.wait_ge(norm_pieces, XF0[r])
                for k in range(done, KD):
                    square(r, k)
                for c, (c0, cn) in enumerate(CH):
                    act.wait_ge(squares_summed, NC * r + c + 1)
                    act.activation(rstd[:, c0:c0 + cn], ps[:, c, 0:cn], ACT.Sqrt, bias=small[:, 8:9], scale=1.0 / D).then_inc(roots_ready, 1)
                if between:
                    between()
                if r in HILO:
                    for c, (c0, cn) in enumerate(CH):
                        for k in range(KD):
                            f = c * KD + k
                            act.wait_ge(norm_pieces, XF0[r] + f + 1)
                            act.activation(xn[:, k, 0, c0:c0 + cn], xf[:, f % 4, 0:cn], ACT.Copy).then_inc(norm_hi, 1)
                        if c == 0 and later:
                            later()

            def proj_hi(m):
                g, half = divmod(m, 2)
                act.wait_ge(proj_w_loaded[m % 2], 16 * (m // 2 + 1))
                if g >= 2:
                    act.wait_ge(proj_done, 9 * (g - 1))
                act.activation(wp[:, g % 2, 0, 4 * half:4 * half + 4], wpraw[:, m % 2], ACT.Copy).then_inc(proj_w_hi, 1)

            norm(0, lambda: (proj_hi(0), proj_hi(1)))
            for m in range(2, 4):
                proj_hi(m)
            for g in range(6):
                for i in range(9):
                    n = P if i < 8 else NS
                    m = g * 9 + i
                    act.wait_ge(proj_done, m + 1)
                    if i < 8:
                        t = g * 8 + i
                        if t >= 3:
                            act.wait_ge(rows_stored[t % 3], 16 * (t // 3))
                        act.activation(tok[:, t % 3], ps[:, m % 8], ACT.Copy).then_inc(proj_rows, 1)
                    else:
                        act.activation(toks[:, g], ps[0:NS, m % 8], ACT.Copy).then_inc(proj_rows, 1)
                if g + 2 < 6:
                    proj_hi(2 * g + 4)
                    proj_hi(2 * g + 5)

            def dec_evac(tr):
                for j in range(0, 8, 2):
                    act.wait_ge(dec_k_turned, tr + j + 1)
                    act.activation(dkT[:, :, j * P:(j + 1) * P], TK(j), ACT.Copy).then_inc(dec_k_even, 1)

            def out_rows(dd):
                act.wait_ge(dec_values_done, dd + 1)
                act.activation(dom[:], ps[:, 3, 0:P], ACT.Copy).then_inc(dec_rows_out, 1)

            def to_osam(b, m):
                act.wait_ge(dec_combined, b * 2 + (m + 1))
                act.activation(osam[:, m, :, bass.ds(b * T, T)], ps[:, 3, 256:288].rearrange("p (j t) -> p j t", t=T),
                               ACT.Copy).then_inc(dec_stored, 1)

            def dec_act(b, m, last=False):
                dd = b * 2 + m
                first = isinstance(dd, int) and dd == 0
                act.wait_ge(dec_negmax, dd + 1)
                act.activation(dse[:, m], dse[:, m], ACT.Exp, bias=dstat[:, m, 1:2], scale=0.125,
                               accum_out=dstat[:, m, 2:3]).then_inc(dec_exps, 1)
                if not first:
                    out_rows(b * 2 + (m - 1))
                if not last:
                    act.wait_ge(dec_scores_done, dd + 1)
                    dec_evac(dd * 8 + 8)
                if not first:
                    to_osam(*((b, 0) if m else (b - 1, 1)))

            dec_evac(0)
            dec_act(0, 0)
            dec_act(0, 1)
            with act.Fori(1, DB - 1) as b:
                dec_act(b, 0)
                dec_act(b, 1)
            dec_act(DB - 1, 0)
            dec_act(DB - 1, 1, True)
            out_rows(2 * DB - 1)
            to_osam(DB - 1, 1)

            prompt_act(act)
            act.activation(xn[:, 0:4, 0, S:NT], osam[:, 0], ACT.Copy).then_inc(attn_hi, 1)
            def hi(n, slot, dst):
                act.wait_ge(unit_loaded[slot], raw_count(n, slot))
                act.activation(dst[:, 0], wraw[:, slot], ACT.Copy).then_inc(unit_hi, 1)

            for w in range(14):
                if w < 12:
                    if w >= 2:
                        act.wait_ge(head_squares_summed, w - 1)
                    src, n, _ = b_chunk(w)
                    act.wait_ge(outputs_hi, 16)
                    act.activation(osq[:, w % 2, 0:n], src, ACT.Square).then_inc(head_squares_ready, 1)
                if 1 <= w < 13:
                    src, n, _ = b_chunk(w - 1)
                    act.wait_ge(head_squares_summed, w)
                    if w >= 5:
                        act.wait_ge(head_scaled, w - 4)
                    act.activation(orms[:, (w - 1) % 4, 0:n], ps[:, (w - 1) % 2, 0:n], ACT.Sqrt, bias=small[:, 9:10],
                                   scale=1.0 / P).then_inc(head_roots, 1)
                if w >= 2:
                    src, n, t0 = b_chunk(w - 2)
                    act.wait_ge(head_scaled, w - 1)
                    act.activation(xn[:, 4 + (w - 2) % 4, 0, t0:t0 + n], src, ACT.Copy).then_inc(attn_hi, 1)
                if w in (5, 9):
                    hi(w // 4 - 1, w // 4 - 1, ws[w // 4 - 1])

            def ffn_hi(layer, b, kinds, par=0):
                for kind in kinds:
                    if kind == "down":
                        act.wait_ge(group_done, b * ADD_PER + FFN_A[layer])
                    elif isinstance(b, int) and b == 0:
                        act.wait_ge(group_done, FFN_A[layer])
                    else:
                        act.wait_ge(gate_up_done, b * GU_PER + FFN_G[layer])
                    hi(unit_of(layer, kind, b), raw_slot(layer, kind, b, par), ws[KINDS.index(kind)])

            def hidden(layer, b, par):
                g0 = b * GU_PER + FFN_G[layer]
                first = isinstance(b, int) and b == 0
                act.wait_ge(group_done, FFN_A[layer] if first else b * ADD_PER + (FFN_A[layer] - ADD_PER))
                for n in range(GU_PER + 1):
                    if n < GU_PER:
                        act.wait_ge(gate_up_done, g0 + (n + 1))
                        if not (first and layer == 0 and n < 2):
                            act.wait_ge(hidden_ready, g0 + (n - 1))
                        cn = CH[n % NC][1]
                        act.activation(act_s[:, n % 2, 0:cn], ps[:, 2 * (n % 2), 0:cn], ACT.Silu).then_inc(silu_ready, 1)
                    if n >= 1:
                        j, c = divmod(n - 1, NC)
                        c0, cn = CH[c]
                        act.wait_ge(hidden_ready, g0 + n)
                        act.activation(hh[:, par, j, 0, c0:c0 + cn], act_h[:, (n - 1) % 2, 0:cn], ACT.Copy).then_inc(hidden_hi, 1)
                    if n == 2 and not first:
                        ffn_hi(layer, b - 1, ("down",), 1 - par)

            def ffn(layer):
                def two(i, last):
                    hidden(layer, i * 2 + 1, 1)
                    ffn_hi(layer, i * 2 + 2, ("gate", "up"), 0)
                    hidden(layer, i * 2 + 2, 0)
                    if not last:
                        ffn_hi(layer, i * 2 + 3, ("gate", "up"), 1)
                norm(1 + 2 * layer, lambda: ffn_hi(layer, 0, ("gate",)), 3 * layer, lambda: ffn_hi(layer, 0, ("up",)))
                act.wait_ge(norm_lo, 24 * (2 + layer))
                if layer == 1:
                    act.wait_ge(state_stored, 32)
                hidden(layer, 0, 0)
                ffn_hi(layer, 1, ("gate", "up"))
                with act.Fori(0, TWOS - 1) as i:
                    two(i, False)
                two(TWOS - 1, True)
                ffn_hi(layer, PAIRS - 1, ("down",))

            for u in range(2, 4):
                if u == 3:
                    act.wait_ge(group_done, 6)
                hi(u, u % 2, ws[u % 3])
            ffn(0)
            act.wait_ge(gate_up_done, FFN_G[1])
            hi(37, 1, ws[0])
            def state_rows():
                act.wait_ge(state_turned, 1)
                for k in range(KD):
                    src = ps[:, 4 + k // 4, (k % 4) * P:(k % 4) * P + DB * STATE]
                    act.activation(sample_cols(yp[:, k])[:, :, 1:16], src.rearrange("p (b t) -> p b t", t=STATE), ACT.Copy).then_inc(state_ready, 1)

            norm(2, state_rows)
            act.wait_ge(state_ready, 8)
            act.wait_ge(norm_pieces, XF0[3])
            act.activation(pcomp[:, :, 0:STATE], yp[:, :, 1 + S:16 + S], ACT.Copy)
            for k in range(KD):
                act.activation(pcomp[:, k, STATE:].rearrange("p (b t) -> p b t", t=STATE), sample_cols(yp[:, k])[:, :, 9:24],
                               ACT.Copy).then_inc(last_rows_ready, 1)
            for k in range(KD):
                act.wait_ge(pooled, k + 1)
                act.activation(xn[:, k, 0], pf[k % 2][:], ACT.Copy).then_inc(pooled_hi, 1)
                if k == 5:
                    act.wait_ge(last_rows_turned, 1)
                    square(3, 0)
                    square(3, 1)
                if k == 6:
                    square(3, 2)
            act.wait_ge(last_rows_turned, 1)
            act.activation(prow[0:STATE, 0], R2(0, STATE), ACT.Copy).then_inc(last_rows_out, 1)
            act.activation(prow[0:DB * STATE, 1], R2(1, DB * STATE), ACT.Copy).then_inc(last_rows_out, 1)
            ffn(1)
            norm(4)
            for i in range(9):
                n = P if i < 8 else NS
                act.wait_ge(out_turned, i + 1)
                if i >= 3:
                    act.wait_ge(out_stored[i % 3], 16 * (i // 3))
                act.activation(yrow[0:n, i % 3], R2(i % 2, n), ACT.Copy).then_inc(out_rows_ready, 1)

        @block.vector
        def _(dve):
            tt, ts, stt = dve.tensor_tensor, dve.tensor_scalar, dve.scalar_tensor_tensor
            dve.memset(ones[:], 1.0).then_inc(fills_done, 1)
            dve.memset(small[:, 8:9], 1e-6).then_inc(fills_done, 1)
            dve.memset(small[:, 9:10], 1e-5).then_inc(fills_done, 1)
            dve.wait_ge(consts_loaded, 160)
            for j in range(2):
                dve.tensor_tensor_reduce(lamtmp[:, j], lamrow[:, 2 * j], lamrow[:, 2 * j + 1], 1.0, 0.0, ALU.mult, ALU.add,
                                         small[0:1, j:j + 1]).then_inc(lambda_dots, 1)
            dve.wait_ge(gains_transposed, 1)
            dve.tensor_copy(gains[:], ps[:, 6, 0:49]).then_inc(gains_ready, 1)
            dve.wait_ge(lambda_exps, 1)
            tt(small[0:1, 10:11], small[0:1, 2:3], small[0:1, 3:4], ALU.subtract).then_inc(small_ready, 1)
            dve.wait_ge(small_ready, 1)
            ts(small[0:1, 4:5], small[0:1, 10:11], LAM0, None, ALU.add).then_inc(small_ready, 1)
            dve.wait_ge(lambda_broadcast, 1)
            dve.tensor_copy(small[:, 5:6], ps[:, 7, 0:1]).then_inc(small_ready, 1)
            ts(small[:, 6:7], ps[:, 7, 0:1], -1.0, None, ALU.mult).then_inc(small_ready, 1)
            dve.wait_ge(gains_ready, 1)
            ts(small[:, 7:8], gains[:, 48:49], 1.0 - LAM0, None, ALU.mult).then_inc(small_ready, 1)
            dve.wait_ge(small_ready, 5)

            def fold(r, k):
                for c, (c0, cn) in enumerate(CH if k == KD - 1 else ((0, NT),)):
                    dve.wait_ge(squares_ready, SQUARES * r + k + 1 + c)
                    dve.wait_ge(squares_added, FOLDS * r + min(k - 1, KD - 2))
                    tt(rstd[:, c0:c0 + cn], rstd[:, c0:c0 + cn], sq[:, k % 2, c0:c0 + cn], ALU.add).then_inc(squares_added, 1)

            def folds_at(r, idx):
                k, c = divmod(idx, NC)
                if c == NC - 1 and k >= 2:
                    fold(r, k - 1)
                if idx == ADD_PER - 1:
                    fold(r, KD - 1)

            def norm(r, between=None, later=None):
                if r == 0:
                    dve.wait_ge(x_ready, 9)
                    for k in range(1, KD):
                        fold(0, k)
                for c, (c0, cn) in enumerate(CH):
                    dve.wait_ge(roots_ready, NC * r + c + 1)
                    dve.reciprocal(rstd[:, c0:c0 + cn], rstd[:, c0:c0 + cn]).then_inc(rstd_ready, 1)
                if between:
                    between()
                if r == 2:
                    pieces = ((0, 364), (364, 364), (728, 296), (S, NS))
                else:
                    pieces = CH
                h0 = 24 * HILO.index(r) if r in HILO else None

                def low(f):
                    c, k = divmod(f, KD)
                    c0, cn = CH[c]
                    dve.wait_ge(norm_hi, h0 + f + 1)
                    tt(xn[:, k, 1, c0:c0 + cn], xf[:, f % 4, 0:cn], xn[:, k, 0, c0:c0 + cn].bitcast(F32), ALU.subtract).then_inc(norm_lo, 1)

                for c, (c0, cn) in enumerate(pieces):
                    dve.wait_ge(rstd_ready, NC * r + min(c, 2) + 1)
                    for k in range(KD):
                        f = c * KD + k
                        src, rs = x[:, k, c0:c0 + cn], rstd[:, c0:c0 + cn]
                        if r in HILO:
                            dst = xf[:, f % 4, 0:cn]
                            if f >= 4:
                                dve.wait_ge(norm_lo, h0 + f - 3)
                        elif r == 4:
                            dst = yf[:, k, c0:c0 + cn]
                        elif c < 3:
                            dst = yp[:, k, 16 + c0:16 + c0 + cn]
                        else:
                            dst, src, rs = sample_cols(yp[:, k])[:, :, 16:24], by_sample(src), by_sample(rs)
                        stt(dst, src, gains[:, GAIN[r] + k:GAIN[r] + k + 1], rs, ALU.mult, ALU.mult).then_inc(norm_pieces, 1)
                        if r in HILO and f >= 2:
                            low(f - 2)
                        if f == 9 and later:
                            later()
                if r in HILO:
                    low(22)
                    low(23)
                    dve.wait_ge(norm_lo, h0 + 24)

            def proj_lo(m):
                g, half = divmod(m, 2)
                dve.wait_ge(proj_w_hi, m + 1)
                part = wp[:, g % 2, :, 4 * half:4 * half + 4]
                tt(part[:, 1], wpraw[:, m % 2], part[:, 0].bitcast(F32), ALU.subtract).then_inc(proj_w_lo, 1)

            norm(0, lambda: (proj_lo(0), proj_lo(1)))
            for m in range(2, 4):
                proj_lo(m)
            dve.wait_ge(rotary_loaded, 16)
            for g in range(6):
                for i in range(9 if g in ROPE0 else 0):
                    n = P if i < 8 else NS
                    rows = tok[:, (g * 8 + i) % 3] if i < 8 else toks[:, g]
                    c = ROPE0[g] + i
                    r16 = rows.rearrange("p (h c) -> p h c", c=64)[:, :, 0:16]
                    co = rope[0:n, c % 2, 0].rearrange("p (h c) -> p h c", c=16)
                    si = rope[0:n, c % 2, 1].rearrange("p (h c) -> p h c", c=16)
                    dve.wait_ge(proj_rows, g * 9 + i + 1)
                    tt(co, r16, cs[0:n, i:i + 1, 0:16].to_broadcast([n, 8, 16]), ALU.mult).then_inc(rotary_products, 1)
                    tt(si, r16, cs[0:n, i:i + 1, 16:32].to_broadcast([n, 8, 16]), ALU.mult).then_inc(rotary_products, 1)
                    dve.wait_ge(rotary_products, 2 * c + 2)
                    tt(r16[:, :, 0:8], co[:, :, 0:8], si[:, :, 8:16], ALU.subtract)
                    tt(r16[:, :, 8:16], co[:, :, 8:16], si[:, :, 0:8], ALU.add).then_inc(rows_rotated, 1)
                if g + 2 < 6:
                    proj_lo(2 * g + 4)
                    proj_lo(2 * g + 5)

            dve.wait_ge(dec_tables_loaded, 80)
            dve.memset(dmask[:, 1, 0:PAST], 0.0).then_inc(dec_mask_ready, 1)
            dve.memset(qblk[:], 0.0).then_inc(dec_q_zeroed, 1)
            stt(comb[:, 2], comb[:, 1], small[:, 6:7], comb[:, 0], ALU.mult, ALU.add).then_inc(dec_comb_ready, 1)
            dve.wait_ge(dec_q_zeroed, 1)
            dve.wait_ge(dec_qk_turned, 4)
            for m in range(2):
                for jp in range(4):
                    for hf in range(2):
                        h64 = slice(64 * hf, 64 * hf + 64)
                        dve.tensor_copy(qblk[h64, m, :, jp, 8 * hf:8 * hf + 8],
                                        ps[h64, 2 * m, 64 * jp:64 * jp + 64].rearrange("p (b t) -> p b t", t=T)).then_inc(dec_qk_ready, 1)
                dve.tensor_copy(knT[:, m], ps[:, 2 * m + 1, 0:256].rearrange("p (j n) -> p j n", n=NS)).then_inc(dec_qk_ready, 1)
            dve.wait_ge(dec_qk_ready, 18)

            def next_q(b, m):
                dve.tensor_copy(qcur[:, m], qblk[:, m, bass.ds(b, 1)].rearrange("p a j n -> p (a j) n")).then_inc(dec_q_current, 1)
                dve.tensor_copy(dmask[:, m, PAST:PAST + NS], dnew[:, m, bass.ds(b * -8 + 56, NS)]).then_inc(dec_mask_ready, 1)

            def dec_evac(tr):
                for j in range(1, 8, 2):
                    dve.wait_ge(dec_k_turned, tr + j + 1)
                    dve.tensor_copy(dkT[:, :, j * P:(j + 1) * P], TK(j)).then_inc(dec_k_odd, 1)

            def dec_dve(b, m, final):
                dd = b * 2 + m
                dve.wait_ge(dec_scores_done, dd + 1)
                dve.wait_ge(dec_mask_ready, dd + 2)
                dve.memset(small[:, 11:12], 0.0)
                dve.tensor_tensor_reduce(dse[:, m], ps[:, 0:3].rearrange("p a n -> p (a n)")[:, 0:PAST + NS], dmask[:, m], 1.0,
                                         -3.0e38, ALU.add, ALU.max, dstat[:, m, 0:1]).then_inc(dec_masked, 1)
                dve.wait_ge(dec_masked, dd + 1)
                ts(dstat[:, m, 1:2], dstat[:, m, 0:1], -0.125, None, ALU.mult).then_inc(dec_negmax, 1)
                if not final:
                    next_q(b + 1, m)
                if not (final and m):
                    dec_evac(dd * 8 + 8)
                dve.wait_ge(dec_exps, dd + 1)
                dve.reciprocal(dstat[:, m, 3:4], dstat[:, m, 2:3]).then_inc(dec_recip, 1)
                dve.wait_ge(dec_recip, dd + 1)
                mix_w = (dmix[:, 1, 0:32], comb[:, 2]) if m else (dmix[:, 0], comb[:, 0:2].rearrange("p a n -> p (a n)"))
                ts(*mix_w, dstat[:, m, 3:4], None, ALU.mult).then_inc(dec_weights, 1)
                dve.wait_ge(dec_p_turned, dd + 1)
                dve.tensor_copy(dpT[:, m, 0:8], ps[:, 6:8].rearrange("p a (k n) -> p (a k) n", n=P))
                dve.tensor_copy(dpT[0:64, m, 8], ps[0:64, 3, P:2 * P]).then_inc(dec_p_ready, 1)

            next_q(0, 0)
            next_q(0, 1)
            dec_evac(0)
            with dve.Fori(0, DB - 1) as b:
                dec_dve(b, 0, False)
                dec_dve(b, 1, False)
            dec_dve(DB - 1, 0, True)
            dec_dve(DB - 1, 1, True)

            prompt_dve(dve)
            dve.wait_ge(attn_hi, 1)
            tt(xn[:, 0:4, 1, S:NT], osam[:, 0], xn[:, 0:4, 0, S:NT].bitcast(F32), ALU.subtract).then_inc(attn_lo, 1)
            def lo(n, slot, dst):
                dve.wait_ge(unit_hi, n + 1)
                tt(dst[:, 1], wraw[:, slot], dst[:, 0].bitcast(F32), ALU.subtract).then_inc(unit_lo, 1)

            for w in range(13):
                if w < 12:
                    src, n, _ = b_chunk(w)
                    root = orms[:, w % 4, 0:n]
                    dve.wait_ge(head_roots, w + 1)
                    dve.reciprocal(root, root).then_inc(head_recips, 1)
                    dve.wait_ge(head_recips, w + 1)
                    stt(src, src, small[:, 7:8], root, ALU.mult, ALU.mult).then_inc(head_scaled, 1)
                if w >= 1:
                    src, n, t0 = b_chunk(w - 1)
                    dve.wait_ge(attn_hi, w + 1)
                    o = xn[:, 4 + (w - 1) % 4, :, t0:t0 + n]
                    tt(o[:, 1], src, o[:, 0].bitcast(F32), ALU.subtract).then_inc(attn_lo, 1)
                if w in (6, 10):
                    lo(w // 4 - 1, w // 4 - 1, ws[w // 4 - 1])

            def ffn_lo(layer, b, kind, par=0):
                lo(unit_of(layer, kind, b), raw_slot(layer, kind, b, par), ws[KINDS.index(kind)])

            def add(a, idx, scale=None):
                k, c = divmod(idx, NC)
                c0, cn = CH[c]
                dst = x[:, k, c0:c0 + cn]
                dve.wait_ge(group_done, a + 1)
                if scale is None:
                    tt(dst, ps[:, 4 + idx % 4, 0:cn], dst, ALU.add).then_inc(group_added, 1)
                else:
                    stt(dst, ps[:, 4 + idx % 4, 0:cn], scale, dst, ALU.mult, ALU.add).then_inc(group_added, 1)

            def hidden(layer, b, par):
                g0 = b * GU_PER + FFN_G[layer]
                first = isinstance(b, int) and b == 0
                for n in range(GU_PER + 1):
                    if n < GU_PER:
                        dve.wait_ge(silu_ready, g0 + (n + 1))
                        if not (first and layer == 0 and n < 2):
                            dve.wait_ge(hidden_lo, g0 + (n - 1))
                        cn = CH[n % NC][1]
                        tt(act_h[:, n % 2, 0:cn], act_s[:, n % 2, 0:cn], ps[:, 2 * (n % 2) + 1, 0:cn], ALU.mult).then_inc(hidden_ready, 1)
                    if n >= 1:
                        j, c = divmod(n - 1, NC)
                        c0, cn = CH[c]
                        dve.wait_ge(hidden_hi, g0 + n)
                        o = hh[:, par, j, :, c0:c0 + cn]
                        tt(o[:, 1], act_h[:, (n - 1) % 2, 0:cn], o[:, 0].bitcast(F32), ALU.subtract).then_inc(hidden_lo, 1)
                    if n == 3 and not first:
                        ffn_lo(layer, b - 1, "down", 1 - par)

            def adds(layer, b, splits=()):
                for idx in range(ADD_PER):
                    add(b * ADD_PER + (FFN_A[layer] + idx), idx)
                    if isinstance(b, int) and b == PAIRS - 1:
                        folds_at(2 * layer + 2, idx)
                    if splits and idx in (2, 6):
                        ffn_lo(layer, splits[0], ("gate", "up")[idx == 6], splits[1])

            def ffn(layer):
                def two(i, last):
                    hidden(layer, i * 2 + 1, 1)
                    adds(layer, i * 2, (i * 2 + 2, 0))
                    hidden(layer, i * 2 + 2, 0)
                    adds(layer, i * 2 + 1, () if last else (i * 2 + 3, 1))
                norm(1 + 2 * layer, lambda: ffn_lo(layer, 0, "gate"), lambda: ffn_lo(layer, 0, "up"))
                if layer == 1:
                    dve.wait_ge(state_stored, 32)
                hidden(layer, 0, 0)
                ffn_lo(layer, 1, "gate")
                ffn_lo(layer, 1, "up")
                with dve.Fori(0, TWOS - 1) as i:
                    two(i, False)
                two(TWOS - 1, True)
                ffn_lo(layer, PAIRS - 1, "down")
                adds(layer, PAIRS - 1)

            lo(2, 0, ws[2])
            for idx in range(ADD_PER):
                add(idx, idx)
                folds_at(1, idx)
                if idx == 5:
                    lo(3, 1, ws[0])
            ffn(0)

            lo(37, 1, ws[0])
            norm(2)
            dve.wait_ge(state_ready, 8)
            dve.wait_ge(pads_zeroed, 2)
            dve.wait_ge(norm_pieces, XF0[3])
            def pool_low(k):
                dve.wait_ge(pooled_hi, k + 1)
                dve.wait_ge(pooled, k + 1)
                tt(xn[:, k, 1], pf[k % 2][:], xn[:, k, 0].bitcast(F32), ALU.subtract).then_inc(pooled_lo, 1)

            def pool_adds(g):
                for idx in range(2 * NC * g, 2 * NC * (g + 1)):
                    kk = idx // NC
                    add(PAIRS * ADD_PER + FFN_A[0] + idx, idx, gains[:, 40 + kk:41 + kk])
                    if g == 3:
                        folds_at(3, idx)

            level = 0
            dve.wait_ge(corr_loaded, 16)
            for k in range(KD):
                g = k // 2
                src = yp[:, k]
                lead = 1
                if k:
                    dve.wait_ge(pooled, k)
                for e in range(g + 1):
                    dst = pa[:, e % 2]
                    step = 1 << e
                    if e:
                        dve.wait_ge(levels_done, level)
                    tt(dst[:, lead:PADW], src[:, lead:PADW], src[:, lead - step:PADW - step], ALU.add).then_inc(levels_done, 1)
                    level += 1
                    src = dst
                    lead += 2 * step
                dve.wait_ge(levels_done, level)
                tt(src[:, 16:32], src[:, 16:32], corr[:, g], ALU.mult).then_inc(levels_done, 1)
                level += 1
                dve.wait_ge(levels_done, level)
                w = 0.5 / (1 << g)
                if k >= 2:
                    dve.wait_ge(pooled_lo, k - 1)
                stt(pf[k % 2][:, 0:S], src[:, 16:16 + S], w, yp[:, k, 16:16 + S], ALU.mult, ALU.subtract)
                stt(by_sample(pf[k % 2][:, S:NT]), sample_cols(src)[:, :, 16:24], w, sample_cols(yp[:, k])[:, :, 16:24],
                    ALU.mult, ALU.subtract).then_inc(pooled, 1)
                if k:
                    pool_low(k - 1)
                if k == 6:
                    fold(3, 1)
                if k % 2 and k > 1:
                    pool_adds(g - 1)
            fold(3, 2)
            pool_low(KD - 1)
            fold(3, 3)
            fold(3, 4)
            pool_adds(3)
            ffn(1)
            norm(4)

        @block.tensor
        def _(pe):
            mm = pe.matmul

            def product(out, pairs, last=None):
                n = len(pairs)
                for i, (w, m) in enumerate(pairs):
                    for q_, (a, b_) in enumerate(((1, 0), (0, 1), (0, 0))):
                        r = mm(out, w(a), m(b_), start=(i == 0 and q_ == 0), stop=(i == n - 1 and q_ == 2))
                return r

            pe.wait_ge(consts_loaded, 160)
            for i in range(9):
                n = P if i < 8 else NS
                pe.wait_ge(input_rows_loaded[i % 3], 16 * (i // 3 + 1))
                if i >= 2:
                    pe.wait_ge(x_ready, i - 1)
                for k in range(KD):
                    r = pe.transpose(T2(i % 2, n)[:, k], xin[0:n, i % 3, k * P:(k + 1) * P], ident[0:n, 0:n])
                r.then_inc(input_transposed, 1)
            pe.transpose(ps[:, 6, 0:49], grow[:], ident[0:49, 0:49]).then_inc(gains_transposed, 1)
            pe.wait_ge(fills_done, 3)
            pe.wait_ge(small_ready, 2)
            mm(ps[:, 7, 0:1], ones[0:1, :], small[0:1, 4:5], start=True, stop=True).then_inc(lambda_broadcast, 1)

            def norm(r):
                for c, (c0, cn) in enumerate(CH):
                    pe.wait_ge(squares_added, FOLDS * r + KD - 1 + c)
                    mm(ps[:, c, 0:cn], ones[:], rstd[:, c0:c0 + cn], start=True, stop=True).then_inc(squares_summed, 1)

            norm(0)
            for g in range(6):
                pe.wait_ge(proj_w_lo, 2 * g + 2)
                for i in range(9):
                    n = P if i < 8 else NS
                    m = g * 9 + i
                    if g == 0:
                        c = 0 if i < 2 else 1 if i < 5 else 2
                        pe.wait_ge(norm_lo, 8 * (c + 1))
                    if m >= 8:
                        pe.wait_ge(proj_rows, m - 7)
                    elif m < 3:
                        pe.wait_ge(roots_ready, 3)
                    elif m >= 6:
                        pe.wait_ge(small_ready, 5)
                    product(ps[0:n, m % 8], [(lambda a, k=k: xn[:, k, a, i * P:i * P + n], lambda a, k=k: wp[:, g % 2, a, k])
                                             for k in range(KD)]).then_inc(proj_done, 1)

            pe.wait_ge(proj_rows, 54)
            pe.wait_ge(rows_rotated, 36)
            for m in range(2):
                for a in range(2):
                    for jp in range(4):
                        q_ = pe.transpose(ps[:, 2 * m + a, 64 * jp:64 * jp + 64], toks[:, 3 * m + a, jp * P:(jp + 1) * P], ident[0:NS, 0:NS])
                    q_.then_inc(dec_qk_turned, 1)

            def dec_transposes(b, m):
                dd = b * 2 + m
                first = isinstance(b, int) and b == 0 and m == 0
                pe.wait_ge(dec_k_loaded[m], (b + 1) * (128 if m else 16))
                for j in range(8):
                    if not (first and j < 2):
                        pe.wait_ge(dec_k_odd if j % 2 else dec_k_even, dd * 4 + j // 2)
                    for jp in range(4):
                        q_ = pe.transpose(TK(j)[:, jp], kraw[m][:, j, jp * P:(jp + 1) * P], ident[:])
                    q_.then_inc(dec_k_turned, 1)

            def dec_scores(b, m):
                dd = b * 2 + m
                pe.wait_ge(dec_q_current, dd + 1)
                pe.wait_ge(dec_k_even, dd * 4 + 4)
                pe.wait_ge(dec_k_odd, dd * 4 + 4)
                if not (isinstance(dd, int) and dd == 0):
                    pe.wait_ge(dec_masked, dd)
                for a in range(3):
                    for jp in range(4):
                        mv = knT[:, m, jp] if a == 2 else dkT[:, jp, a * 512:(a + 1) * 512]
                        q_ = mm(ps[32 * jp:32 * jp + 32, a, 0:(64 if a == 2 else 512)], qcur[:, m, jp], mv, start=True, stop=True)
                q_.then_inc(dec_scores_done, 1)

            def dec_turn(dd, m):
                pe.wait_ge(dec_exps, dd + 1)
                pe.wait_ge(dec_p_ready, dd)
                for j in range(8):
                    if j == 7:
                        pe.wait_ge(dec_stored, dd)
                    pe.transpose(ps[:, 6 + j // 4, (j % 4) * P:(j % 4 + 1) * P], dse[:, m, j * P:(j + 1) * P], ident[:])
                pe.transpose(ps[0:NS, 3, P:2 * P], dse[:, m, PAST:PAST + NS], ident[:]).then_inc(dec_p_turned, 1)

            def dec_values(b, m):
                dd = b * 2 + m
                pe.wait_ge(dec_p_ready, dd + 1)
                pe.wait_ge(dec_rows_out, dd)
                pe.wait_ge(dec_v_loaded[m], (b + 1) * (128 if m else 16))
                for j in range(9):
                    for jp in range(4):
                        rows, cols = slice(32 * jp, 32 * jp + 32), slice(jp * P, (jp + 1) * P)
                        w, v = ((dpT[:, m, j, rows], vraw[m][:, j, cols]) if j < 8 else
                                (dpT[0:NS, m, 8, rows], toks[:, 3 * m + 2, cols]))
                        q_ = mm(ps[rows, 3, 0:P], w, v, start=(j == 0), stop=(j == 8))
                q_.then_inc(dec_values_done, 1)

            def dec_combine(dd, m):
                pe.wait_ge(dec_rows_out, dd + 1)
                pe.wait_ge(dec_weights, dd + 1)
                if m:
                    mm(ps[:, 3, 256:288], dom[:], dmix[:, 1, 0:32], start=True, stop=True).then_inc(dec_combined, 1)
                else:
                    for hf in range(2):
                        h64 = slice(64 * hf, 64 * hf + 64)
                        q_ = mm(ps[h64, 3, 256:288], dom[:, h64], dmix[:, 0, 32 * hf:32 * hf + 32], start=True, stop=True)
                    q_.then_inc(dec_combined, 1)

            def dec_step(b, m, last=False):
                dd = b * 2 + m
                nxt = (b + 1, 0) if m else (b, 1)
                if not last:
                    dec_transposes(*nxt)
                if not (isinstance(dd, int) and dd == 0):
                    dec_combine(b * 2 + (m - 1), 1 - m)
                dec_turn(dd, m)
                if not last:
                    dec_scores(*nxt)
                dec_values(b, m)

            dec_transposes(0, 0)
            dec_scores(0, 0)
            dec_step(0, 0)
            dec_step(0, 1)
            with pe.Fori(1, DB - 1) as b:
                dec_step(b, 0)
                dec_step(b, 1)
            dec_step(DB - 1, 0)
            dec_step(DB - 1, 1, True)
            dec_combine(2 * DB - 1, 1)

            prompt_pe(pe)
            def head_squares(chunks):
                for w in chunks:
                    _, n, _ = b_chunk(w)
                    pe.wait_ge(head_squares_ready, w + 1)
                    if w >= 2:
                        pe.wait_ge(head_roots, w - 1)
                    mm(ps[:, w % 2, 0:n], ones[:], osq[:, w % 2, 0:n], start=True, stop=True).then_inc(head_squares_summed, 1)

            head_squares(range(8))
            def group(a, idx, pairs):
                k, c = divmod(idx, NC)
                if not isinstance(a, int) or a >= 4:
                    pe.wait_ge(group_added, a - 3)
                product(ps[:, 4 + idx % 4, 0:CH[c][1]], pairs).then_inc(group_done, 1)

            def moving(k, c):
                c0, cn = CH[c]
                return lambda a: xn[:, k, a, c0:c0 + cn]

            for idx in range(ADD_PER):
                kt, c = divmod(idx, NC)
                u, e = divmod(kt, 2)
                if idx == 1:
                    head_squares(range(8, 12))
                pe.wait_ge(unit_lo, u + 1)
                if kt == 0:
                    pe.wait_ge(attn_lo, 5 + 4 * c)
                group(idx, idx, [(lambda a, k=k: ws[u % 3][:, a, k * 256 + e * P:k * 256 + e * P + P], moving(k, c)) for k in range(KD)])

            def hidden(layer, b):
                g0 = b * GU_PER + FFN_G[layer]
                first = isinstance(b, int) and b == 0
                pe.wait_ge(unit_lo, unit_of(layer, "gate" if first else "up", b) + 1)
                for n in range(GU_PER):
                    j, c = divmod(n, NC)
                    if first and j == 0:
                        f0 = 24 * (1 + layer) + 8 * (c + 1)
                        pe.wait_ge(norm_lo, f0)
                    if not (first and layer == 0 and n < 2):
                        pe.wait_ge(hidden_ready, g0 + (n - 1))
                    elif n == 0:
                        pe.wait_ge(roots_ready, 6)
                    for a_ in range(2):
                        if first and n == 0 and a_:
                            pe.wait_ge(unit_lo, unit_of(layer, "up", 0) + 1)
                        q_ = product(ps[:, 2 * (n % 2) + a_, 0:CH[c][1]],
                                     [(lambda a, k=k: ws[a_][:, a, k * 256 + j * P:k * 256 + j * P + P], moving(k, c)) for k in range(KD)])
                    q_.then_inc(gate_up_done, 1)

            def down(layer, b, par):
                pe.wait_ge(hidden_lo, b * GU_PER + (FFN_G[layer] + GU_PER))
                pe.wait_ge(unit_lo, unit_of(layer, "down", b) + 1)
                for idx in range(ADD_PER):
                    kt, c = divmod(idx, NC)
                    c0, cn = CH[c]
                    group(b * ADD_PER + (FFN_A[layer] + idx), idx,
                          [(lambda a, j=j: ws[2][:, a, j * D + kt * P:j * D + kt * P + P], lambda a, j=j: hh[:, par, j, a, c0:c0 + cn])
                           for j in range(2)])

            def ffn(layer):
                norm(1 + 2 * layer)
                hidden(layer, 0)
                with pe.Fori(0, TWOS) as i:
                    hidden(layer, i * 2 + 1)
                    down(layer, i * 2, 0)
                    hidden(layer, i * 2 + 2)
                    down(layer, i * 2 + 1, 1)
                down(layer, PAIRS - 1, 0)

            ffn(0)
            pe.wait_ge(state_loaded, 16)
            pe.wait_ge(group_added, FFN_A[0] + PAIRS * ADD_PER)
            for k in range(KD):
                q_ = pe.transpose(ps[:, 4 + k // 4, (k % 4) * P:(k % 4) * P + DB * STATE], stin[:, k * P:(k + 1) * P], ident[0:120, 0:120])
            q_.then_inc(state_turned, 1)
            norm(2)
            pe.wait_ge(last_rows_ready, KD)
            pe.wait_ge(roots_ready, 9)
            for k in range(KD):
                pe.transpose(R2(0, STATE)[:, k * P:(k + 1) * P], pcomp[:, k, 0:STATE], ident[:])
                q_ = pe.transpose(R2(1, DB * STATE)[:, k * P:(k + 1) * P], pcomp[:, k, STATE:], ident[:])
            q_.then_inc(last_rows_turned, 1)
            pe.wait_ge(unit_lo, 38)
            for idx in range(ADD_PER):
                kt, c = divmod(idx, NC)
                g, e = divmod(kt, 2)
                pe.wait_ge(pooled_lo, 2 * g + 2)
                group(PAIRS * ADD_PER + FFN_A[0] + idx, idx,
                      [(lambda a, j=j: ws[0][:, a, (2 * g + j) * 256 + e * P:(2 * g + j) * 256 + e * P + P], moving(2 * g + j, c)) for j in range(2)])
            pe.wait_ge(last_rows_out, 2)
            ffn(1)
            norm(4)
            for i in range(9):
                n = P if i < 8 else NS
                c = 0 if i < 2 else 1 if i < 5 else 2
                pe.wait_ge(norm_pieces, XF0[4] + 8 * (c + 1))
                if i >= 2:
                    pe.wait_ge(out_rows_ready, i - 1)
                else:
                    pe.wait_ge(roots_ready, 15)
                for k in range(KD):
                    q_ = pe.transpose(R2(i % 2, n)[:, k * P:(k + 1) * P], yf[:, k, i * P:i * P + n], ident[:])
                q_.then_inc(out_turned, 1)


_INS = ["x_prompt", "x_sample", "cache_k_b", "cache_v_b", "cache_win_k_a", "cache_win_v_a", "state_pool", "page_table",
        "ln_mix", "ln_ffn", "ln_final", "w_in", "w_out", "lambda_q1", "lambda_k1", "lambda_q2", "lambda_k2", "subln_g",
        "pool_w", "pool_scale", "w_gate", "w_up", "w_down"]
_OUTS = [("o_y_p", (1, S, D)), ("o_y_s", (DB, T, D)),
         ("o_kb_p", (1, 1, S, 4, 128)), ("o_vb_p", (1, 1, S, 4, 128)),
         ("o_kb_s", (1, DB, T, 4, 128)), ("o_vb_s", (1, DB, T, 4, 128)),
         ("o_wk_p", (1, 1, S, 8, 64)), ("o_wv_p", (1, 1, S, 8, 64)),
         ("o_wk_s", (1, DB, PAST, 8, 64)), ("o_wv_s", (1, DB, PAST, 8, 64)),
         ("o_pl_p", (1, 1, STATE, D)), ("o_pl_s", (1, DB, STATE, D))]


def kernel(**inputs):
    import numpy as _np
    import concourse.bacc as _bacc
    from concourse import mybir as _mybir
    from concourse.bass_utils import run_bass_kernel_spmd as _run

    nc = _bacc.Bacc("TRN2", target_bir_lowering=False, num_devices=1)
    arrays, aps = {}, {}
    for name in _INS:
        a = _np.ascontiguousarray(inputs[name])
        arrays[name] = a
        aps[name] = nc.dram_tensor(name, a.shape, _mybir.dt.from_np(a.dtype), kind="ExternalInput").ap()
    arrays["consts"] = shape_constants()
    aps["consts"] = nc.dram_tensor("consts", (P, CONST_W), F32, kind="ExternalInput").ap()
    for name, shape in _OUTS:
        aps[name] = nc.dram_tensor(name, shape, F32, kind="ExternalOutput").ap()
    build_step(nc, aps)
    r = _run(nc, [arrays], core_ids=[0])
    return tuple(r.results[0][name] for name, _ in _OUTS)
```
